# Optimizing a Trainium2 kernel written in Bass

```python
import math
import jax, jax.numpy as jnp
from jax import lax
import numpy as np

D_MODEL = 1024
BATCH = 1
SEQ = 256
DEPTH = 1

HEAD_DIM = 64
N_MOBA_HEADS = 6
N_DIFF_HEADS = 6
N_SB_HEADS = 6
DIFF_QK_DIM = HEAD_DIM // 2
MOBA_BLOCK = 256
MOBA_TOPK = 3
MOBA_Q_CHUNK = 64
Q_BLOCK = 128
D_FF = 2816
N_BRANCH = 3
LN_EPS = 1e-5
SUBLN_EPS = 1e-5
MOBA_W = N_MOBA_HEADS * HEAD_DIM
DIFF_QK_W = N_DIFF_HEADS * 2 * DIFF_QK_DIM
DIFF_V_W = N_DIFF_HEADS * HEAD_DIM
SB_W = N_SB_HEADS * HEAD_DIM
IN_SIZES = (MOBA_W, MOBA_W, MOBA_W, DIFF_QK_W, DIFF_QK_W, DIFF_V_W, SB_W, SB_W, SB_W, N_BRANCH * D_MODEL)
N_IN = 3 * MOBA_W + 2 * DIFF_QK_W + DIFF_V_W + 3 * SB_W + N_BRANCH * D_MODEL


F32 = jnp.float32

def _alibi_slopes(n):
    return (2.0 ** (-8.0 * np.arange(1, n + 1, dtype=np.float32) / n)).astype(np.float32)

def layer_norm(x, g, b):
    xf = x.astype(F32)
    mu = jnp.mean(xf, axis=-1, keepdims=True)
    var = jnp.mean(jnp.square(xf - mu), axis=-1, keepdims=True)
    return ((xf - mu) * lax.rsqrt(var + LN_EPS) * g + b).astype(x.dtype)

def swiglu(x, w_gate, w_up, w_down):
    return (jax.nn.silu(x @ w_gate) * (x @ w_up)) @ w_down

def split_heads(t, n_heads):
    B, S, _ = t.shape
    return t.reshape(B, S, n_heads, -1).transpose(0, 2, 1, 3)

def merge_heads(t):
    B, H, S, d = t.shape
    return t.transpose(0, 2, 1, 3).reshape(B, S, H * d)

def moba_attention(q, k, v, slopes):
    B, H, S, Dh = q.shape
    nb = -(-S // MOBA_BLOCK)
    pad = nb * MOBA_BLOCK - S
    kp = jnp.pad(k, ((0, 0), (0, 0), (0, pad), (0, 0)))
    vp = jnp.pad(v, ((0, 0), (0, 0), (0, pad), (0, 0)))
    kb = kp.reshape(B, H, nb, MOBA_BLOCK, Dh)
    vb = vp.reshape(B, H, nb, MOBA_BLOCK, Dh)
    kmean = jnp.mean(kb.astype(F32), axis=3)
    topk = min(MOBA_TOPK, nb)
    scale = Dh ** -0.5
    bi = jnp.arange(B)[:, None, None, None]
    hi = jnp.arange(H)[None, :, None, None]
    slope = slopes.reshape(1, H, 1, 1)
    blk_off = jnp.arange(MOBA_BLOCK)
    blk_ids = jnp.arange(nb)
    n_chunks = S // MOBA_Q_CHUNK

    def chunk(i):
        t0 = i * MOBA_Q_CHUNK
        qc = lax.dynamic_slice_in_dim(q, t0, MOBA_Q_CHUNK, axis=2)
        tpos = t0 + jnp.arange(MOBA_Q_CHUNK)
        own = t0 // MOBA_BLOCK
        gate = jnp.einsum('bhcd,bhnd->bhcn', qc.astype(F32), kmean)
        gate = jnp.where(blk_ids < own, gate, -jnp.inf)
        _, sel = lax.top_k(gate, topk)
        valid = sel < own
        ksel = kb[bi, hi, sel]
        vsel = vb[bi, hi, sel]
        s_sel = jnp.einsum('bhcd,bhcnkd->bhcnk', qc, ksel).astype(F32) * scale
        dist_sel = tpos[None, None, :, None, None] - (sel[..., None] * MOBA_BLOCK + blk_off)
        s_sel = jnp.where(valid[..., None], s_sel - slope[..., None] * dist_sel, -jnp.inf)
        kown = lax.dynamic_index_in_dim(kb, own, axis=2, keepdims=False)
        vown = lax.dynamic_index_in_dim(vb, own, axis=2, keepdims=False)
        s_own = jnp.einsum('bhcd,bhkd->bhck', qc, kown).astype(F32) * scale
        dist_own = tpos[:, None] - (own * MOBA_BLOCK + blk_off)[None, :]
        s_own = jnp.where(dist_own >= 0, s_own - slope * dist_own, -jnp.inf)
        scores = jnp.concatenate([s_sel.reshape(B, H, MOBA_Q_CHUNK, topk * MOBA_BLOCK), s_own], axis=-1)
        p = jax.nn.softmax(scores, axis=-1).astype(v.dtype)
        p_sel = p[..., :topk * MOBA_BLOCK].reshape(B, H, MOBA_Q_CHUNK, topk, MOBA_BLOCK)
        p_own = p[..., topk * MOBA_BLOCK:]
        return (jnp.einsum('bhcnk,bhcnkd->bhcd', p_sel, vsel)
                + jnp.einsum('bhck,bhkd->bhcd', p_own, vown))

    out = lax.map(chunk, jnp.arange(n_chunks))
    return out.transpose(1, 2, 0, 3, 4).reshape(B, H, S, Dh)

def diff_attention(q, k, v, slopes, lam, subln_g, lambda_init):
    B, H, _, S, dq = q.shape
    dv = v.shape[-1]
    scale = dq ** -0.5
    kpos = jnp.arange(S)
    slope = slopes.reshape(1, H, 1, 1, 1)

    def block(i):
        t0 = i * Q_BLOCK
        qc = lax.dynamic_slice_in_dim(q, t0, Q_BLOCK, axis=3)
        dist = (t0 + jnp.arange(Q_BLOCK))[:, None] - kpos[None, :]
        s = jnp.einsum('bhmcd,bhmsd->bhmcs', qc, k).astype(F32) * scale
        s = jnp.where(dist >= 0, s - slope * dist, -jnp.inf)
        p = jax.nn.softmax(s, axis=-1)
        w = p[:, :, 0] - lam * p[:, :, 1]
        return jnp.einsum('bhcs,bhsd->bhcd', w.astype(v.dtype), v)

    o = lax.map(block, jnp.arange(S // Q_BLOCK))
    o = o.transpose(1, 2, 0, 3, 4).reshape(B, H, S, dv).astype(F32)
    o = o * lax.rsqrt(jnp.mean(jnp.square(o), axis=-1, keepdims=True) + SUBLN_EPS) * subln_g
    return (o * (1.0 - lambda_init)).astype(v.dtype)

def stick_breaking_attention(q, k, v):
    B, H, S, Dh = q.shape
    scale = Dh ** -0.5
    kpos = jnp.arange(S)

    def block(i):
        t0 = i * Q_BLOCK
        qc = lax.dynamic_slice_in_dim(q, t0, Q_BLOCK, axis=2)
        before = kpos[None, :] < (t0 + jnp.arange(Q_BLOCK))[:, None]
        z = jnp.einsum('bhcd,bhsd->bhcs', qc, k).astype(F32) * scale
        log_1m = jnp.where(before, jax.nn.log_sigmoid(-z), 0.0)
        tail = lax.cumsum(log_1m, axis=3, reverse=True) - log_1m
        w = jnp.where(before, jnp.exp(jax.nn.log_sigmoid(z) + tail), 0.0)
        return jnp.einsum('bhcs,bhsd->bhcd', w.astype(v.dtype), v)

    o = lax.map(block, jnp.arange(S // Q_BLOCK))
    return o.transpose(1, 2, 0, 3, 4).reshape(B, H, S, Dh)

def hybrid_mixer(x, w_in, b_gate, diff_lambda, diff_subln_g, w_br_moba, w_br_diff, w_br_sb, w_out, layer_idx):
    B, S, D = x.shape
    h = x @ w_in
    offs = []
    acc = 0
    for n in IN_SIZES[:-1]:
        acc += n
        offs.append(acc)
    q_m, k_m, v_m, q_d, k_d, v_d, q_s, k_s, v_s, g = jnp.split(h, offs, axis=-1)

    slopes = jnp.asarray(_alibi_slopes(N_MOBA_HEADS + N_DIFF_HEADS))
    o_m = moba_attention(split_heads(q_m, N_MOBA_HEADS), split_heads(k_m, N_MOBA_HEADS),
                         split_heads(v_m, N_MOBA_HEADS), slopes[0::2])

    lambda_init = 0.8 - 0.6 * math.exp(-0.3 * layer_idx)
    lf = diff_lambda.astype(F32)
    lam = jnp.exp(jnp.sum(lf[0] * lf[1])) - jnp.exp(jnp.sum(lf[2] * lf[3])) + lambda_init
    qd = q_d.reshape(B, S, N_DIFF_HEADS, 2, DIFF_QK_DIM).transpose(0, 2, 3, 1, 4)
    kd = k_d.reshape(B, S, N_DIFF_HEADS, 2, DIFF_QK_DIM).transpose(0, 2, 3, 1, 4)
    o_d = diff_attention(qd, kd, split_heads(v_d, N_DIFF_HEADS), slopes[1::2], lam, diff_subln_g, lambda_init)

    o_s = stick_breaking_attention(split_heads(q_s, N_SB_HEADS), split_heads(k_s, N_SB_HEADS),
                                   split_heads(v_s, N_SB_HEADS))

    gates = jax.nn.sigmoid((g.reshape(B, S, N_BRANCH, D) + b_gate).astype(F32)).astype(x.dtype)
    merged = (gates[:, :, 0] * (merge_heads(o_m) @ w_br_moba)
              + gates[:, :, 1] * (merge_heads(o_d) @ w_br_diff)
              + gates[:, :, 2] * (merge_heads(o_s) @ w_br_sb))
    return merged @ w_out

def first_inputs(seed: int = 0) -> dict:
    key = jax.random.key(seed)
    ks = jax.random.split(key, 14)
    D = D_MODEL
    beta = (8.0 * DEPTH) ** -0.25
    nrm = jax.random.normal
    segs = [(MOBA_W, 1.0), (MOBA_W, 1.0), (MOBA_W, beta), (DIFF_QK_W, 1.0), (DIFF_QK_W, 1.0),
            (DIFF_V_W, beta), (SB_W, 1.0), (SB_W, 1.0), (SB_W, beta), (N_BRANCH * D, 1.0)]
    col_scale = jnp.asarray(np.concatenate([np.full(n, s, np.float32) for n, s in segs]))
    return {
        "x": nrm(ks[0], (BATCH, SEQ, D), F32),
        "ln_g": 1.0 + 0.02 * nrm(ks[1], (DEPTH, 3, D), F32),
        "ln_b": 0.02 * nrm(ks[2], (DEPTH, 3, D), F32),
        "ffn_w_gate": nrm(ks[3], (DEPTH, 2, D, D_FF), F32) * D ** -0.5,
        "ffn_w_up": nrm(ks[4], (DEPTH, 2, D, D_FF), F32) * (D ** -0.5 * beta),
        "ffn_w_down": nrm(ks[5], (DEPTH, 2, D_FF, D), F32) * (D_FF ** -0.5 * beta),
        "w_in": nrm(ks[6], (DEPTH, D, N_IN), F32) * D ** -0.5 * col_scale,
        "b_gate": 0.01 * nrm(ks[7], (DEPTH, N_BRANCH, D), F32),
        "diff_lambda": 0.1 * nrm(ks[8], (DEPTH, 4, DIFF_QK_DIM), F32),
        "diff_subln_g": 1.0 + 0.02 * nrm(ks[9], (DEPTH, HEAD_DIM), F32),
        "w_br_moba": nrm(ks[10], (DEPTH, MOBA_W, D), F32) * MOBA_W ** -0.5,
        "w_br_diff": nrm(ks[11], (DEPTH, DIFF_V_W, D), F32) * DIFF_V_W ** -0.5,
        "w_br_sb": nrm(ks[12], (DEPTH, SB_W, D), F32) * SB_W ** -0.5,
        "w_out": nrm(ks[13], (DEPTH, D, D), F32) * (D ** -0.5 * beta),
    }

def first_block(x, ln_g, ln_b, ffn_w_gate, ffn_w_up, ffn_w_down, w_in, b_gate, diff_lambda,
              diff_subln_g, w_br_moba, w_br_diff, w_br_sb, w_out):
    alpha = (2.0 * DEPTH) ** 0.25
    for l in range(DEPTH):
        x = layer_norm(alpha * x + 0.5 * swiglu(x, ffn_w_gate[l, 0], ffn_w_up[l, 0], ffn_w_down[l, 0]),
                       ln_g[l, 0], ln_b[l, 0])
        x = layer_norm(alpha * x + hybrid_mixer(x, w_in[l], b_gate[l], diff_lambda[l], diff_subln_g[l],
                                                w_br_moba[l], w_br_diff[l], w_br_sb[l], w_out[l], l),
                       ln_g[l, 1], ln_b[l, 1])
        x = layer_norm(alpha * x + 0.5 * swiglu(x, ffn_w_gate[l, 1], ffn_w_up[l, 1], ffn_w_down[l, 1]),
                       ln_g[l, 2], ln_b[l, 2])
    return x


PLE_DIM = 256
EPS = 1e-6
NEG = -1e30

GDN_HEADS = 4
GDN_DK = 128
GDN_DV = 128
GDN_CONV = 4
GDN_CHUNK = 64

NSA_HEADS = 8
NSA_GROUPS = 2
NSA_HPG = NSA_HEADS // NSA_GROUPS
NSA_DK = 64
NSA_DV = 64
CMP_LEN = 32
CMP_STRIDE = 16
CMP_HIDDEN = 256
SEL_BLOCK = 64
SEL_TOPN = 16
SEL_QCHUNK = 64
WINDOW = 512
WIN_QBLOCK = 128
FORCED_SCORE = 1e9

FFN_CONV = 3

IN_SPLITS = (
    GDN_HEADS * GDN_DK,
    GDN_HEADS * GDN_DK,
    GDN_HEADS * GDN_DV,
    GDN_HEADS * GDN_DV,
    GDN_HEADS,
    GDN_HEADS,
    NSA_HEADS * NSA_DK,
    NSA_GROUPS * NSA_DK,
    NSA_GROUPS * NSA_DV,
    NSA_GROUPS * NSA_DK,
    NSA_GROUPS * NSA_DV,
    NSA_GROUPS * NSA_DK,
    NSA_GROUPS * NSA_DV,
    NSA_HEADS * 3,
    2 * D_MODEL,
)
D_IN = sum(IN_SPLITS)


def rmsnorm(x, w):
    xf = x.astype(jnp.float32)
    y = xf * lax.rsqrt(jnp.mean(xf * xf, axis=-1, keepdims=True) + EPS)
    return (y * w.astype(jnp.float32)).astype(x.dtype)

def l2norm(x):
    return x * lax.rsqrt(jnp.sum(x * x, axis=-1, keepdims=True) + EPS)

def causal_dwconv(x, w):
    width, c = w.shape
    return lax.conv_general_dilated(
        x, w[:, None, :].astype(x.dtype), window_strides=(1,), padding=((width - 1, 0),),
        dimension_numbers=('NWC', 'WIO', 'NWC'), feature_group_count=c)

def alibi_slopes(n):
    return 2.0 ** (-8.0 * jnp.arange(1, n + 1, dtype=jnp.float32) / n)

def masked_softmax(s, valid):
    p = jax.nn.softmax(jnp.where(valid, s, NEG), axis=-1)
    return jnp.where(valid, p, 0.0)

def chunk_gated_delta_rule(q, k, v, beta, g):
    B, S, H, dk = q.shape
    dv = v.shape[-1]
    C = GDN_CHUNK
    n = S // C

    def chunks(t):
        t = t.reshape((B, n, C, H) + t.shape[3:])
        return jnp.moveaxis(t, (1, 3), (0, 2))

    qc, kc, vc, bc = chunks(q), chunks(k), chunks(v), chunks(beta)
    gcum = jnp.cumsum(chunks(g), axis=-1)
    idx = jnp.arange(C)
    strict = idx[:, None] > idx[None, :]
    incl = idx[:, None] >= idx[None, :]
    gdiff = gcum[..., :, None] - gcum[..., None, :]
    dec_strict = jnp.where(strict, jnp.exp(jnp.where(strict, gdiff, 0.0)), 0.0)
    dec_incl = jnp.where(incl, jnp.exp(jnp.where(incl, gdiff, 0.0)), 0.0)
    lower = bc[..., None] * jnp.einsum('nbhid,nbhjd->nbhij', kc, kc) * dec_strict
    gam = jnp.exp(gcum)
    rhs = jnp.concatenate([(bc * gam)[..., None] * kc, bc[..., None] * vc], axis=-1)
    sol = lax.linalg.triangular_solve(lower + jnp.eye(C, dtype=q.dtype), rhs,
                                      left_side=True, lower=True, unit_diagonal=True)
    w_c, u0_c = sol[..., :dk], sol[..., dk:]
    qk = jnp.einsum('nbhid,nbhjd->nbhij', qc, kc) * dec_incl
    q_dec = qc * gam[..., None]
    k_tail = kc * jnp.exp(gcum[..., -1:] - gcum)[..., None]
    g_last = gam[..., -1]

    def step(state, inp):
        w_, u0_, qk_, qd_, kt_, gl_ = inp
        u = u0_ - jnp.einsum('bhcd,bhde->bhce', w_, state)
        o = jnp.einsum('bhcd,bhde->bhce', qd_, state) + jnp.einsum('bhij,bhje->bhie', qk_, u)
        new_state = gl_[..., None, None] * state + jnp.einsum('bhcd,bhce->bhde', kt_, u)
        return new_state, o

    s0 = jnp.zeros((B, H, dk, dv), q.dtype)
    _, o = lax.scan(step, s0, (w_c, u0_c, qk, q_dec, k_tail, g_last))
    return jnp.moveaxis(o, (0, 2), (1, 3)).reshape(B, S, H, dv)

def gdn_mixer(q, k, v, z, b, a, conv_w, a_log, dt_bias, norm_w):
    B, S, _ = q.shape
    H, dk, dv = GDN_HEADS, GDN_DK, GDN_DV
    f32 = jnp.float32
    qkv = jax.nn.silu(causal_dwconv(jnp.concatenate([q, k, v], axis=-1), conv_w))
    q, k, v = jnp.split(qkv, [H * dk, 2 * H * dk], axis=-1)
    q = l2norm(q.reshape(B, S, H, dk).astype(f32)) * (dk ** -0.5)
    k = l2norm(k.reshape(B, S, H, dk).astype(f32))
    v = v.reshape(B, S, H, dv).astype(f32)
    beta = jax.nn.sigmoid(b.astype(f32))
    g = -jnp.exp(a_log.astype(f32)) * jax.nn.softplus(a.astype(f32) + dt_bias.astype(f32))
    o = chunk_gated_delta_rule(q, k, v, beta, g).astype(z.dtype)
    o = rmsnorm(o, norm_w) * jax.nn.silu(z.reshape(B, S, H, dv))
    return o.reshape(B, S, H * dv)

def compress_blocks(x, pos, w1, w2):
    B, S, G, d = x.shape
    r = CMP_LEN // CMP_STRIDE
    xs = x.reshape(B, S // CMP_STRIDE, CMP_STRIDE, G, d)
    nc = S // CMP_STRIDE - r + 1
    blocks = jnp.concatenate([xs[:, i:i + nc] for i in range(r)], axis=2)
    blocks = blocks + pos[:, None, :]
    flat = jnp.moveaxis(blocks, 3, 2).reshape(B, nc, G, CMP_LEN * d)
    return jax.nn.gelu(flat @ w1) @ w2

def nsa_mixer(q, k_cmp, v_cmp, k_slc, v_slc, k_win, v_win, gate,
              cmp_pos_k, cmp_w1_k, cmp_w2_k, cmp_pos_v, cmp_w1_v, cmp_w2_v):
    B, S, _ = q.shape
    H, G, R, dk, dv = NSA_HEADS, NSA_GROUPS, NSA_HPG, NSA_DK, NSA_DV
    f32 = jnp.float32
    slopes = alibi_slopes(H).reshape(G, R)
    t = jnp.arange(S)
    qh = q.reshape(B, S, G, R, dk) * (dk ** -0.5)
    grp = lambda y, d: y.reshape(B, S, G, d)

    kc = compress_blocks(grp(k_cmp, dk), cmp_pos_k, cmp_w1_k, cmp_w2_k)
    vc = compress_blocks(grp(v_cmp, dv), cmp_pos_v, cmp_w1_v, cmp_w2_v)
    nc = kc.shape[1]
    blk_start = jnp.arange(nc) * CMP_STRIDE
    dist_c = t[:, None] - (blk_start + CMP_LEN - 1)[None, :]
    s_c = jnp.einsum('bsgrd,bngd->bgrsn', qh, kc).astype(f32) \
        - slopes[None, :, :, None, None] * dist_c.astype(f32)
    p_c = masked_softmax(s_c, dist_c >= 0)
    o_cmp = jnp.einsum('bgrsn,bngd->bsgrd', p_c.astype(vc.dtype), vc)

    ns = S // SEL_BLOCK
    sel_start = jnp.arange(ns) * SEL_BLOCK
    overlap = jnp.clip(jnp.minimum(blk_start[:, None] + CMP_LEN, sel_start[None, :] + SEL_BLOCK)
                       - jnp.maximum(blk_start[:, None], sel_start[None, :]), 0, None).astype(f32) / CMP_LEN
    imp = jnp.einsum('bgsn,nj->bgsj', p_c.sum(axis=2), overlap)
    cur = t // SEL_BLOCK
    j = jnp.arange(ns)
    forced = (j[None, :] == 0) | (j[None, :] == cur[:, None]) | (j[None, :] == cur[:, None] - 1)
    sel_valid = j[None, :] <= cur[:, None]
    imp = jnp.where(sel_valid, jnp.where(forced, FORCED_SCORE, imp), NEG)
    n_sel = min(SEL_TOPN, ns)
    _, sel_idx = lax.top_k(imp, n_sel)

    ks = k_slc.reshape(B, ns, SEL_BLOCK, G, dk).transpose(0, 3, 1, 2, 4)
    vs = v_slc.reshape(B, ns, SEL_BLOCK, G, dv).transpose(0, 3, 1, 2, 4)
    QC = SEL_QCHUNK
    nq = S // QC
    q_ch = qh.reshape(B, nq, QC, G, R, dk).transpose(1, 0, 3, 4, 2, 5)
    idx_ch = sel_idx.reshape(B, G, nq, QC, n_sel).transpose(2, 0, 1, 3, 4)
    t_ch = t.reshape(nq, QC)
    nk = n_sel * SEL_BLOCK

    def sel_chunk(args):
        qb, ib, tb = args
        flat = ib.reshape(B, G, QC * n_sel)[:, :, :, None, None]
        kg = jnp.take_along_axis(ks, flat, axis=2).reshape(B, G, QC, nk, dk)
        vg = jnp.take_along_axis(vs, flat, axis=2).reshape(B, G, QC, nk, dv)
        pos = (ib[..., None] * SEL_BLOCK + jnp.arange(SEL_BLOCK)).reshape(B, G, QC, nk)
        dist = tb[None, None, :, None] - pos
        s = jnp.einsum('bgrqd,bgqkd->bgrqk', qb, kg).astype(f32) \
            - slopes[None, :, :, None, None] * dist[:, :, None].astype(f32)
        pr = masked_softmax(s, (dist >= 0)[:, :, None])
        return jnp.einsum('bgrqk,bgqkd->bgrqd', pr.astype(vg.dtype), vg)

    o_slc = lax.map(sel_chunk, (q_ch, idx_ch, t_ch))
    o_slc = o_slc.transpose(1, 0, 4, 2, 3, 5).reshape(B, S, G, R, dv)

    QB = WIN_QBLOCK
    nb = S // QB
    nwb = WINDOW // QB

    def band(y, d):
        yb = y.reshape(B, nb, QB, G, d).transpose(1, 0, 3, 2, 4)
        yp = jnp.pad(yb, ((nwb, 0), (0, 0), (0, 0), (0, 0), (0, 0)))
        return jnp.concatenate([yp[i:i + nb] for i in range(nwb + 1)], axis=3)

    kband, vband = band(k_win, dk), band(v_win, dv)
    q_wb = qh.reshape(B, nb, QB, G, R, dk).transpose(1, 0, 3, 4, 2, 5)
    qpos = t.reshape(nb, QB)
    kpos = (jnp.arange(nb)[:, None] - nwb) * QB + jnp.arange((nwb + 1) * QB)[None, :]

    def win_block(args):
        qb, kb, vb, tq, tk = args
        dist = tq[:, None] - tk[None, :]
        valid = (dist >= 0) & (dist < WINDOW) & (tk[None, :] >= 0)
        s = jnp.einsum('bgrqd,bgkd->bgrqk', qb, kb).astype(f32) \
            - slopes[None, :, :, None, None] * dist.astype(f32)
        pr = masked_softmax(s, valid)
        return jnp.einsum('bgrqk,bgkd->bgrqd', pr.astype(vb.dtype), vb)

    o_win = lax.map(win_block, (q_wb, kband, vband, qpos, kpos))
    o_win = o_win.transpose(1, 0, 4, 2, 3, 5).reshape(B, S, G, R, dv)

    gates = jax.nn.sigmoid(gate).reshape(B, S, G, R, 3)
    o = gates[..., 0:1] * o_cmp + gates[..., 1:2] * o_slc + gates[..., 2:3] * o_win
    return o.reshape(B, S, H * dv)

def second_inputs(seed: int = 0) -> dict:
    key = jax.random.key(seed)
    ks = jax.random.split(key, 32)
    L, D = DEPTH, D_MODEL
    f32 = jnp.float32

    def nrm(k, shape, fan_in):
        return jax.random.normal(k, shape, f32) * (fan_in ** -0.5)

    def gain(k, n):
        return 1.0 + 0.05 * jax.random.normal(k, (L, n), f32)

    dt = jnp.exp(jax.random.uniform(ks[6], (L, GDN_HEADS), f32, minval=np.log(1e-3), maxval=np.log(1e-1)))
    return {
        'x': jax.random.normal(ks[0], (BATCH, SEQ, D), f32),
        'p': jax.random.normal(ks[1], (DEPTH, BATCH, SEQ, PLE_DIM), f32),
        'norm_mix_pre': gain(ks[2], D),
        'w_in': nrm(ks[3], (L, D, D_IN), D),
        'conv_qkv': nrm(ks[4], (L, GDN_CONV, 2 * GDN_HEADS * GDN_DK + GDN_HEADS * GDN_DV), GDN_CONV),
        'a_log': jnp.log(jax.random.uniform(ks[5], (L, GDN_HEADS), f32, minval=1.0, maxval=16.0)),
        'dt_bias': dt + jnp.log(-jnp.expm1(-dt)),
        'gdn_norm': gain(ks[7], GDN_DV),
        'cmp_pos_k': 0.1 * jax.random.normal(ks[8], (L, CMP_LEN, NSA_DK), f32),
        'cmp_w1_k': nrm(ks[9], (L, CMP_LEN * NSA_DK, CMP_HIDDEN), CMP_LEN * NSA_DK),
        'cmp_w2_k': nrm(ks[10], (L, CMP_HIDDEN, NSA_DK), CMP_HIDDEN),
        'cmp_pos_v': 0.1 * jax.random.normal(ks[11], (L, CMP_LEN, NSA_DV), f32),
        'cmp_w1_v': nrm(ks[12], (L, CMP_LEN * NSA_DV, CMP_HIDDEN), CMP_LEN * NSA_DV),
        'cmp_w2_v': nrm(ks[13], (L, CMP_HIDDEN, NSA_DV), CMP_HIDDEN),
        'w_a2d': nrm(ks[14], (L, GDN_HEADS * GDN_DV, D), GDN_HEADS * GDN_DV),
        'w_b2d': nrm(ks[15], (L, NSA_HEADS * NSA_DV, D), NSA_HEADS * NSA_DV),
        'w_o': nrm(ks[16], (L, D, D), D),
        'norm_mix_post': gain(ks[17], D),
        'norm_ffn_pre': gain(ks[18], D),
        'w_up': nrm(ks[19], (L, D, 2 * D_FF), D),
        'conv_ffn': nrm(ks[20], (L, FFN_CONV, 2 * D_FF), FFN_CONV),
        'conv_ffn_b': 0.02 * jax.random.normal(ks[21], (L, 2 * D_FF), f32),
        'w_down': nrm(ks[22], (L, D_FF, D), D_FF),
        'norm_ffn_post': gain(ks[23], D),
        'w_ple': nrm(ks[24], (L, PLE_DIM, D), PLE_DIM),
        'w_ple_gate': nrm(ks[25], (L, D, D), D),
        'norm_ple_post': gain(ks[26], D),
    }

def second_block(x, p, norm_mix_pre, w_in, conv_qkv, a_log, dt_bias, gdn_norm,
              cmp_pos_k, cmp_w1_k, cmp_w2_k, cmp_pos_v, cmp_w1_v, cmp_w2_v,
              w_a2d, w_b2d, w_o, norm_mix_post, norm_ffn_pre, w_up, conv_ffn, conv_ffn_b,
              w_down, norm_ffn_post, w_ple, w_ple_gate, norm_ple_post):
    offs = np.cumsum(IN_SPLITS)[:-1].tolist()
    h = x
    for i in range(DEPTH):
        u = rmsnorm(h, norm_mix_pre[i])
        (qa, ka, va, za, ba, aa, qb, kcm, vcm, ksl, vsl, kwi, vwi, gnsa, gmix) = \
            jnp.split(u @ w_in[i], offs, axis=-1)
        ya = gdn_mixer(qa, ka, va, za, ba, aa, conv_qkv[i], a_log[i], dt_bias[i], gdn_norm[i])
        yb = nsa_mixer(qb, kcm, vcm, ksl, vsl, kwi, vwi, gnsa,
                       cmp_pos_k[i], cmp_w1_k[i], cmp_w2_k[i], cmp_pos_v[i], cmp_w1_v[i], cmp_w2_v[i])
        g_a, g_b = jnp.split(jax.nn.sigmoid(gmix), 2, axis=-1)
        mixed = (g_a * (ya @ w_a2d[i]) + g_b * (yb @ w_b2d[i])) @ w_o[i]
        h = h + rmsnorm(mixed, norm_mix_post[i])
        f = rmsnorm(h, norm_ffn_pre[i]) @ w_up[i]
        f = causal_dwconv(f, conv_ffn[i]) + conv_ffn_b[i]
        f_gate, f_val = jnp.split(f, 2, axis=-1)
        f = (jax.nn.gelu(f_gate) * f_val) @ w_down[i]
        h = h + rmsnorm(f, norm_ffn_post[i])
        e = (p[i] @ w_ple[i]) * jax.nn.sigmoid(h @ w_ple_gate[i])
        h = h + rmsnorm(e, norm_ple_post[i])
    return h


def setup_inputs(seed=0):
    out = dict(first_inputs(seed))
    for name, value in second_inputs(seed + 1).items():
        if name != "x":
            out[name + "_2"] = value
    return out


def reference(
    x, ln_g, ln_b, ffn_w_gate, ffn_w_up, ffn_w_down, w_in, b_gate, diff_lambda, diff_subln_g,
    w_br_moba, w_br_diff, w_br_sb, w_out, p_2, norm_mix_pre_2, w_in_2, conv_qkv_2, a_log_2,
    dt_bias_2, gdn_norm_2, cmp_pos_k_2, cmp_w1_k_2, cmp_w2_k_2, cmp_pos_v_2, cmp_w1_v_2,
    cmp_w2_v_2, w_a2d_2, w_b2d_2, w_o_2, norm_mix_post_2, norm_ffn_pre_2, w_up_2, conv_ffn_2,
    conv_ffn_b_2, w_down_2, norm_ffn_post_2, w_ple_2, w_ple_gate_2, norm_ple_post_2,
):
    x = first_block(
        x, ln_g, ln_b, ffn_w_gate, ffn_w_up, ffn_w_down, w_in, b_gate, diff_lambda,
        diff_subln_g, w_br_moba, w_br_diff, w_br_sb, w_out,
    )
    return second_block(
        x, p_2, norm_mix_pre_2, w_in_2, conv_qkv_2, a_log_2, dt_bias_2, gdn_norm_2, cmp_pos_k_2,
        cmp_w1_k_2, cmp_w2_k_2, cmp_pos_v_2, cmp_w1_v_2, cmp_w2_v_2, w_a2d_2, w_b2d_2, w_o_2,
        norm_mix_post_2, norm_ffn_pre_2, w_up_2, conv_ffn_2, conv_ffn_b_2, w_down_2,
        norm_ffn_post_2, w_ple_2, w_ple_gate_2, norm_ple_post_2,
    )


_drawn_inputs = setup_inputs


def setup_inputs(seed=0):
    import zlib

    import numpy as np

    out = dict(_drawn_inputs(seed))
    spreads = {}
    factors = {'b_gate': 8.0,
     'diff_lambda': 3.586,
     'diff_subln_g': 8.0,
     'cmp_pos_k_2': 8.0,
     'conv_ffn_b_2': 3.87}
    for name, (base, spread) in spreads.items():
        noise = np.random.default_rng([zlib.crc32(name.encode()), seed]).standard_normal(out[name].shape)
        drawn = base * np.exp(spread * noise) if base else spread * noise
        out[name] = __import__('jax').numpy.asarray(drawn.astype(out[name].dtype))
    for name, factor in factors.items():
        out[name] = (out[name] * factor).astype(out[name].dtype)
    return out
```

```python
from contextlib import ExitStack

import numpy as np

import concourse.bass as bass
from concourse import mybir

ALU = mybir.AluOpType
ACT = mybir.ActivationFunctionType
AX = mybir.AxisListType
F32 = mybir.dt.float32

P = 128
T = 256
D = 1024
KD = D // P
FF = 2816
NF = FF // P
RING = 3
CB = 16
NBANK = 4
GROUP = 4
TURNS = GROUP * 24 // CB // RING

H1 = 6
W1 = H1 * 64
SLOPES1 = [float(np.float32(2.0 ** (-8.0 * (i + 1) / 12))) for i in range(12)]
H2 = 8
SLOPES2 = [2.0 ** -(i + 1) for i in range(H2)]
NC = 15
HG = 4
LEVELS = 7
ALPHA = float(2.0 ** 0.25)
NEG = -1e30
N_INST1 = 3 * H1
N_INST2 = 2 * H2


def constants():
    i = np.arange(P)
    row, col = i[:, None], i[None, :]
    parts = {}
    parts["ident"] = (row == col).astype(np.float32)
    parts["ones"] = np.ones((P, P), np.float32)
    parts["upper"] = (row <= col).astype(np.float32)
    parts["lower"] = (row >= col).astype(np.float32)
    d0 = row - col
    d1 = (row + P) - np.arange(T)[None, :]
    parts["negdist"] = np.concatenate([np.where(d >= 0, -d, NEG) for d in (d0, d1)], 1)
    parts["sbmask"] = np.concatenate([np.where(row < np.arange(T)[None, :], 0, NEG), np.where(row < col, 0, NEG)], 1)
    parts["decmask"] = np.where(row <= col, 0, NEG)
    for lv in range(LEVELS):
        m = (row < col) & (row >> (lv + 1) == col >> (lv + 1)) & (row >> lv != col >> lv)
        parts[f"level{lv}"] = m
    n = np.arange(32)[None, :]
    for t in range(2):
        dist = (row + P * t) - (16 * n + 31)
        ok = (dist >= 0) & (n < NC)
        parts[f"cmp{t}"] = np.concatenate([np.where(ok, -dist * s, NEG) for s in SLOPES2], 1)
    parts["rowvalid"] = (i >= 31)[:, None]
    for name, v in (("eps_ln", 1e-5), ("eps_ln4", 4e-5), ("eps_rms", 1e-6), ("one", 1.0), ("zero", 0.0)):
        parts[name] = np.full((P, 1), v)
    at, off = {}, 0
    for k, v in parts.items():
        at[k] = (off, v.shape[1])
        off += v.shape[1]
    return np.concatenate([np.asarray(v, np.float32) for v in parts.values()], 1), at


COLS = (("ln_g0", KD), ("ln_b0", KD), ("ln_g1", KD), ("ln_b1", KD), ("mix_pre", KD), ("ffn_pre", KD), ("b_gate", 24),
        ("conv_qkv", 48), ("conv_ffn", 3 * 2 * NF), ("conv_ffn_b", 2 * NF), ("pos_k", 16), ("pos_v", 16))
BIG_ROWS = (("ln_g0", "ln_b0"), ("ln_g1", "ln_b1"), ("ln_g2", "ln_b2"), ("mix_post",), ("ffn_post",), ("ple_post",))
SMALL_ROWS = (("gdn_norm", P), ("subln", 64), ("lambda", P), ("a_log", HG), ("dt_bias", HG))


def offsets(items):
    at, off = {}, 0
    for k, n in items:
        at[k] = off
        off += n
    return at, off


COL_AT, N_COLS = offsets(COLS)
SROW_AT, N_SROW = offsets(SMALL_ROWS)


def stream_parts():
    ffn = 3 * 8 * NF
    return (("ffn0", ffn), ("qk", 18 * 8), ("v", 9 * 8), ("gate", 24 * 8), ("branch", 72), ("w_out", 64), ("ffn1", ffn),
            ("conv", 12 * 8), ("small", 32), ("z", 32), ("kc", 8), ("vc", 8), ("qb", 32), ("ks", 8), ("kw", 8),
            ("w1k", 32), ("w1v", 32), ("w2", 8), ("gmix", 128), ("ab", 64), ("w_o", 64), ("ple", 16), ("ffn2", ffn),
            ("ple_gate", 64))


PART_AT, N_BLOCKS = offsets(stream_parts())
N_CHUNKS = -(-N_BLOCKS // CB)


def job_table():
    jobs = []

    def job(name, *frees):
        jobs.append((name, frees))

    def ffn(n):
        for f in range(NF):
            job(f"ffn{n}.{f}", ("hidden", NF * n + f + 1) if n < 2 else ("taps", f + 1))

    def turn(i):
        for g in range(4):
            job(f"turn{i}.{g}", ("xT_ready", 8 * i + 2 * g + 2))

    ffn(0)
    turn(0)
    for t in range(18):
        job(f"qk{t}", ("qk_ready", t + 1))
    for c in range(3):
        for tok in range(2):
            job(f"v{c}.{tok}", ("v_ready", 2 * c + tok + 1))
    for i in range(N_INST1 + 2):
        attention_jobs(job, i, 0, N_INST1)
        if i < 16:
            job(f"gate{i}", ("gate_raw", i + 1))
    for i in range(H1 + 3):
        if i < H1:
            job(f"sbz{i}", ("sb_neg", i + 1))
        if 1 <= i <= H1:
            job(f"sbr{i - 1}", ("sb_exponent", i))
        if i >= 3:
            job(f"sbo{i - 3}", ("sb_out", i - 2))
        if i < 8:
            job(f"gate{16 + i}", ("gate_raw", 17 + i))
    for k in range(5):
        job(f"oT{k}", ("oT_ready", k + 1))
    for n in range(8):
        job(f"branch{n}.a", ("branch_a", n + 1))
        job(f"branch{n}.b", ("branch_b", n + 1))
    turn(1)
    ffn(1)
    turn(2)
    for t in range(12):
        job(f"conv{t}", ("qkv_taps", t + 1))
    for tok in range(2):
        job(f"small{tok}", ("small_ready", tok + 1))
    for tok in range(2):
        job(f"z{tok}", ("z_ready", tok + 1))
    job("kc", ("kc_shifted", 1))
    job("vc", ("vc_shifted", 1))
    for t in range(4):
        job(f"qb{t}", ("qb_ready", t + 1))
    job("ks", ("kdup_ready", 1))
    job("kw", ("kdup_ready", 2))
    for t in range(4):
        job(f"l2_{t}", ("l2_log", t + 1))
    job("hk", ("cmp_hidden", 1))
    job("hv", ("cmp_hidden", 2))
    job("kc2", ("kcomp_ready", 1))
    job("vc2", ("vcomp_ready", 1))
    job("gcum", ("gcum_ready", 1))
    for c in range(2):
        job(f"grow{c}", ("decay_arg", c + 1), ("tail_arg", 1))
    for c in range(2):
        job(f"brow{c}", ("beta_row", c + 1))
    for c in range(2):
        job(f"ktm{c}", ("ktm_ready", c + 1))
        job(f"vtm{c}", ("vtm_ready", c + 1))
        job(f"kk{c}", ("kk_ready", c + 1))
        job(f"qk2_{c}", ("qkd_ready", c + 1))
    for c in range(2):
        job(f"x0_{c}", ("x_ready", c + 1))
    for lv in range(1, LEVELS):
        for c in range(2):
            job(f"y{lv}.{c}", ("y_ready", 2 * (lv - 1) + c + 1))
        for c in range(2):
            job(f"zt{lv}.{c}", ("xt_ready", 2 * lv + c + 1))
            if lv < LEVELS - 1:
                job(f"zz{lv}.{c}", ("x_ready", 2 * lv + c + 1))
        for k in range(2):
            job(f"gmix{2 * (lv - 1) + k}", ("gmix_raw", 2 * (lv - 1) + k + 1))
    job("u0", ("u_ready", 1))
    job("u1", ("u_ready", 2))
    job("wT", ("wT_ready", 1))
    job("state", ("state_ready", 1))
    job("ws", ("u_ready", 3))
    job("oi0", ("gdn_out", 1))
    job("oi1", ("gdn_out", 3))
    job("ox", ("gdn_out", 2))
    for tok in range(2):
        job(f"cs{tok}", ("cmp_biased", tok + 1))
    for tok in range(2):
        job(f"ct{tok}", ("cmp_pt", tok + 1))
    for tok in range(2):
        job(f"co{tok}", ("cmp_out", tok + 1))
    for i in range(N_INST2 + 2):
        attention_jobs(job, i, N_INST1, N_INST2)
        if i < 4:
            job(f"gmix{12 + i}", ("gmix_raw", 13 + i))
    for k in range(4):
        job(f"yT{k}", ("yT_ready", k + 1))
    for n in range(8):
        job(f"mix{n}", ("mix_gated", n + 1))
    for k in range(4):
        job(f"ple{k}", ("ple_ready", k + 1))
    turn(3)
    ffn(2)
    turn(4)
    return jobs


def attention_jobs(job, i, base, n):
    if i < n:
        job(f"s{base + i}", ("biased", base + i + 1))
    if 1 <= i <= n:
        job(f"t{base + i - 1}", ("pt_ready", base + i))
    if i >= 2:
        job(f"o{base + i - 2}", ("attn_out", base + i - 1))


SEMS = """p_in consts_in cols_in rows_in x_in xT_in big_rows_in0 big_rows_in1 out_stored used job_done dve_step act_step
hidden act_done taps tap_in down_done acc_done acc_read xT_ready xn_ready norm_sum var_ready std_ready sq_ready row_free
qk_ready v_ready biased row_max probs pt_ready coef attn_out gate_raw gates_ready
sb_neg sb_log sb_softplus sb_exponent sb_weight sb_out oT_ready branch_a branch_b merged lam_arg lam_exp subln_sum
subln_std o_normed qkv_tap_in qkv_taps qkv_ready qkv_sq l2_log l2_scale l2_ready small_ready z_ready kc_shifted vc_shifted
kv_pos qb_ready kdup_ready cmp_hidden kcomp_ready vcomp_ready sg_arg sg_exp sg_ready dt_arg dt_log g_ready g_rows
gcum_ready gcum_neg decay_arg decay tail_arg tail gam beta_row ktm_ready vtm_ready kk_ready lt_ready qkd_ready xt_ready
x_ready ot_ready y_ready gmix_raw gmix_ready rhs_ready u_ready wT_ready state_ready gdn_out gdn_sum gdn_std gdn_normed
cmp_biased cmp_arg cmp_probs cmp_pt cmp_out yT_ready mix_gated mixed ple_ready ple_gated final zeroed""".split()


def build(nc, x_tm, x_fm, p_fm, stream, consts, cols, big_rows, small_rows, out, const_at):
    jobs = job_table()
    index = {name: j for j, (name, _) in enumerate(jobs)}
    assert len(index) == len(jobs)

    with ExitStack() as ctx:
        block_one, block_two = ExitStack(), ExitStack()

        def sb(name, shape, where=ctx):
            return where.enter_context(nc.sbuf_tensor(name, [P] + list(shape), F32))

        S = {n: ctx.enter_context(nc.semaphore(n)) for n in SEMS}
        arrived = [ctx.enter_context(nc.semaphore(f"arrived{i}")) for i in range(RING)]
        acc = ctx.enter_context(nc.psum_tensor("acc", [P, 4, 512], F32))
        banks = ctx.enter_context(nc.psum_tensor("banks", [P, NBANK, 512], F32))

        ring = sb("ring", [RING, CB * P])
        cst = sb("cst", [consts.shape[1]])
        col = sb("col", [N_COLS])
        rows = sb("rows", [2, 2 * D])
        srow = sb("srow", [N_SROW])
        xs = sb("xs", [2, 2, D])
        res = sb("res", [2, D])
        xT = sb("xT", [KD, T])
        mT = sb("mT", [KD, T])
        act_buf = sb("act_buf", [2, 2 * T])
        gel = sb("gel", [2, T])
        hT = sb("hT", [GROUP, T])
        stat = sb("stat", [64])
        sS = sb("sS", [2, 384])
        prob = sb("prob", [2, 384])
        pT = sb("pT", [2, 384])
        nmx = sb("nmx", [2, 2])
        den = sb("den", [2, 2])
        coef = sb("coef", [2, 2])
        tmp = sb("tmp", [2, 2 * T])

        def c(name, lo=0, n=None):
            off, w = const_at[name]
            return cst[:, off + lo:off + (lo + n if n else w)]

        def pcol(name, i):
            return col[:, COL_AT[name] + i:COL_AT[name] + i + 1]

        def sr(name, n, lo=0):
            return srow[:, SROW_AT[name] + lo:SROW_AT[name] + lo + n]

        ident, ones = c("ident"), c("ones")

        qkT = sb("qkT", [18, T], block_one)
        v1 = sb("v1", [2, 3 * W1], block_one)
        gates1 = sb("gates1", [3, 8, T], block_one)
        o1 = sb("o1", [2, 3 * W1], block_one)
        zm = res[:].rearrange("p a n -> p (a n)")[:, 0:1152].rearrange("p (a n) -> p a n", a=3)
        lg = mT[:].rearrange("p a n -> p (a n)")[:, 0:1152].rearrange("p (a n) -> p a n", a=3)
        sp = xs[:, 0].rearrange("p a n -> p (a n)")[:, 0:1152].rearrange("p (a n) -> p a n", a=3)
        wT_sb = sb("wT_sb", [3, 384], block_one)
        sq1 = tmp[:].rearrange("p a n -> p (a n)")[:, 0:2 * W1].rearrange("p (a n) -> p a n", a=2)
        oT = qkT
        block_one.close()
        cv = sb("cv", [12, T], block_two)
        zs = sb("zs", [2, 512], block_two)
        sm = sb("sm", [2, 288], block_two)
        xc = sb("xc", [2, 2, T], block_two)
        rc = sb("rc", [2, 16, 2, NC], block_two)
        hh = sb("hh", [2, 2, 2 * NC], block_two)
        qbT = sb("qbT", [4, T], block_two)
        kdup = sb("kdup", [2, 2, T], block_two)
        bdk = sb("bdk", [2, 64], block_two)
        bdv = sb("bdv", [2, T], block_two)
        gates2 = sb("gates2", [2, 8, T], block_two)
        gk = sb("gk", [160], block_two)
        grow = sb("grow", [8, P], block_two)
        brep = sb("brep", [8, P], block_two)
        dec = sb("dec", [8, P], block_two)
        ktm = sb("ktm", [2, 512], block_two)
        vtm = sb("vtm", [2, 512], block_two)
        kbg = sb("kbg", [512], block_two)
        ktail = sb("ktail", [512], block_two)
        pT_in = sb("pT_in", [2, T], block_two)
        block_two.close()
        csq = mT
        cs_sb, cpT = xc[:, 0], xc[:, 1]
        og = res[:, 0, :].rearrange("p (a n) -> p a n", a=2)
        o2 = res[:, 1, :].rearrange("p (a n) -> p a n", a=2)
        lt = xs[:, 0, 0, :].rearrange("p (a n) -> p a n", a=8)
        qkd = xs[:, 0, 1, :].rearrange("p (a n) -> p a n", a=8)
        xinv, xinvT, yb = grow, dec, brep
        ot = (act_buf[:].rearrange("p a (b n) -> p (a b) n", n=P), hT[:].rearrange("p a (b n) -> p (a b) n", n=P))
        ub = ktm
        state, wT2 = vtm[:, 0, :], vtm[:, 1, :]
        yT = cv
        ple_flat = gates2[:].rearrange("p a b t -> p (a b t)")

        block = ctx.enter_context(nc.Block())

        def bank(name):
            return banks[:, index[name] % NBANK, :]

        def job_wait(eng, name, more=0):
            eng.wait_ge(S["job_done"], index[name] + 1 + more)

        def need(eng, sem, value):
            if not isinstance(value, int) or value > 0:
                eng.wait_ge(S[sem], value)

        def instances(base):
            made = []
            if base == 0:
                for h in range(H1):
                    made.append((0 + h // 2, 3 + h // 2, 64 * (h % 2), 64, 64 * h, SLOPES1[2 * h], 64 * h, "first"))
                for h in range(H1):
                    for m in range(2):
                        made.append((6 + h // 2, 9 + h // 2, 64 * (h % 2) + 32 * m, 32, W1 + 64 * h, SLOPES1[2 * h + 1],
                                     W1 + 64 * h, "second" if m else "first"))
            else:
                for h in range(H2):
                    for kind in range(2):
                        made.append((h // 2, (kind, h // 4), 64 * (h % 2), 64, P * kind + 64 * (h // 4), SLOPES2[h],
                                     64 * h, (h, kind)))
            return made

        inst = {0: instances(0), N_INST1: instances(N_INST1)}

        @block.sync
        def _(sp_eng):
            def load(slot, chunk):
                src = stream[chunk] if isinstance(chunk, int) else stream[bass.ds(chunk, 1)].rearrange("a p n -> (a p) n")
                sp_eng.dma_start(ring[:, slot, :], src).then_inc(arrived[slot], 16)

            for s in range(RING):
                load(s, s)
            full = N_CHUNKS // RING
            with nc.sync.Fori(1, full) as g:
                for s in range(RING):
                    sp_eng.wait_ge(S["used"], RING * g + (s - RING + 1))
                    load(s, RING * g + s)
            for ch in range(full * RING, N_CHUNKS):
                sp_eng.wait_ge(S["used"], ch - RING + 1)
                load(ch % RING, ch)
            sp_eng.wait_ge(S["final"], 2)
            for tok in range(2):
                sp_eng.dma_start(out[0, P * tok:P * tok + P, :], xs[:, 0, tok, :]).then_inc(S["out_stored"], 16)
            sp_eng.wait_ge(S["out_stored"], 32)

        def level_masks(pool):
            pool.wait_ge(S["xn_ready"], 6)
            nc.gpsimd.dma_start(pT_in[:], p_fm).then_inc(S["p_in"], 16)
            nc.gpsimd.memset(bdk[:], 0.0).then_inc(S["zeroed"], 1)
            nc.gpsimd.memset(bdv[:], 0.0).then_inc(S["zeroed"], 1)
            pool.wait_ge(S["lt_ready"], 2)
            for lv in range(LEVELS):
                if lv == 2:
                    pool.wait_ge(S["xt_ready"], 2)
                if lv >= 3:
                    job_wait(pool, f"y{lv - 2}.1")
                nc.gpsimd.tensor_tensor(ot[lv % 2], lt, c(f"level{lv}").unsqueeze(1).broadcast_to([P, 8, P]),
                                        ALU.mult).then_inc(S["ot_ready"], 1)

        @block.gpsimd
        def _(pool):
            def rows_in(k):
                n = len(BIG_ROWS[k]) * D
                nc.gpsimd.dma_start(rows[:, k % 2, 0:n], big_rows[k:k + 1, 0:n].partition_broadcast(P)
                                    ).then_inc(S[f"big_rows_in{k % 2}"], 16)

            rows_in(0)
            rows_in(1)
            for k in range(2, len(BIG_ROWS)):
                pool.wait_ge(S["row_free"], k - 1)
                if k == 3:
                    level_masks(pool)
                rows_in(k)

        @block.tensor
        def _(pe):
            at = [0]
            now = [0]
            release = [False]

            def weights(n):
                b = at[0]
                at[0] += n
                if b % CB == 0:
                    ch = b // CB
                    pe.wait_ge(arrived[ch % RING], 16 * (ch // RING + 1))
                    release[0] = ch > 0
                slot, pos = (b // CB) % RING, b % CB
                return ring[:, slot, pos * P:(pos + n) * P]

            def mm(o, lhsT, rhs, start, stop, **kw):
                ins = nc.tensor.matmul(o, lhsT, rhs, start=start, stop=stop, **kw)
                if release[0] and not stop:
                    ins.then_inc(S["used"], 1)
                    release[0] = False
                return ins

            def take(name):
                assert jobs[now[0]][0] == name, (jobs[now[0]][0], name)
                j = now[0]
                now[0] += 1
                if j >= NBANK:
                    for sem, value in jobs[j - NBANK][1]:
                        pe.wait_ge(S[sem], value)
                return bank(name)

            def done(ins):
                ins.then_inc(S["job_done"], 1)

            def project_fm(name, src, half=None):
                o = take(name)
                for k in range(KD):
                    last = mm(o[:, 0:T], weights(1), src[:, k, :], k == 0, k == KD - 1)
                done(last)

            def project_tm(names, width, stored, src):
                o = [take(n) for n in names]
                for k in range(KD):
                    w = weights(stored)
                    for tok in range(2):
                        last = mm(o[tok][:, 0:width], src[:, k, P * tok:P * tok + P], w[:, 0:width], k == 0, k == KD - 1)
                        if k == KD - 1:
                            done(last)

            def into_acc(src, k, first, last, count=True):
                for half in range(2):
                    w = weights(4)
                    for tok in range(2):
                        ins = mm(acc[:, 2 * tok + half, :], src[:, P * tok:P * tok + P], w, first, last)
                return ins

            def turn(i):
                for g in range(4):
                    o = take(f"turn{i}.{g}")
                    for kk in range(2):
                        for tok in range(2):
                            if g == 0 and kk == 0:
                                pe.wait_ge(S["xn_ready"], 2 * i + tok + 1)
                            k = 2 * g + kk
                            last = nc.tensor.transpose(o[:, (2 * kk + tok) * P:(2 * kk + tok + 1) * P],
                                                       res[:, tok, k * P:(k + 1) * P], ident)
                    done(last)

            def ffn(n):
                b0, j0 = PART_AT[f"ffn{n}"], index[f"ffn{n}.0"]

                def gate_up(f, it=0):
                    at[0] = b0 + (0 if f == 0 else 24 * f - 8)
                    o = banks[:, (j0 + f) % NBANK, :]
                    for half in range(2):
                        for k in range(KD):
                            if half == 0 and k == 0:
                                if j0 + f < NBANK:
                                    pass
                                elif f < NBANK:
                                    for sem, value in jobs[j0 + f - NBANK][1]:
                                        pe.wait_ge(S[sem], value)
                                else:
                                    sem, value = jobs[j0 + f - NBANK][1][0]
                                    pe.wait_ge(S[sem], value + GROUP * it)
                            last = mm(o[:, half * T:half * T + T], loop_weights(1, it), xT[:, k, :], k == 0, k == KD - 1)
                    done(last)

                def loop_weights(nb, it):
                    b = at[0]
                    at[0] += nb
                    ch = b // CB
                    if b % CB == 0:
                        pe.wait_ge(arrived[ch % RING], 16 * (ch // RING + 1) + 16 * TURNS * it)
                        release[0] = ch > 0
                    return ring[:, ch % RING, (b % CB) * P:(b % CB + nb) * P]

                def down(f, it=0):
                    at[0] = b0 + 24 * f + 32 if f < NF - 1 else b0 + 24 * f + 16
                    pe.wait_ge(S["hidden"], NF * n + f + 1 + GROUP * it)
                    if f == 0:
                        need(pe, "acc_read", 4 * n_acc_before)
                    for half in range(2):
                        w = loop_weights(4, it)
                        for tok in range(2):
                            first, last = isinstance(it, int) and f + GROUP * it == 0, isinstance(it, int) and f == NF - 1
                            ins = mm(acc[:, 2 * tok + half, :], hT[:, f % GROUP, P * tok:P * tok + P], w, first, last,
                                     skip_group_check=True)
                    if f == NF - 1:
                        ins.then_inc(S["acc_done"], 1)
                    else:
                        ins.then_inc(S["down_done"], 1)

                n_acc_before = (0, 2, 4)[n]
                gate_up(0)
                for f in range(1, 1 + GROUP):
                    gate_up(f)
                    down(f - 1)
                with nc.tensor.Fori(1, (NF - 2) // GROUP) as it:
                    for f in range(1, 1 + GROUP):
                        gate_up(f + GROUP, it - 1)
                        down(f - 1 + GROUP, it - 1)
                f = NF - 1
                gate_up(f)
                down(f - 1)
                down(f)
                now[0] = j0 + NF
                at[0] = b0 + 24 * NF

            def attention(step, base, n, kq, kk, v, src_inst):
                i = step
                if i < n:
                    qi, ki, row, depth, *_ = src_inst[i]
                    o = take(f"s{base + i}")
                    q = kq(qi)[row:row + depth, :]
                    k = kk(ki)[row:row + depth, :]
                    mm(o[:, 0:P], q[:, 0:P], k[:, 0:P], True, True)
                    done(mm(o[:, P:3 * P], q[:, P:T], k[:, 0:T], True, True))
                if 1 <= i <= n:
                    j = base + i - 1
                    o = take(f"t{j}")
                    pe.wait_ge(S["probs"], 2 * (j + 1))
                    for b in range(3):
                        last = nc.tensor.transpose(o[:, b * P:(b + 1) * P], prob[:, j % 2, b * P:(b + 1) * P], ident)
                    done(last)
                if i >= 2:
                    j = base + i - 2
                    vc = src_inst[i - 2][4]
                    o = take(f"o{j}")
                    pe.wait_ge(S["pt_ready"], j + 1)
                    mm(o[:, 0:64], pT[:, j % 2, 0:P], v[:, 0, vc:vc + 64], True, True)
                    mm(o[:, 64:P], pT[:, j % 2, P:2 * P], v[:, 0, vc:vc + 64], True, False)
                    done(mm(o[:, 64:P], pT[:, j % 2, 2 * P:3 * P], v[:, 1, vc:vc + 64], False, True))

            pe.wait_ge(S["xT_in"], 16)
            ffn(0)
            pe.wait_ge(S["consts_in"], 16)
            turn(0)
            pe.wait_ge(S["xT_ready"], 8)
            for t in range(18):
                project_fm(f"qk{t}", xT)
            for ch in range(3):
                project_tm([f"v{ch}.0", f"v{ch}.1"], 512 if ch < 2 else P, 4 if ch < 2 else 1, xT)
            pe.wait_ge(S["qk_ready"], 18)
            pe.wait_ge(S["v_ready"], 6)
            for i in range(N_INST1 + 2):
                attention(i, 0, N_INST1, lambda t: qkT[:, t, :], lambda t: qkT[:, t, :], v1, inst[0])
                if i < 16:
                    project_fm(f"gate{i}", xT)
            for i in range(H1 + 3):
                if i < H1:
                    o = take(f"sbz{i}")
                    r = 64 * (i % 2)
                    q, k = qkT[r:r + 64, 12 + i // 2, :], qkT[r:r + 64, 15 + i // 2, :]
                    mm(o[:, 0:T], k[:, 0:P], q, True, True)
                    done(mm(o[:, T:T + P], k[:, P:T], q[:, P:T], True, True))
                if 1 <= i <= H1:
                    h = i - 1
                    o = take(f"sbr{h}")
                    pe.wait_ge(S["sb_softplus"], h + 1)
                    mm(o[:, 0:T], c("lower"), sp[:, h % 3, 0:T], True, False)
                    mm(o[:, P:T], ones, sp[:, h % 3, T:T + P], False, True)
                    done(mm(o[:, T:T + P], c("lower"), sp[:, h % 3, T:T + P], True, True))
                if i >= 3:
                    h = i - 3
                    o = take(f"sbo{h}")
                    pe.wait_ge(S["sb_weight"], h + 1)
                    vc = 2 * W1 + 64 * h
                    mm(o[:, 0:64], wT_sb[:, h % 3, 0:P], v1[:, 0, vc:vc + 64], True, True)
                    mm(o[:, 64:P], wT_sb[:, h % 3, P:T], v1[:, 0, vc:vc + 64], True, False)
                    done(mm(o[:, 64:P], wT_sb[:, h % 3, T:T + P], v1[:, 1, vc:vc + 64], False, True))
                if i < 8:
                    project_fm(f"gate{16 + i}", xT)
            pe.wait_ge(S["o_normed"], 1)
            for k in range(5):
                o = take(f"oT{k}")
                if k == 3:
                    pe.wait_ge(S["sb_out"], H1)
                for kk in range(2 if k < 4 else 1):
                    for tok in range(2):
                        f = 2 * k + kk
                        last = nc.tensor.transpose(o[:, (2 * kk + tok) * P:(2 * kk + tok + 1) * P],
                                                   o1[:, tok, f * P:(f + 1) * P], ident)
                done(last)
            pe.wait_ge(S["oT_ready"], 5)
            for n in range(8):
                o = take(f"branch{n}.a")
                for b in range(2):
                    for k in range(3):
                        last = mm(o[:, b * T:b * T + T], weights(1), oT[:, 3 * b + k, :], k == 0, k == 2)
                done(last)
                o = take(f"branch{n}.b")
                for k in range(3):
                    last = mm(o[:, 0:T], weights(1), oT[:, 6 + k, :], k == 0, k == 2)
                done(last)
            for k in range(KD):
                pe.wait_ge(S["merged"], k + 1)
                if k == 0:
                    pe.wait_ge(S["acc_read"], 4)
                last = into_acc(mT[:, k, :], k, k == 0, k == KD - 1)
            last.then_inc(S["acc_done"], 1)
            turn(1)
            pe.wait_ge(S["xT_ready"], 16)
            ffn(1)
            turn(2)
            pe.wait_ge(S["xT_ready"], 24)
            for t in range(12):
                project_fm(f"conv{t}", xT)
            project_tm(["small0", "small1"], 288, 4, xT)
            project_tm(["z0", "z1"], 512, 4, xT)
            project_fm("kc", xT)
            project_fm("vc", xT)
            for t in range(4):
                project_fm(f"qb{t}", xT)
            project_fm("ks", xT)
            project_fm("kw", xT)
            for t in range(4):
                o = take(f"l2_{t}")
                pe.wait_ge(S["qkv_sq"], 2 * t + 2)
                nc.tensor.matmul(o[:, 0:T], ones, csq[:, 2 * t, :], start=True, stop=True)
                done(nc.tensor.matmul(o[:, T:2 * T], ones, csq[:, 2 * t + 1, :], start=True, stop=True))
            for kv, name in enumerate(("hk", "hv")):
                o = take(name)
                pe.wait_ge(S["kv_pos"], kv + 1)
                for ht in range(2):
                    for k in range(16):
                        last = mm(o[:, ht * 2 * NC:(ht + 1) * 2 * NC], weights(1),
                                  rc[:, kv, k].rearrange("p g n -> p (g n)"), k == 0, k == 15)
                done(last)
            o = take("kc2")
            pe.wait_ge(S["cmp_hidden"], 1)
            w2k = [weights(1), weights(1)]
            for ht in range(2):
                last = mm(o[0:64, 0:2 * NC], w2k[ht][:, 0:64], hh[:, 0, ht, :], ht == 0, ht == 1)
            done(last)
            o = take("vc2")
            pe.wait_ge(S["cmp_hidden"], 2)
            w2v = [weights(1), weights(1)]
            for g in range(2):
                for ht in range(2):
                    last = mm(o[0:NC, 64 * g:64 * g + 64], hh[:, 1, ht, NC * g:NC * g + NC], w2v[ht][:, 0:64],
                              ht == 0, ht == 1)
            done(last)
            at[0] = PART_AT["gmix"]
            o = take("gcum")
            pe.wait_ge(S["g_ready"], 1)
            for ch in range(2):
                last = nc.tensor.matmul(o[:, HG * ch:HG * ch + HG], c("upper"), gk[:, HG * ch:HG * ch + HG], start=True, stop=True)
            done(last)
            for ch in range(2):
                o = take(f"grow{ch}")
                pe.wait_ge(S["g_rows"], 1)
                for h in range(HG):
                    last = nc.tensor.matmul(o[:, h * P:(h + 1) * P], grow[:, HG * ch + h, :], c("upper"), start=True, stop=True)
                done(last)
            for ch in range(2):
                o = take(f"brow{ch}")
                pe.wait_ge(S["g_rows"], 2)
                for h in range(HG):
                    last = nc.tensor.matmul(o[:, h * P:(h + 1) * P], brep[:, HG * ch + h, :], ident, start=True, stop=True)
                done(last)
            pe.wait_ge(S["l2_ready"], 4)
            pe.wait_ge(S["qkv_ready"], 12)
            for ch in range(2):
                t0 = P * ch
                for name, first in ((f"ktm{ch}", 4), (f"vtm{ch}", 8)):
                    o = take(name)
                    for h in range(HG):
                        last = nc.tensor.transpose(o[:, h * P:(h + 1) * P], cv[:, first + h, t0:t0 + P], ident)
                    done(last)
                for name, first in ((f"kk{ch}", 4), (f"qk2_{ch}", 0)):
                    o = take(name)
                    for h in range(HG):
                        last = nc.tensor.matmul(o[:, h * P:(h + 1) * P], cv[:, 4 + h, t0:t0 + P],
                                                cv[:, first + h, t0:t0 + P], start=True, stop=True)
                    done(last)

            def per_head(name, ch, lhsT, rhs):
                o = take(name)
                for h in range(HG):
                    last = nc.tensor.matmul(o[:, h * P:(h + 1) * P], lhsT(HG * ch + h), rhs(HG * ch + h), start=True, stop=True)
                done(last)

            for ch in range(2):
                o = take(f"x0_{ch}")
                pe.wait_ge(S["xt_ready"], ch + 1)
                for h in range(HG):
                    last = nc.tensor.transpose(o[:, h * P:(h + 1) * P], xinvT[:, HG * ch + h, :], ident)
                done(last)
            for lv in range(1, LEVELS):
                pe.wait_ge(S["ot_ready"], lv + 1)
                for ch in range(2):
                    pe.wait_ge(S["x_ready"], 2 * (lv - 1) + ch + 1)
                    per_head(f"y{lv}.{ch}", ch, lambda m: ot[lv % 2][:, m, :], lambda m: xinv[:, m, :])
                for ch in range(2):
                    pe.wait_ge(S["y_ready"], 2 * (lv - 1) + ch + 1)
                    pe.wait_ge(S["xt_ready"], 2 * (lv - 1) + ch + 1)
                    per_head(f"zt{lv}.{ch}", ch, lambda m: yb[:, m, :], lambda m: xinvT[:, m, :])
                    if lv < LEVELS - 1:
                        per_head(f"zz{lv}.{ch}", ch, lambda m: xinvT[:, m, :], lambda m: yb[:, m, :])
                for k in range(2):
                    project_fm(f"gmix{2 * (lv - 1) + k}", xT)
            pe.wait_ge(S["rhs_ready"], 4)
            pe.wait_ge(S["xt_ready"], 2 * LEVELS)
            per_head("u0", 0, lambda m: xinvT[:, m, :], lambda m: vtm[:, 0, m * P:(m + 1) * P])
            per_head("u1", 1, lambda m: xinvT[:, m, :], lambda m: vtm[:, 1, (m - HG) * P:(m - HG + 1) * P])
            per_head("wT", 1, lambda m: kbg[:, (m - HG) * P:(m - HG + 1) * P], lambda m: xinvT[:, m, :])
            pe.wait_ge(S["u_ready"], 2)
            per_head("state", 0, lambda m: ktail[:, m * P:(m + 1) * P], lambda m: ub[:, 0, m * P:(m + 1) * P])
            pe.wait_ge(S["state_ready"], 1)
            pe.wait_ge(S["wT_ready"], 1)
            per_head("ws", 0, lambda m: wT2[:, m * P:(m + 1) * P], lambda m: state[:, m * P:(m + 1) * P])
            per_head("oi0", 0, lambda m: qkd[:, m, :], lambda m: ub[:, 0, m * P:(m + 1) * P])
            pe.wait_ge(S["u_ready"], 3)
            per_head("oi1", 1, lambda m: qkd[:, m, :], lambda m: ub[:, 1, (m - HG) * P:(m - HG + 1) * P])
            per_head("ox", 0, lambda m: cv[:, m, P:T], lambda m: state[:, m * P:(m + 1) * P])
            pe.wait_ge(S["kcomp_ready"], 1)
            pe.wait_ge(S["qb_ready"], 4)
            for tok in range(2):
                o = take(f"cs{tok}")
                for pr in range(4):
                    last = nc.tensor.matmul(o[:, 64 * pr:64 * pr + 64], qbT[:, pr, P * tok:P * tok + P], bdk[:, pr // 2, :],
                                            start=True, stop=True)
                done(last)
            for tok in range(2):
                o = take(f"ct{tok}")
                pe.wait_ge(S["cmp_probs"], tok + 1)
                for g in range(2):
                    last = nc.tensor.transpose(o[:, g * P:(g + 1) * P], cs_sb[:, tok, g * P:(g + 1) * P], ident)
                done(last)
            pe.wait_ge(S["vcomp_ready"], 1)
            for tok in range(2):
                o = take(f"co{tok}")
                pe.wait_ge(S["cmp_pt"], tok + 1)
                for g in range(2):
                    last = nc.tensor.matmul(o[:, g * T:(g + 1) * T], cpT[:, tok, g * P:(g + 1) * P], bdv[:, g, :],
                                            start=True, stop=True)
                done(last)
            pe.wait_ge(S["kdup_ready"], 2)
            for i in range(N_INST2 + 2):
                attention(i, N_INST1, N_INST2, lambda t: qbT[:, t, :], lambda t: kdup[:, t[0], t[1], :], sm, inst[N_INST1])
                if i < 4:
                    project_fm(f"gmix{12 + i}", xT)
            for k in range(4):
                o = take(f"yT{k}")
                if k == 0:
                    pe.wait_ge(S["gdn_normed"], 1)
                src = og if k < 2 else o2
                if k == 2:
                    pe.wait_ge(S["attn_out"], N_INST1 + N_INST2)
                for kk in range(2):
                    for tok in range(2):
                        f = 2 * (k % 2) + kk
                        last = nc.tensor.transpose(o[:, (2 * kk + tok) * P:(2 * kk + tok + 1) * P],
                                                   src[:, tok, f * P:(f + 1) * P], ident)
                done(last)
            pe.wait_ge(S["yT_ready"], 4)
            for n in range(8):
                o = take(f"mix{n}")
                for b in range(2):
                    for k in range(4):
                        last = mm(o[:, b * T:b * T + T], weights(1), yT[:, 4 * b + k, :], k == 0, k == 3)
                done(last)
            for k in range(KD):
                pe.wait_ge(S["mixed"], k + 1)
                if k == 0:
                    pe.wait_ge(S["acc_read"], 12)
                last = into_acc(mT[:, k, :], k, k == 0, k == KD - 1)
            last.then_inc(S["acc_done"], 1)
            pe.wait_ge(S["p_in"], 16)
            o = [take(f"ple{k}") for k in range(4)]
            for k in range(2):
                for half in range(2):
                    w = weights(4)
                    for tok in range(2):
                        last = mm(o[2 * tok + half], pT_in[:, k, P * tok:P * tok + P], w, k == 0, k == 1)
                        if k == 1 and (half, tok) == (1, 1):
                            last.then_inc(S["job_done"], 4)
            turn(3)
            pe.wait_ge(S["xT_ready"], 32)
            ffn(2)
            turn(4)
            pe.wait_ge(S["xT_ready"], 40)
            pe.wait_ge(S["acc_read"], 20)
            for k in range(KD):
                last = into_acc(xT[:, k, :], k, k == 0, k == KD - 1)
            last.then_inc(S["acc_done"], 1)
            assert now[0] == len(jobs) and at[0] == N_BLOCKS, (now, len(jobs), at, N_BLOCKS)

        @block.scalar
        def _(act):
            steps = [0]

            def link(ins):
                steps[0] += 1
                ins.then_inc(S["act_step"], 1)
                act.wait_ge(S["act_step"], steps[0])

            act.dma_start(xT[:], x_fm).then_inc(S["xT_in"], 16)
            act.dma_start(col[:], cols).then_inc(S["cols_in"], 16)
            act.dma_start(cst[:], consts).then_inc(S["consts_in"], 16)
            act.dma_start(xs[:, 0], x_tm).then_inc(S["x_in"], 16)
            act.dma_start(srow[:], small_rows.partition_broadcast(P)).then_inc(S["rows_in"], 16)

            def ffn_act(n, f, it=0):
                j = index[f"ffn{n}.0"] + f
                act.wait_ge(S["job_done"], j + 1 + GROUP * it)
                if NF * n + f >= 2:
                    act.wait_ge(S["hidden"], NF * n + f - 1 + GROUP * it)
                nc.scalar.activation(act_buf[:, f % 2, 0:T], banks[:, j % NBANK, 0:T], ACT.Silu
                                     ).then_inc(S["act_done"], 1)

            def conv_col(name, i, it, per):
                o = COL_AT[name] + i
                if isinstance(it, int):
                    return col[:, o + per * GROUP * it:o + per * GROUP * it + 1]
                return col[:, bass.ds(o + per * GROUP * it, 1)]

            def geglu_act(f, it=0):
                j = index["ffn2.0"] + f
                act.wait_ge(S["job_done"], j + 1 + GROUP * it)
                act.wait_ge(S["hidden"], 2 * NF + f - 1 + GROUP * it)
                for half in range(2):
                    last = nc.scalar.activation(act_buf[:, f % 2, half * T:half * T + T], banks[:, j % NBANK, half * T:half * T + T],
                                                ACT.Identity, bias=conv_col("conv_ffn_b", half * NF + f, it, 1),
                                                scale=conv_col("conv_ffn", 3 * (half * NF + f) + 2, it, 3))
                last.then_inc(S["tap_in"], 1)
                act.wait_ge(S["taps"], f + 1 + GROUP * it)
                nc.scalar.activation(gel[:, f % 2, :], act_buf[:, f % 2, 0:T], ACT.Gelu_apprx_tanh).then_inc(S["act_done"], 1)

            def over_ffn(body):
                for f in range(0, 1 + GROUP):
                    body(f)
                with nc.scalar.Fori(1, (NF - 2) // GROUP) as it:
                    for f in range(1, 1 + GROUP):
                        body(f + GROUP, it - 1)
                body(NF - 1)

            def std(i, col_in, col_out, scale, eps):
                nc.scalar.activation(stat[:, col_out:col_out + 2], stat[:, col_in:col_in + 2], ACT.Sqrt, bias=c(eps), scale=scale
                                     ).then_inc(S["std_ready"], 1)

            def turn(i, gain=None, bias=None):
                for g in range(4):
                    job_wait(act, f"turn{i}.{g}")
                    for kk in range(2):
                        k = 2 * g + kk
                        src = bank(f"turn{i}.{g}")[:, kk * T:kk * T + T]
                        if gain is None:
                            ins = nc.scalar.copy(xT[:, k, :], src)
                        elif bias is None:
                            ins = nc.scalar.activation(xT[:, k, :], src, ACT.Copy, scale=pcol(gain, k))
                        else:
                            ins = nc.scalar.activation(xT[:, k, :], src, ACT.Identity, bias=pcol(bias, k), scale=pcol(gain, k))
                        ins.then_inc(S["xT_ready"], 1)

            def attention(i, base, n):
                if i < n:
                    j = base + i
                    act.wait_ge(S["row_max"], 2 * (j + 1))
                    if j >= 2:
                        if i >= 2:
                            job_wait(act, f"t{j - 2}")
                        act.wait_ge(S["coef"], j - 1)
                    for t, lo, hi in ((0, 0, P), (1, P, 3 * P)):
                        nc.scalar.activation(prob[:, j % 2, lo:hi], sS[:, j % 2, lo:hi], ACT.Exp, bias=nmx[:, j % 2, t:t + 1],
                                             accum_out=den[:, j % 2, t:t + 1]).then_inc(S["probs"], 1)
                if 1 <= i <= n:
                    j = base + i - 1
                    job_wait(act, f"t{j}")
                    if i >= 3:
                        job_wait(act, f"o{j - 2}")
                    nc.scalar.copy(pT[:, j % 2, :], bank(f"t{j}")[:, 0:384]).then_inc(S["pt_ready"], 1)

            over_ffn(lambda f, it=0: ffn_act(0, f, it))
            act.wait_ge(S["consts_in"], 16)
            act.wait_ge(S["cols_in"], 16)
            act.wait_ge(S["var_ready"], 1)
            std(0, 0, 4, 1.0, "eps_ln4")
            turn(0, "ln_g0", "ln_b0")
            scale = {0: 0.125, 2: float(np.float32(32 ** -0.5)), 4: 0.125}
            for t in range(18):
                job_wait(act, f"qk{t}")
                ps = bank(f"qk{t}")[:, 0:T]
                nc.scalar.activation(qkT[:, t, :], ps, ACT.Copy, scale=scale.get(t // 3, 1.0)).then_inc(S["qk_ready"], 1)
            act.wait_ge(S["lam_arg"], 1)
            nc.scalar.activation(stat[:, 18:20], stat[:, 16:18], ACT.Exp).then_inc(S["lam_exp"], 1)

            def gate_raw(k):
                job_wait(act, f"gate{k}")
                nc.scalar.activation(gates1[:, k // 8, k % 8, :], bank(f"gate{k}")[:, 0:T], ACT.Identity,
                                     bias=pcol("b_gate", k)).then_inc(S["gate_raw"], 1)

            for i in range(N_INST1 + 2):
                attention(i, 0, N_INST1)
                if i < 16:
                    gate_raw(i)
            for i in range(H1 + 3):
                if i < H1:
                    act.wait_ge(S["sb_neg"], i + 1)
                    link(nc.scalar.activation(lg[:, i % 3, :], lg[:, i % 3, :], ACT.Exp))
                    nc.scalar.activation(lg[:, i % 3, :], lg[:, i % 3, :], ACT.Ln, bias=c("one")).then_inc(S["sb_log"], 1)
                if 2 <= i < H1 + 2:
                    h = i - 2
                    act.wait_ge(S["sb_exponent"], h + 1)
                    if h >= 3:
                        job_wait(act, f"sbo{h - 3}")
                    nc.scalar.activation(wT_sb[:, h % 3, :], zm[:, h % 3, :], ACT.Exp).then_inc(S["sb_weight"], 1)
                if i < 8:
                    gate_raw(16 + i)
            act.wait_ge(S["subln_sum"], 1)
            nc.scalar.activation(stat[:, 32:44], stat[:, 20:32], ACT.Sqrt, bias=c("eps_ln"), scale=1.0 / 64
                                 ).then_inc(S["subln_std"], 1)
            act.wait_ge(S["gate_raw"], 24)
            g1 = gates1[:].rearrange("p a b t -> p (a b t)")
            nc.scalar.activation(g1, g1, ACT.Sigmoid).then_inc(S["gates_ready"], 1)
            act.wait_ge(S["var_ready"], 2)
            std(1, 0, 4, 1.0, "eps_ln")
            turn(1, "ln_g1", "ln_b1")
            over_ffn(lambda f, it=0: ffn_act(1, f, it))
            act.wait_ge(S["var_ready"], 3)
            std(2, 0, 4, 1.0, "eps_ln4")

            def sum_squares(k, src, junk):
                for tok in range(2):
                    ins = nc.scalar.activation(junk, src(tok), ACT.Square, accum_out=stat[:, 8 + tok:9 + tok])
                    if tok == 0:
                        link(ins)
                    else:
                        ins.then_inc(S["sq_ready"], 1)
                act.wait_ge(S["sq_ready"], k)
                std(0, 8, 4, 1.0 / D, "eps_rms")

            junk2 = tmp[:].rearrange("p a b -> p (a b)")
            act.wait_ge(S["norm_sum"], 1)
            sum_squares(1, lambda tok: xs[:, 1, tok, :], junk2)
            turn(2, "mix_pre")

            def conv_silu(t):
                act.wait_ge(S["qkv_taps"], t + 1)
                nc.scalar.activation(cv[:, t, :], cv[:, t, :], ACT.Silu).then_inc(S["qkv_ready"], 1)
                if t < 8:
                    act.wait_ge(S["qkv_ready"], t + 1)
                    nc.scalar.activation(csq[:, t, :], cv[:, t, :], ACT.Square).then_inc(S["qkv_sq"], 1)

            for t in range(12):
                job_wait(act, f"conv{t}")
                nc.scalar.activation(cv[:, t, :], bank(f"conv{t}")[:, 0:T], ACT.Copy, scale=pcol("conv_qkv", 4 * t + 3)
                                     ).then_inc(S["qkv_tap_in"], 1)
                if t >= 1:
                    conv_silu(t - 1)
            conv_silu(11)
            for tok in range(2):
                job_wait(act, f"z{tok}")
                nc.scalar.activation(zs[:, tok, :], bank(f"z{tok}"), ACT.Silu).then_inc(S["z_ready"], 1)
            act.wait_ge(S["sg_arg"], 1)
            nc.scalar.activation(sm[:, :, 256:284], sm[:, :, 256:284], ACT.Exp, scale=-1.0).then_inc(S["sg_exp"], 1)
            act.wait_ge(S["dt_arg"], 1)
            link(nc.scalar.activation(gk[:, 24:32], gk[:, 24:32], ACT.Exp))
            nc.scalar.activation(gk[:, 24:32], gk[:, 24:32], ACT.Ln, bias=c("one"))
            nc.scalar.activation(gk[:, 32:36], sr("a_log", HG), ACT.Exp).then_inc(S["dt_log"], 1)
            for t in range(4):
                job_wait(act, f"qb{t}")
                nc.scalar.activation(qbT[:, t, :], bank(f"qb{t}")[:, 0:T], ACT.Copy, scale=0.125).then_inc(S["qb_ready"], 1)
            for t in range(4):
                job_wait(act, f"l2_{t}")
                pair = csq[:, 2 * t:2 * t + 2, :].rearrange("p a t -> p (a t)")
                nc.scalar.activation(pair, bank(f"l2_{t}"), ACT.Ln, bias=c("eps_rms")).then_inc(S["l2_log"], 1)
                act.wait_ge(S["l2_log"], t + 1)
                nc.scalar.activation(pair, pair, ACT.Exp, scale=-0.5).then_inc(S["l2_scale"], 1)
            for kv, name in enumerate(("hk", "hv")):
                job_wait(act, name)
                nc.scalar.activation(hh[:, kv].rearrange("p a n -> p (a n)"), bank(name)[:, 0:4 * NC], ACT.Gelu_apprx_tanh
                                     ).then_inc(S["cmp_hidden"], 1)
            act.wait_ge(S["gcum_neg"], 1)
            nc.scalar.activation(gk[:, 64:72], gk[:, 40:48], ACT.Exp).then_inc(S["gam"], 1)
            act.wait_ge(S["tail_arg"], 1)
            nc.scalar.activation(gk[:, 72:76], gk[:, 72:76], ACT.Exp).then_inc(S["tail"], 1)
            for ch in range(2):
                act.wait_ge(S["decay_arg"], ch + 1)
                for h in range(HG):
                    m = HG * ch + h
                    nc.scalar.activation(dec[:, m, :], dec[:, m, :], ACT.Exp, bias=gk[:, 48 + m:49 + m]).then_inc(S["decay"], 1)
            for ch in range(2):
                job_wait(act, f"ktm{ch}")
                nc.scalar.copy(ktm[:, ch, :], bank(f"ktm{ch}")).then_inc(S["ktm_ready"], 1)
                job_wait(act, f"vtm{ch}")
                nc.scalar.copy(vtm[:, ch, :], bank(f"vtm{ch}")).then_inc(S["vtm_ready"], 1)

            def gmix_raw(k):
                job_wait(act, f"gmix{k}")
                nc.scalar.copy(gates2[:, k // 8, k % 8, :], bank(f"gmix{k}")[:, 0:T]).then_inc(S["gmix_raw"], 1)

            for lv in range(1, LEVELS):
                for ch in range(2):
                    job_wait(act, f"y{lv}.{ch}")
                    nc.scalar.copy(yb[:, HG * ch:HG * ch + HG, :].rearrange("p a t -> p (a t)"), bank(f"y{lv}.{ch}")
                                   ).then_inc(S["y_ready"], 1)
                for k in range(2):
                    gmix_raw(2 * (lv - 1) + k)
            for ch in range(2):
                job_wait(act, f"u{ch}")
                nc.scalar.copy(ub[:, ch, :], bank(f"u{ch}")).then_inc(S["u_ready"], 1)
            job_wait(act, "wT")
            nc.scalar.copy(wT2, bank("wT")).then_inc(S["wT_ready"], 1)
            job_wait(act, "state")
            nc.scalar.copy(state, bank("state")).then_inc(S["state_ready"], 1)
            for tok in range(2):
                act.wait_ge(S["cmp_arg"], tok + 1)
                nc.scalar.activation(cs_sb[:, tok, :], cs_sb[:, tok, :], ACT.Exp).then_inc(S["cmp_probs"], 1)
            for tok in range(2):
                job_wait(act, f"ct{tok}")
                nc.scalar.copy(cpT[:, tok, :], bank(f"ct{tok}")[:, 0:T]).then_inc(S["cmp_pt"], 1)
            for i in range(N_INST2 + 2):
                attention(i, N_INST1, N_INST2)
                if i < 4:
                    gmix_raw(12 + i)
            act.wait_ge(S["gdn_sum"], 1)
            nc.scalar.activation(stat[:, 32:40], stat[:, 20:28], ACT.Sqrt, bias=c("eps_rms"), scale=1.0 / P
                                 ).then_inc(S["gdn_std"], 1)
            act.wait_ge(S["gmix_raw"], 16)
            g2 = gates2[:].rearrange("p a b t -> p (a b t)")
            nc.scalar.activation(g2, g2, ACT.Sigmoid).then_inc(S["gmix_ready"], 1)
            for k in range(4):
                job_wait(act, f"yT{k}")
                nc.scalar.copy(yT[:, 2 * k:2 * k + 2, :].rearrange("p a t -> p (a t)"), bank(f"yT{k}")).then_inc(S["yT_ready"], 1)
            act.wait_ge(S["acc_done"], 4)
            act.wait_ge(S["mixed"], 8)
            sum_squares(2, lambda tok: acc[:, 2 * tok:2 * tok + 2, :].rearrange("p a n -> p (a n)"), junk2)
            for k in range(4):
                job_wait(act, f"ple{k}")
                nc.scalar.copy(ple_flat[:, 512 * k:512 * k + 512], bank(f"ple{k}")).then_inc(S["ple_ready"], 1)
            act.wait_ge(S["norm_sum"], 2)
            sum_squares(3, lambda tok: xs[:, 0, tok, :], junk2)
            turn(3, "ffn_pre")
            over_ffn(geglu_act)
            act.wait_ge(S["acc_done"], 5)
            sum_squares(4, lambda tok: acc[:, 2 * tok:2 * tok + 2, :].rearrange("p a n -> p (a n)"), junk2)
            turn(4)
            act.wait_ge(S["acc_done"], 6)
            for tok in range(2):
                nc.scalar.activation(res[:, tok, :], acc[:, 2 * tok:2 * tok + 2, :].rearrange("p a n -> p (a n)"), ACT.Sigmoid
                                     ).then_inc(S["acc_read"], 1)
            act.wait_ge(S["ple_gated"], 2)
            sum_squares(5, lambda tok: res[:, tok, :], junk2)

        @block.vector
        def _(dve):
            steps = [0]
            v = nc.vector

            def link(ins):
                steps[0] += 1
                ins.then_inc(S["dve_step"], 1)
                dve.wait_ge(S["dve_step"], steps[0])

            def mark(ins, sem, value):
                ins.then_inc(S[sem], 1)
                dve.wait_ge(S[sem], value)

            def hidden(n, f, it=0):
                j = index[f"ffn{n}.0"] + f
                dve.wait_ge(S["act_done"], NF * n + f + 1 + GROUP * it)
                if f >= GROUP:
                    dve.wait_ge(S["down_done"], (NF - 1) * n + f - GROUP + 1 + GROUP * it)
                v.tensor_tensor(hT[:, f % GROUP, :], act_buf[:, f % 2, 0:T], banks[:, j % NBANK, T:2 * T], ALU.mult
                                ).then_inc(S["hidden"], 1)

            def conv_col(i, it):
                o = COL_AT["conv_ffn"] + i
                if isinstance(it, int):
                    return col[:, o:o + 1]
                return col[:, bass.ds(o + 3 * GROUP * it, 1)]

            def conv_hidden(f, it=0):
                j = index["ffn2.0"] + f
                dve.wait_ge(S["tap_in"], f + 1 + GROUP * it)
                for tap in (1, 0):
                    sh = 2 - tap
                    for half in range(2):
                        buf = act_buf[:, f % 2, half * T + sh:half * T + T]
                        last = v.scalar_tensor_tensor(buf, banks[:, j % NBANK, half * T:half * T + T - sh],
                                                      conv_col(3 * (half * NF + f) + tap, it), buf, ALU.mult, ALU.add)
                    if tap == 1:
                        last.then_inc(S["dve_step"], 1)
                        dve.wait_ge(S["dve_step"], steps[0] + f + 1 + GROUP * it)
                last.then_inc(S["taps"], 1)
                dve.wait_ge(S["act_done"], 2 * NF + f + 1 + GROUP * it)
                dve.wait_ge(S["down_done"], (NF - 1) * 2 + f - GROUP + 1 + GROUP * it)
                v.tensor_tensor(hT[:, f % GROUP, :], gel[:, f % 2, :], act_buf[:, f % 2, T:2 * T], ALU.mult
                                ).then_inc(S["hidden"], 1)

            def over_ffn(body):
                for f in range(0, 1 + GROUP):
                    body(f)
                with nc.vector.Fori(1, (NF - 2) // GROUP) as it:
                    for f in range(1, 1 + GROUP):
                        body(f + GROUP, it - 1)
                body(NF - 1)

            def layer_norm(i, src, dst, factor, k, w):
                dve.wait_ge(S["acc_done"], (1, 2, 3)[i])
                for tok in range(2):
                    for half in range(2):
                        hs = slice(512 * half, 512 * half + 512)
                        mark(v.scalar_tensor_tensor(res[:, tok, hs], xs[:, src, tok, hs], factor, acc[:, 2 * tok + half, :],
                                                    ALU.mult, ALU.add), "acc_read", 4 * i + 2 * tok + half + 1)
                        link(v.bn_stats(stat[:, 44 + 6 * half:50 + 6 * half], res[:, tok, hs]))
                    link(v.bn_aggr(stat[:, 12 + 2 * tok:14 + 2 * tok], stat[:, 44:56]))
                v.tensor_copy(stat[:, 0:2], stat[:, 12:16].rearrange("p (a b) -> p a b", b=2)[:, :, 1]).then_inc(S["var_ready"], 1)
                dve.wait_ge(S["std_ready"], w)
                link(v.reciprocal(stat[:, 6:8], stat[:, 4:6]))
                for tok in range(2):
                    ins = v.tensor_scalar(res[:, tok, :], res[:, tok, :], stat[:, 12 + 2 * tok:13 + 2 * tok], stat[:, 6 + tok:7 + tok],
                                          ALU.subtract, ALU.mult)
                    if k is not None:
                        ins.then_inc(S["xn_ready"], 1)
                        dve.wait_ge(S["xn_ready"], k + tok + 1)
                    else:
                        link(ins)
                dve.wait_ge(S[f"big_rows_in{i % 2}"], 16 * (i // 2 + 1))
                for tok in range(2):
                    link(v.tensor_tensor(xs[:, dst, tok, :], res[:, tok, :], rows[:, i % 2, 0:D], ALU.mult))
                    ins = v.tensor_tensor(xs[:, dst, tok, :], xs[:, dst, tok, :], rows[:, i % 2, D:2 * D], ALU.add)
                    if tok:
                        mark(ins, "row_free", i + 1)
                    else:
                        link(ins)

            def rms_scaled(src, k, w):
                dve.wait_ge(S["std_ready"], w)
                link(v.reciprocal(stat[:, 6:8], stat[:, 4:6]))
                for tok in range(2):
                    v.tensor_scalar(res[:, tok, :], xs[:, src, tok, :], stat[:, 6 + tok:7 + tok], None, ALU.mult
                                    ).then_inc(S["xn_ready"], 1)

            def add_normed(i, src, dst, value, w, final=False):
                dve.wait_ge(S["std_ready"], w)
                link(v.reciprocal(stat[:, 6:8], stat[:, 4:6]))
                dve.wait_ge(S[f"big_rows_in{i % 2}"], 16 * (i // 2 + 1))
                for tok in range(2):
                    for half in range(2):
                        hs = slice(512 * half, 512 * half + 512)
                        ins = v.scalar_tensor_tensor(xs[:, dst, tok, hs], value(tok, half), stat[:, 6 + tok:7 + tok],
                                                     rows[:, i % 2, hs], ALU.mult, ALU.mult)
                        if final:
                            link(ins)
                        else:
                            mark(ins, "acc_read", (12, 16)[i - 3] + 2 * tok + half + 1)
                    ins = v.tensor_tensor(xs[:, dst, tok, :], xs[:, dst, tok, :], xs[:, src, tok, :], ALU.add)
                    if final:
                        ins.then_inc(S["final"], 1)
                    elif tok:
                        mark(ins, "row_free", i + 1)
                    else:
                        link(ins)

            def signal(sem):
                v.tensor_copy(stat[:, 63:64], stat[:, 6:7]).then_inc(S[sem], 1)

            def attention(i, base, n):
                if i < n:
                    j = base + i
                    slope = inst[base][i][5]
                    job_wait(dve, f"s{j}")
                    if j >= 2:
                        dve.wait_ge(S["probs"], 2 * (j - 1))
                    mark(v.scalar_tensor_tensor(sS[:, j % 2, :], c("negdist"), slope, bank(f"s{j}")[:, 0:384], ALU.mult, ALU.add),
                         "biased", j + 1)
                    for t, lo, hi in ((0, 0, P), (1, P, 3 * P)):
                        v.tensor_reduce(nmx[:, j % 2, t:t + 1], sS[:, j % 2, lo:hi], AX.X, ALU.max, negate=True
                                        ).then_inc(S["row_max"], 1)
                if i >= 1 and i <= n:
                    j = base + i - 1
                    how = inst[base][i - 1][7]
                    dve.wait_ge(S["probs"], 2 * (j + 1))
                    if isinstance(how, tuple):
                        h, kind = how
                        link(v.reciprocal(coef[:, j % 2, :], den[:, j % 2, :]))
                        mark(v.tensor_tensor(coef[:, j % 2, :], coef[:, j % 2, :], sm[:, :, T + 3 * h + kind + 1], ALU.mult),
                             "coef", j + 1)
                    elif how == "second":
                        link(v.reciprocal(coef[:, j % 2, :], den[:, j % 2, :]))
                        mark(v.tensor_scalar(coef[:, j % 2, :], coef[:, j % 2, :], stat[:, 61:62], None, ALU.mult), "coef", j + 1)
                    else:
                        mark(v.reciprocal(coef[:, j % 2, :], den[:, j % 2, :]), "coef", j + 1)
                if i >= 2:
                    j = base + i - 2
                    oc, how = inst[base][i - 2][6:8]
                    dst = o1 if base == 0 else o2
                    job_wait(dve, f"o{j}")
                    for tok in range(2):
                        src = bank(f"o{j}")[:, 64 * tok:64 * tok + 64]
                        d = dst[:, tok, oc:oc + 64]
                        if how == "first":
                            last = v.tensor_scalar(d, src, coef[:, j % 2, tok:tok + 1], None, ALU.mult)
                        else:
                            last = v.scalar_tensor_tensor(d, src, coef[:, j % 2, tok:tok + 1], d, ALU.mult, ALU.add)
                    mark(last, "attn_out", j + 1)

            over_ffn(lambda f, it=0: hidden(0, f, it))
            dve.wait_ge(S["x_in"], 16)
            layer_norm(0, 0, 1, 2 * ALPHA, 0, 1)
            dve.wait_ge(S["rows_in"], 16)
            lam = sr("lambda", P)
            la = lam.rearrange("p (a b d) -> p a b d", a=2, b=2)
            link(v.tensor_tensor(act_buf[:, 0, 0:64].rearrange("p (a d) -> p a d", a=2), la[:, :, 0, :], la[:, :, 1, :], ALU.mult))
            v.tensor_reduce(stat[:, 16:18], act_buf[:, 0, 0:64].rearrange("p (a d) -> p a d", a=2), AX.X, ALU.add
                            ).then_inc(S["lam_arg"], 1)
            for ch in range(3):
                for tok in range(2):
                    n = 512 if ch < 2 else P
                    job_wait(dve, f"v{ch}.{tok}")
                    v.tensor_copy(v1[:, tok, 512 * ch:512 * ch + n], bank(f"v{ch}.{tok}")[:, 0:n]).then_inc(S["v_ready"], 1)
            dve.wait_ge(S["lam_exp"], 1)
            link(v.tensor_tensor(stat[:, 60:61], stat[:, 19:20], stat[:, 18:19], ALU.subtract))
            link(v.tensor_scalar(stat[:, 61:62], stat[:, 60:61], -(0.8 - 0.6), None, ALU.add))
            for i in range(N_INST1 + 2):
                attention(i, 0, N_INST1)
            for i in range(H1 + 3):
                if i < H1:
                    job_wait(dve, f"sbz{i}")
                    if i >= 3:
                        dve.wait_ge(S["sb_weight"], i - 2)
                    link(v.tensor_tensor(zm[:, i % 3, :], bank(f"sbz{i}")[:, 0:384], c("sbmask"), ALU.add))
                    mark(v.scalar_tensor_tensor(lg[:, i % 3, :], zm[:, i % 3, :], -1.0, zm[:, i % 3, :], ALU.mult, ALU.min),
                         "sb_neg", i + 1)
                if 1 <= i <= H1:
                    h = i - 1
                    dve.wait_ge(S["sb_log"], h + 1)
                    mark(v.scalar_tensor_tensor(sp[:, h % 3, :], zm[:, h % 3, :], 0.0, lg[:, h % 3, :], ALU.max, ALU.add),
                         "sb_softplus", h + 1)
                if 2 <= i < H1 + 2:
                    h = i - 2
                    job_wait(dve, f"sbr{h}")
                    mark(v.tensor_tensor(zm[:, h % 3, :], zm[:, h % 3, :], bank(f"sbr{h}")[:, 0:384], ALU.subtract),
                         "sb_exponent", h + 1)
                if i >= 3:
                    h = i - 3
                    job_wait(dve, f"sbo{h}")
                    oc = 2 * W1 + 64 * h
                    v.tensor_copy(o1[:, :, oc:oc + 64], bank(f"sbo{h}")[:, 0:P].rearrange("p (a d) -> p a d", a=2)
                                  ).then_inc(S["sb_out"], 1)
            od = o1[:, :, W1:2 * W1]
            odh = od.rearrange("p a (h d) -> p a h d", d=64)
            link(v.tensor_tensor(sq1, od, od, ALU.mult))
            v.tensor_reduce(stat[:, 20:32], sq1.rearrange("p a (h d) -> p (a h) d", d=64), AX.X, ALU.add
                            ).then_inc(S["subln_sum"], 1)
            dve.wait_ge(S["subln_std"], 1)
            link(v.reciprocal(stat[:, 44:56], stat[:, 32:44]))
            link(v.tensor_scalar(stat[:, 44:56], stat[:, 44:56], 1.0 - (0.8 - 0.6), None, ALU.mult))
            for tok in range(2):
                link(v.tensor_tensor(odh[:, tok], odh[:, tok],
                                     stat[:, 44 + H1 * tok:44 + H1 * tok + H1].unsqueeze(2).broadcast_to([P, H1, 64]), ALU.mult))
                ins = v.tensor_tensor(odh[:, tok], odh[:, tok], sr("subln", 64).unsqueeze(1).broadcast_to([P, H1, 64]), ALU.mult)
            ins.then_inc(S["o_normed"], 1)
            for k in range(5):
                n = 2 if k < 4 else 1
                job_wait(dve, f"oT{k}")
                v.tensor_copy(oT[:, 2 * k:2 * k + n, :].rearrange("p a t -> p (a t)"), bank(f"oT{k}")[:, 0:n * T]
                              ).then_inc(S["oT_ready"], 1)
            dve.wait_ge(S["gates_ready"], 1)
            for n in range(8):
                job_wait(dve, f"branch{n}.a")
                mark(v.tensor_tensor(tmp[:, 0, :].rearrange("p (a t) -> p a t", a=2), gates1[:, 0:2, n, :],
                                     bank(f"branch{n}.a").rearrange("p (a t) -> p a t", a=2), ALU.mult), "branch_a", n + 1)
                job_wait(dve, f"branch{n}.b")
                mark(v.tensor_tensor(tmp[:, 1, 0:T], gates1[:, 2, n, :], bank(f"branch{n}.b")[:, 0:T], ALU.mult), "branch_b", n + 1)
                link(v.tensor_tensor(tmp[:, 0, 0:T], tmp[:, 0, 0:T], tmp[:, 0, T:2 * T], ALU.add))
                mark(v.tensor_tensor(mT[:, n, :], tmp[:, 0, 0:T], tmp[:, 1, 0:T], ALU.add), "merged", n + 1)
            layer_norm(1, 1, 0, ALPHA, 2, 2)
            over_ffn(lambda f, it=0: hidden(1, f, it))
            layer_norm(2, 0, 1, 2 * ALPHA, None, 3)
            signal("norm_sum")
            rms_scaled(1, 4, 4)

            for t in range(12):
                dve.wait_ge(S["qkv_tap_in"], t + 1)
                for tap in (2, 1, 0):
                    sh = 3 - tap
                    ins = v.scalar_tensor_tensor(cv[:, t, sh:T], bank(f"conv{t}")[:, 0:T - sh], pcol("conv_qkv", 4 * t + tap),
                                                 cv[:, t, sh:T], ALU.mult, ALU.add)
                    if tap:
                        link(ins)
                    else:
                        ins.then_inc(S["qkv_taps"], 1)
            for tok in range(2):
                job_wait(dve, f"small{tok}")
                mark(v.tensor_copy(sm[:, tok, :], bank(f"small{tok}")[:, 0:288]), "small_ready", tok + 1)
            signal("sg_arg")
            a8 = gk[:, 16:24]
            link(v.tensor_tensor(a8.rearrange("p (a h) -> p a h", a=2), sm[:, :, 284:288],
                                 sr("dt_bias", HG).unsqueeze(1).broadcast_to([P, 2, HG]), ALU.add))
            v.scalar_tensor_tensor(gk[:, 24:32], a8, -1.0, a8, ALU.mult, ALU.min).then_inc(S["dt_arg"], 1)
            dve.wait_ge(S["sg_exp"], 1)
            link(v.tensor_scalar(sm[:, :, 256:284], sm[:, :, 256:284], 1.0, None, ALU.add))
            mark(v.reciprocal(sm[:, :, 256:284], sm[:, :, 256:284]), "sg_ready", 1)
            dve.wait_ge(S["dt_log"], 1)
            link(v.scalar_tensor_tensor(gk[:, 24:32], a8, 0.0, gk[:, 24:32], ALU.max, ALU.add))
            g8 = gk[:, 0:8]
            mark(v.scalar_tensor_tensor(g8.rearrange("p (a h) -> p a h", a=2), gk[:, 24:32].rearrange("p (a h) -> p a h", a=2), -1.0,
                                        gk[:, 32:36].unsqueeze(1).broadcast_to([P, 2, HG]), ALU.mult, ALU.mult), "g_ready", 1)
            mark(v.tensor_copy(grow[:], g8.unsqueeze(2).broadcast_to([P, 8, P])), "g_rows", 1)
            b8 = gk[:, 8:16]
            link(v.tensor_copy(b8.rearrange("p (a h) -> p a h", a=2), sm[:, :, 280:284]))
            mark(v.tensor_copy(brep[:], b8.unsqueeze(2).broadcast_to([P, 8, P])), "g_rows", 2)
            for kv, name in enumerate(("kc", "vc")):
                job_wait(dve, name)
                ps = bank(name)
                for g in range(2):
                    for l in range(2):
                        last = v.tensor_copy(xc[64 * l:64 * l + 64, kv, g, 0:T - l], ps[64 * g:64 * g + 64, l:T])
                mark(last, f"{name}_shifted", 1)
                x16 = xc[:, kv, :, 0:240].rearrange("p g (n k l) -> p g n k l", k=8, l=2)[:, :, :, :, 0]
                y16 = xc[:, kv, :, 16:256].rearrange("p g (n k l) -> p g n k l", k=8, l=2)[:, :, :, :, 0]
                pos = COL_AT["pos_k" if kv == 0 else "pos_v"]
                for g in range(2):
                    for half, src in ((0, x16), (1, y16)):
                        last = v.tensor_tensor(rc[:, kv, 8 * half:8 * half + 8, g, :], src[:, g].rearrange("p n k -> p k n"),
                                               col[:, pos + 8 * half:pos + 8 * half + 8].unsqueeze(2).broadcast_to([P, 8, NC]), ALU.add)
                mark(last, "kv_pos", kv + 1)
            for kind, name in enumerate(("ks", "kw")):
                job_wait(dve, name)
                ps = bank(name)
                for g in range(2):
                    for half in range(2):
                        last = v.tensor_copy(kdup[64 * half:64 * half + 64, kind, g, :], ps[64 * g:64 * g + 64, 0:T])
                last.then_inc(S["kdup_ready"], 1)
            for t in range(4):
                dve.wait_ge(S["l2_scale"], t + 1)
                dve.wait_ge(S["qkv_ready"], 2 * t + 2)
                two = cv[:, 2 * t:2 * t + 2, :].rearrange("p a t -> p (a t)")
                v.scalar_tensor_tensor(two, two, float(np.float32(P ** -0.5)) if t < 2 else 1.0,
                                       csq[:, 2 * t:2 * t + 2, :].rearrange("p a t -> p (a t)"), ALU.mult, ALU.mult
                                       ).then_inc(S["l2_ready"], 1)
            dve.wait_ge(S["zeroed"], 2)
            job_wait(dve, "kc2")
            for g in range(2):
                for half in range(2):
                    last = v.tensor_copy(bdk[64 * half:64 * half + 64, g, 32 * half:32 * half + NC],
                                         bank("kc2")[0:64, NC * g:NC * g + NC])
            last.then_inc(S["kcomp_ready"], 1)
            job_wait(dve, "vc2")
            for g in range(2):
                for h in range(4):
                    last = v.tensor_copy(bdv[32 * h:32 * h + NC, g, 64 * h:64 * h + 64], bank("vc2")[0:NC, 64 * g:64 * g + 64])
            last.then_inc(S["vcomp_ready"], 1)
            job_wait(dve, "gcum")
            mark(v.tensor_copy(gk[:, 40:48], bank("gcum")[:, 0:8]), "gcum_ready", 1)
            mark(v.tensor_scalar(gk[:, 48:56], gk[:, 40:48], -1.0, None, ALU.mult), "gcum_neg", 1)
            job_wait(dve, "grow0")
            v.tensor_tensor(gk[:, 72:76], bank("grow0").rearrange("p (h t) -> p h t", h=HG)[:, :, P - 1], gk[:, 40:44], ALU.subtract
                            ).then_inc(S["tail_arg"], 1)
            for ch in range(2):
                job_wait(dve, f"grow{ch}")
                v.tensor_tensor(dec[:, HG * ch:HG * ch + HG, :], bank(f"grow{ch}").rearrange("p (h t) -> p h t", h=HG),
                                c("decmask").unsqueeze(1).broadcast_to([P, HG, P]), ALU.add).then_inc(S["decay_arg"], 1)
            for ch in range(2):
                job_wait(dve, f"brow{ch}")
                v.tensor_copy(brep[:, HG * ch:HG * ch + HG, :].rearrange("p h t -> p (h t)"), bank(f"brow{ch}")
                              ).then_inc(S["beta_row"], 1)
            for ch in range(2):
                hs = slice(HG * ch, HG * ch + HG)
                job_wait(dve, f"kk{ch}")
                dve.wait_ge(S["decay"], HG * (ch + 1))
                dve.wait_ge(S["beta_row"], ch + 1)
                mark(v.tensor_tensor(lt[:, hs, :], bank(f"kk{ch}").rearrange("p (h t) -> p h t", h=HG), dec[:, hs, :], ALU.mult),
                     "kk_ready", ch + 1)
                mark(v.tensor_tensor(lt[:, hs, :], lt[:, hs, :], brep[:, hs, :], ALU.mult), "lt_ready", ch + 1)
                job_wait(dve, f"qk2_{ch}")
                v.tensor_tensor(qkd[:, hs, :], bank(f"qk2_{ch}").rearrange("p (h t) -> p h t", h=HG), dec[:, hs, :], ALU.mult
                                ).then_inc(S["qkd_ready"], 1)
            dve.wait_ge(S["ot_ready"], 1)
            for ch in range(2):
                hs = slice(HG * ch, HG * ch + HG)
                mark(v.tensor_tensor(xinvT[:, hs, :], ident.unsqueeze(1).broadcast_to([P, HG, P]), ot[0][:, hs, :], ALU.subtract),
                     "xt_ready", ch + 1)
            for ch in range(2):
                job_wait(dve, f"x0_{ch}")
                v.tensor_copy(xinv[:, HG * ch:HG * ch + HG, :].rearrange("p h t -> p (h t)"), bank(f"x0_{ch}")
                              ).then_inc(S["x_ready"], 1)
            def heads(buf):
                return buf.rearrange("p (h t) -> p h t", h=HG)

            def wide(lo):
                return gk[:, lo:lo + HG].unsqueeze(2).broadcast_to([P, HG, P])

            dve.wait_ge(S["vtm_ready"], 2)
            dve.wait_ge(S["gam"], 1)
            dve.wait_ge(S["tail"], 1)
            link(v.tensor_tensor(gk[:, 80:84], gk[:, 12:16], gk[:, 68:72], ALU.mult))
            v.tensor_tensor(heads(vtm[:, 0, :]), heads(vtm[:, 0, :]), wide(8), ALU.mult).then_inc(S["rhs_ready"], 1)
            v.tensor_tensor(heads(vtm[:, 1, :]), heads(vtm[:, 1, :]), wide(12), ALU.mult).then_inc(S["rhs_ready"], 1)
            v.tensor_tensor(heads(kbg[:]), heads(ktm[:, 1, :]), wide(80), ALU.mult).then_inc(S["rhs_ready"], 1)
            v.tensor_tensor(heads(ktail[:]), heads(ktm[:, 0, :]), wide(72), ALU.mult).then_inc(S["rhs_ready"], 1)
            for lv in range(1, LEVELS):
                for ch in range(2):
                    hs = slice(HG * ch, HG * ch + HG)
                    job_wait(dve, f"zz{lv}.{ch}" if lv < LEVELS - 1 else f"zt{lv}.{ch}")
                    flat = xinvT[:, hs, :].rearrange("p h t -> p (h t)")
                    v.tensor_tensor(flat, flat, bank(f"zt{lv}.{ch}"), ALU.subtract).then_inc(S["xt_ready"], 1)
                    if lv < LEVELS - 1:
                        flat = xinv[:, hs, :].rearrange("p h t -> p (h t)")
                        v.tensor_tensor(flat, flat, bank(f"zz{lv}.{ch}"), ALU.subtract).then_inc(S["x_ready"], 1)
            job_wait(dve, "ws")
            v.tensor_tensor(ub[:, 1, :], ub[:, 1, :], bank("ws"), ALU.subtract).then_inc(S["u_ready"], 1)
            job_wait(dve, "oi0")
            v.tensor_copy(og[:, 0, :], bank("oi0")).then_inc(S["gdn_out"], 1)
            job_wait(dve, "ox")
            mark(v.tensor_tensor(heads(og[:, 1, :]), heads(bank("ox")), wide(68), ALU.mult), "gdn_out", 2)
            job_wait(dve, "oi1")
            mark(v.tensor_tensor(og[:, 1, :], og[:, 1, :], bank("oi1"), ALU.add), "gdn_out", 3)
            ccol = gk[:, 96:160]
            for tok in range(2):
                job_wait(dve, f"cs{tok}")
                s3 = cs_sb[:, tok, :].rearrange("p (h n) -> p h n", h=H2)
                mark(v.tensor_tensor(cs_sb[:, tok, :], bank(f"cs{tok}")[:, 0:T], c(f"cmp{tok}"), ALU.add), "cmp_biased", tok + 1)
                mx = ccol[:, 24 * tok:24 * tok + 8]
                link(v.tensor_reduce(mx, s3, AX.X, ALU.max))
                v.tensor_tensor(s3, s3, mx.unsqueeze(2).broadcast_to([P, H2, 32]), ALU.subtract).then_inc(S["cmp_arg"], 1)
            for tok in range(2):
                s3 = cs_sb[:, tok, :].rearrange("p (h n) -> p h n", h=H2)
                sums, cc = ccol[:, 24 * tok + 8:24 * tok + 16], ccol[:, 24 * tok + 16:24 * tok + 24]
                dve.wait_ge(S["cmp_probs"], tok + 1)
                link(v.tensor_reduce(sums, s3, AX.X, ALU.add))
                link(v.reciprocal(cc, sums))
                link(v.tensor_tensor(cc, cc, sm[:, tok, T:T + 24].rearrange("p (h b) -> p h b", b=3)[:, :, 0], ALU.mult))
                if tok == 0:
                    link(v.tensor_scalar(cc, cc, c("rowvalid"), None, ALU.mult))
            for tok in range(2):
                job_wait(dve, f"co{tok}")
                cc = ccol[:, 24 * tok + 16:24 * tok + 24]
                mark(v.tensor_tensor(o2[:, tok, :].rearrange("p (h d) -> p h d", h=H2), bank(f"co{tok}").rearrange("p (h d) -> p h d", h=H2),
                                     cc.unsqueeze(2).broadcast_to([P, H2, 64]), ALU.mult), "cmp_out", tok + 1)
            ogf = res[:, 0, :]
            og8 = ogf.rearrange("p (m d) -> p m d", d=P)
            ybf = yb[:].rearrange("p h t -> p (h t)")
            link(v.tensor_tensor(ybf, ogf, ogf, ALU.mult))
            v.tensor_reduce(stat[:, 20:28], yb[:], AX.X, ALU.add).then_inc(S["gdn_sum"], 1)
            for i in range(N_INST2 + 2):
                attention(i, N_INST1, N_INST2)
            dve.wait_ge(S["gdn_std"], 1)
            dve.wait_ge(S["z_ready"], 2)
            link(v.reciprocal(stat[:, 44:52], stat[:, 32:40]))
            link(v.tensor_tensor(og8, og8, stat[:, 44:52].unsqueeze(2).broadcast_to([P, 8, P]), ALU.mult))
            link(v.tensor_tensor(og8, og8, sr("gdn_norm", P).unsqueeze(1).broadcast_to([P, 8, P]), ALU.mult))
            v.tensor_tensor(ogf, ogf, zs[:].rearrange("p a n -> p (a n)"), ALU.mult).then_inc(S["gdn_normed"], 1)
            dve.wait_ge(S["gmix_ready"], 1)
            for n in range(8):
                job_wait(dve, f"mix{n}")
                mark(v.tensor_tensor(tmp[:, n % 2, :].rearrange("p (a t) -> p a t", a=2), gates2[:, :, n, :],
                                     bank(f"mix{n}").rearrange("p (a t) -> p a t", a=2), ALU.mult), "mix_gated", n + 1)
                mark(v.tensor_tensor(mT[:, n, :], tmp[:, n % 2, 0:T], tmp[:, n % 2, T:2 * T], ALU.add), "mixed", n + 1)
            add_normed(3, 1, 0, lambda tok, half: acc[:, 2 * tok + half, :], 5)
            signal("norm_sum")
            rms_scaled(0, 6, 6)
            over_ffn(conv_hidden)
            steps[0] += NF
            dve.wait_ge(S["acc_done"], 5)
            add_normed(4, 0, 1, lambda tok, half: acc[:, 2 * tok + half, :], 7)
            for tok in range(2):
                v.tensor_copy(res[:, tok, :], xs[:, 1, tok, :]).then_inc(S["xn_ready"], 1)
            dve.wait_ge(S["ple_ready"], 4)
            for tok in range(2):
                dve.wait_ge(S["acc_read"], 20 + tok + 1)
                v.tensor_tensor(res[:, tok, :], res[:, tok, :], ple_flat[:, D * tok:D * tok + D], ALU.mult).then_inc(S["ple_gated"], 1)
            dve.wait_ge(S["ple_gated"], 2)
            add_normed(5, 1, 0, lambda tok, half: res[:, tok, 512 * half:512 * half + 512], 8, final=True)


def fm_blocks(w):
    k, n = w.shape
    return w.reshape(k // P, P, n // P, P).transpose(2, 0, 1, 3).reshape(-1, P, P)


def tm_blocks(w):
    k, n = w.shape
    return w.reshape(k // P, P, n // P, P).transpose(0, 2, 1, 3).reshape(-1, P, P)


def ffn_blocks(gate, up, down):
    g, u, d = (a.reshape(NF, 8, P, P) for a in (fm_blocks(gate), fm_blocks(up), tm_blocks(down)))
    parts = [g[0], u[0]]
    for f in range(1, NF):
        parts += [g[f], u[f], d[f - 1]]
    return parts + [d[NF - 1]]


def padded(w, n):
    out = np.zeros((w.shape[0], n), w.dtype)
    out[:, :w.shape[1]] = w
    return out


def pack_stream(a):
    w_in, w2 = a["w_in"][0], a["w_in_2"][0]
    parts = ffn_blocks(a["ffn_w_gate"][0, 0], a["ffn_w_up"][0, 0], a["ffn_w_down"][0, 0])
    q = W1
    for m in range(3):
        parts += [fm_blocks(w_in[:, 3 * q * m:3 * q * m + q]), fm_blocks(w_in[:, 3 * q * m + q:3 * q * m + 2 * q])]
    vcat = np.concatenate([w_in[:, 3 * q * m + 2 * q:3 * q * m + 3 * q] for m in range(3)], 1)
    parts += [tm_blocks(vcat[:, 0:512]), tm_blocks(vcat[:, 512:1024]), tm_blocks(vcat[:, 1024:1152])]
    parts.append(fm_blocks(w_in[:, 9 * q:]))
    br = [fm_blocks(a[n][0]).reshape(8, 3, P, P) for n in ("w_br_moba", "w_br_diff", "w_br_sb")]
    parts.append(np.stack(br, 1).reshape(-1, P, P))
    parts.append(tm_blocks(a["w_out"][0]))
    parts += ffn_blocks(a["ffn_w_gate"][0, 1], a["ffn_w_up"][0, 1], a["ffn_w_down"][0, 1])
    at = {}
    off = 0
    for name, n in (("qkv", 1536), ("z", 512), ("b", 4), ("a", 4), ("q", 512), ("kc", 128), ("vc", 128), ("ks", 128),
                    ("vs", 128), ("kw", 128), ("vw", 128), ("gn", 24), ("gm", 2048)):
        at[name] = w2[:, off:off + n]
        off += n
    parts.append(fm_blocks(at["qkv"]))
    small = np.concatenate([at["vs"], at["vw"], at["gn"], at["b"], at["a"]], 1)
    parts.append(tm_blocks(padded(small, 512)))
    parts.append(tm_blocks(at["z"]))
    parts += [fm_blocks(at[n]) for n in ("kc", "vc", "q", "ks", "kw")]
    parts += [fm_blocks(a["cmp_w1_k_2"][0]), fm_blocks(a["cmp_w1_v_2"][0])]
    parts += [fm_blocks(padded(a["cmp_w2_k_2"][0], P)), fm_blocks(padded(a["cmp_w2_v_2"][0], P)), np.zeros((4, P, P), np.float32)]
    parts.append(fm_blocks(at["gm"]))
    ab = [fm_blocks(a[n][0]).reshape(8, 4, P, P) for n in ("w_a2d_2", "w_b2d_2")]
    parts.append(np.stack(ab, 1).reshape(-1, P, P))
    parts.append(tm_blocks(a["w_o_2"][0]))
    parts.append(tm_blocks(a["w_ple_2"][0]))
    up = a["w_up_2"][0]
    parts += ffn_blocks(up[:, :FF], up[:, FF:], a["w_down_2"][0])
    parts.append(tm_blocks(a["w_ple_gate_2"][0]))
    blocks = np.concatenate(parts, 0)
    assert blocks.shape[0] == N_BLOCKS, (blocks.shape, N_BLOCKS)
    if N_CHUNKS * CB > N_BLOCKS:
        blocks = np.concatenate([blocks, np.zeros((N_CHUNKS * CB - N_BLOCKS, P, P), blocks.dtype)], 0)
    return np.ascontiguousarray(blocks.reshape(N_CHUNKS, CB, P, P).transpose(0, 2, 1, 3).reshape(N_CHUNKS, P, CB * P))


def as_cols(vec):
    return vec.reshape(-1, P).T


def kernel(**inputs):
    import concourse.bacc as bacc
    from concourse.bass_utils import run_bass_kernel_spmd

    a = {k: np.asarray(v) for k, v in inputs.items()}
    const, const_at = constants()
    lg_, lb_ = a["ln_g"][0], a["ln_b"][0]

    def pos_cols(pos):
        return pos.reshape(16, 2 * 64).T

    cols = np.concatenate([
        as_cols(lg_[0]), as_cols(lb_[0]), as_cols(lg_[1]), as_cols(lb_[1]), as_cols(a["norm_mix_pre_2"][0]),
        as_cols(a["norm_ffn_pre_2"][0]), as_cols(a["b_gate"][0].reshape(-1)),
        a["conv_qkv_2"][0].reshape(4, 12, P).transpose(2, 1, 0).reshape(P, -1),
        a["conv_ffn_2"][0].reshape(3, 2 * NF, P).transpose(2, 1, 0).reshape(P, -1),
        as_cols(a["conv_ffn_b_2"][0]), pos_cols(a["cmp_pos_k_2"][0]), pos_cols(a["cmp_pos_v_2"][0])], 1)
    big = np.zeros((len(BIG_ROWS), 2 * D), np.float32)
    named = {f"ln_g{i}": lg_[i] for i in range(3)} | {f"ln_b{i}": lb_[i] for i in range(3)} | {
        "mix_post": a["norm_mix_post_2"][0], "ffn_post": a["norm_ffn_post_2"][0], "ple_post": a["norm_ple_post_2"][0]}
    for i, names in enumerate(BIG_ROWS):
        for j, n in enumerate(names):
            big[i, D * j:D * j + D] = named[n]
    small = np.concatenate([a["gdn_norm_2"][0], a["diff_subln_g"][0], a["diff_lambda"][0].reshape(-1), a["a_log_2"][0],
                            a["dt_bias_2"][0]])[None, :]
    x = a["x"][0]
    arrays = {
        "x_tm": x.reshape(2, P, D).transpose(1, 0, 2), "x_fm": x.T.reshape(KD, P, T).transpose(1, 0, 2),
        "p_fm": a["p_2"][0, 0].T.reshape(2, P, T).transpose(1, 0, 2), "stream": pack_stream(a), "consts": const,
        "cols": cols, "big_rows": big, "small_rows": small,
    }
    arrays = {k: np.ascontiguousarray(v) for k, v in arrays.items()}
    nc = bacc.Bacc("TRN2", target_bir_lowering=False, num_devices=1)
    args = [nc.dram_tensor(f"in_{k}", v.shape, mybir.dt.from_np(v.dtype), kind="ExternalInput").ap() for k, v in arrays.items()]
    out = nc.dram_tensor("out_0", (1, T, D), F32, kind="ExternalOutput").ap()
    build(nc, *args, out, const_at)
    r = run_bass_kernel_spmd(nc, [{f"in_{k}": v for k, v in arrays.items()}], core_ids=[0])
    return r.results[0]["out_0"]
```

```python
from contextlib import ExitStack

import numpy as np

import concourse.bass as bass
from concourse import mybir

ALU = mybir.AluOpType
ACT = mybir.ActivationFunctionType
AX = mybir.AxisListType
F32 = mybir.dt.float32
F32R = mybir.dt.float32r

P = 128
T = 256
D = 1024
KD = D // P
FF = 2816
NF = FF // P
RING = 4
CB = 8
NBANK = 4
GROUP = 4
ROUND = GROUP * 24 // CB

H1 = 6
W1 = H1 * 64
SLOPES1 = [float(np.float32(2.0 ** (-8.0 * (i + 1) / 12))) for i in range(12)]
H2 = 8
SLOPES2 = [2.0 ** -(i + 1) for i in range(H2)]
NC = 15
HG = 4
LEVELS = 7
ALPHA = float(2.0 ** 0.25)
NEG = -1e30
N_INST1 = 3 * H1
N_INST2 = 2 * H2


def constants():
    i = np.arange(P)
    row, col = i[:, None], i[None, :]
    parts = {}
    parts["ident"] = (row == col).astype(np.float32)
    parts["ones"] = np.ones((P, P), np.float32)
    parts["upper"] = (row <= col).astype(np.float32)
    parts["lower"] = (row >= col).astype(np.float32)
    d0 = row - col
    d1 = (row + P) - np.arange(T)[None, :]
    parts["negdist"] = np.concatenate([np.where(d >= 0, -d, NEG) for d in (d0, d1)], 1)
    parts["sbmask"] = np.concatenate([np.where(row < np.arange(T)[None, :], 0, NEG), np.where(row < col, 0, NEG)], 1)
    parts["decmask"] = np.where(row <= col, 0, NEG)
    for lv in range(LEVELS):
        m = (row < col) & (row >> (lv + 1) == col >> (lv + 1)) & (row >> lv != col >> lv)
        parts[f"level{lv}"] = m
    n = np.arange(32)[None, :]
    for t in range(2):
        dist = (row + P * t) - (16 * n + 31)
        ok = (dist >= 0) & (n < NC)
        parts[f"cmp{t}"] = np.concatenate([np.where(ok, -dist * s, NEG) for s in SLOPES2], 1)
    parts["rowvalid"] = (i >= 31)[:, None]
    for name, v in (("eps_ln", 1e-5), ("eps_ln4", 4e-5), ("eps_rms", 1e-6), ("one", 1.0), ("zero", 0.0)):
        parts[name] = np.full((P, 1), v)
    at, off = {}, 0
    for k, v in parts.items():
        at[k] = (off, v.shape[1])
        off += v.shape[1]
    return np.concatenate([np.asarray(v, np.float32) for v in parts.values()], 1), at


COLS = (("ln_g0", KD), ("ln_b0", KD), ("ln_g1", KD), ("ln_b1", KD), ("mix_pre", KD), ("ffn_pre", KD), ("b_gate", 24),
        ("conv_qkv", 48), ("conv_ffn", 3 * 2 * NF), ("conv_ffn_b", 2 * NF), ("pos_k", 16), ("pos_v", 16))
BIG_ROWS = (("ln_g0", "ln_b0"), ("ln_g1", "ln_b1"), ("ln_g2", "ln_b2"), ("mix_post",), ("ffn_post",), ("ple_post",))
SMALL_ROWS = (("gdn_norm", P), ("subln", 64), ("lambda", P), ("a_log", HG), ("dt_bias", HG))


def offsets(items):
    at, off = {}, 0
    for k, n in items:
        at[k] = off
        off += n
    return at, off


COL_AT, N_COLS = offsets(COLS)
SROW_AT, N_SROW = offsets(SMALL_ROWS)


def stream_parts():
    ffn = 3 * 8 * NF
    return (("ffn0", ffn), ("qk", 18 * 8), ("v", 96), ("gate", 24 * 8), ("branch", 72), ("w_out", 64), ("ffn1", ffn),
            ("conv", 12 * 8), ("small", 32), ("z", 32), ("kc", 8), ("vc", 8), ("qb", 32), ("ks", 8), ("kw", 8),
            ("w1k", 32), ("w1v", 32), ("w2", 8), ("gmix", 128), ("ab", 64), ("w_o", 64), ("ple", 16), ("ffn2", ffn),
            ("ple_gate", 64))


PART_AT, N_BLOCKS = offsets(stream_parts())
N_CHUNKS = -(-N_BLOCKS // CB)


def job_table():
    jobs = []
    pos = [0]

    def job(name, *frees, blocks=0):
        pos[0] += blocks
        jobs.append((name, frees, pos[0]))

    def ffn(n):
        for f in range(NF):
            pos[0] = PART_AT[f"ffn{n}"] + ffn_end(f)
            job(f"ffn{n}.{f}", ("hidden", NF * n + f + 1) if n < 2 else ("taps", f + 1))
        pos[0] = PART_AT[f"ffn{n}"] + 24 * NF

    def turn(i):
        for g in range(4):
            job(f"turn{i}.{g}", ("xT_ready", 8 * i + 2 * g + 2))

    ffn(0)
    turn(0)
    for t in range(18):
        job(f"qk{t}", ("qk_ready", t + 1), blocks=8)
    for c in range(3):
        for tok in range(2):
            job(f"v{c}.{tok}", ("v_ready", 2 * c + tok + 1), blocks=32 * (1 - tok))
    for i in range(N_INST1 + 2):
        attention_jobs(job, i, 0, N_INST1)
        if i < 16:
            job(f"gate{i}", ("gate_raw", i + 1), blocks=8)
    for first in range(0, H1 + 4, 2):
        for i in sb_heads(first):
            job(f"sbz{i}", ("sb_neg", i + 1))
        for i in sb_gates(first, 0):
            job(f"gate{i}", ("gate_raw", i + 1), blocks=8)
        for h in sb_heads(first - 2):
            job(f"sbr{h}", ("sb_exponent", h + 1))
        for i in sb_gates(first, 1):
            job(f"gate{i}", ("gate_raw", i + 1), blocks=8)
        for h in sb_heads(first - 4):
            job(f"sbo{h}", ("sb_out", h + 1))
    for k in range(5):
        job(f"oT{k}", ("oT_ready", k + 1))
    for n in range(8):
        job(f"branch{n}.a", ("branch_a", n + 1), blocks=6)
        job(f"branch{n}.b", ("branch_b", n + 1), blocks=3)
    pos[0] = PART_AT["ffn1"]
    turn(1)
    ffn(1)
    turn(2)
    for t in range(12):
        job(f"conv{t}", ("qkv_taps", t + 1), blocks=8)
    for tok in range(2):
        job(f"small{tok}", ("small_ready", tok + 1), blocks=32 * (1 - tok))
    for tok in range(2):
        job(f"z{tok}", ("z_ready", tok + 1), blocks=32 * (1 - tok))
    job("kc", ("kc_shifted", 1), blocks=8)
    job("vc", ("vc_shifted", 1), blocks=8)
    for t in range(4):
        job(f"qb{t}", ("qb_ready", t + 1), blocks=8)
    job("ks", ("kdup_ready", 1), blocks=8)
    job("kw", ("kdup_ready", 2), blocks=8)
    for t in range(4):
        job(f"l2_{t}", ("l2_log", t + 1))
    job("hk", ("cmp_hidden", 1), blocks=32)
    job("hv", ("cmp_hidden", 2), blocks=32)
    for kv, name in enumerate(("hkT", "hvT")):
        job(name, ("cmp_turned", kv + 1))
    job("kc2", ("kcomp_ready", 1), blocks=2)
    job("vc2", ("vcomp_ready", 1), blocks=2)
    pos[0] = PART_AT["gmix"]
    job("gcum", ("gcum_ready", 1))
    for c in range(2):
        job(f"grow{c}", ("decay_arg", c + 1), ("tail_arg", 1))
    for c in range(2):
        job(f"brow{c}", ("beta_row", c + 1))
    for c in range(2):
        job(f"ktm{c}", ("ktm_ready", c + 1))
        job(f"vtm{c}", ("vtm_ready", c + 1))
        job(f"kk{c}", ("kk_ready", c + 1))
        job(f"qk2_{c}", ("qkd_ready", c + 1))
    for c in range(2):
        job(f"x0_{c}", ("x_ready", c + 1))
    for lv in range(1, LEVELS):
        for c in range(2):
            job(f"y{lv}.{c}", ("y_ready", 2 * (lv - 1) + c + 1))
        for c in range(2):
            job(f"zt{lv}.{c}", ("xt_ready", 2 * lv + c + 1))
            if lv < LEVELS - 1:
                job(f"zz{lv}.{c}", ("x_ready", 2 * lv + c + 1))
        for k in range(2):
            job(f"gmix{2 * (lv - 1) + k}", ("gmix_raw", 2 * (lv - 1) + k + 1), blocks=8)
    job("u0", ("u_ready", 1))
    job("u1", ("u_ready", 2))
    job("wT", ("wT_ready", 1))
    job("state", ("state_ready", 1))
    job("ws", ("u_ready", 3))
    job("oi0", ("gdn_out", 1))
    job("oi1", ("gdn_out", 3))
    job("ox", ("gdn_out", 2))
    for tok in range(2):
        job(f"cs{tok}", ("cmp_biased", tok + 1))
    for tok in range(2):
        job(f"ct{tok}", ("cmp_pt", tok + 1))
    for tok in range(2):
        job(f"co{tok}", ("cmp_out", tok + 1))
    for i in range(N_INST2 + 2):
        attention_jobs(job, i, N_INST1, N_INST2)
        if i < 4:
            job(f"gmix{12 + i}", ("gmix_raw", 13 + i), blocks=8)
    for k in range(4):
        job(f"yT{k}", ("yT_ready", k + 1))
    for n in range(8):
        job(f"mix{n}", ("mix_gated", n + 1), blocks=8)
    pos[0] = PART_AT["ple"] + 16
    for k in range(4):
        job(f"ple{k}", ("ple_ready", k + 1))
    turn(3)
    ffn(2)
    turn(4)
    return jobs


def ffn_end(f):
    return 24 * f + (16 if f == 0 else 8)


def sb_heads(first):
    return range(first, first + 2) if 0 <= first < H1 else ()


def sb_gates(first, half):
    return (16 + first + half,) if first < 8 else ()


def attention_jobs(job, i, base, n):
    if i < n:
        job(f"s{base + i}", ("biased", base + i + 1))
    if 1 <= i <= n:
        job(f"t{base + i - 1}", ("pt_ready", base + i))
    if i >= 2:
        job(f"o{base + i - 2}", ("attn_out", base + i - 1))


SEMS = """p_in p_split x_split hi_ready lo_ready xT_high h_made h_high oT_high yT_high ot_used x_high consts_in cols_in rows_in x_in xT_in big_rows_in0 big_rows_in1 out_stored used job_done dve_step act_step
hidden act_done taps tap_in down_done acc_done acc_read xT_ready xn_ready norm_sum var_ready std_ready sq_ready row_free
qk_ready v_ready biased row_max probs pt_ready coef attn_out gate_raw gates_ready
sb_neg sb_exp sb_log sb_softplus sb_exponent sb_weight sb_out oT_ready branch_a branch_b merged lam_arg lam_exp subln_sum
subln_std o_normed qkv_tap_in qkv_taps qkv_ready qkv_sq l2_log l2_scale l2_ready small_ready z_ready kc_shifted vc_shifted
kv_pos qb_ready kdup_ready cmp_hidden cmp_turned kcomp_ready vcomp_ready sg_arg sg_exp sg_ready dt_arg dt_log g_ready g_rows
gcum_ready gcum_neg decay_arg decay tail_arg tail gam beta_row ktm_ready vtm_ready kk_ready lt_ready qkd_ready xt_ready
x_ready ot_ready y_ready gmix_raw gmix_ready rhs_ready u_ready wT_ready state_ready gdn_out gdn_sum gdn_std gdn_normed
cmp_biased cmp_arg cmp_probs cmp_pt cmp_out yT_ready mix_gated mixed ple_ready ple_gated final zeroed""".split()


def build(nc, x_tm, x_fm, p_fm, stream, consts, cols, big_rows, small_rows, out, const_at):
    jobs = job_table()
    index = {job[0]: j for j, job in enumerate(jobs)}
    assert len(index) == len(jobs)

    with ExitStack() as ctx:
        in_ffn, block_one, block_two, early = ExitStack(), ExitStack(), ExitStack(), ExitStack()

        def sb(name, shape, where=ctx, dtype=F32):
            return where.enter_context(nc.sbuf_tensor(name, [P] + list(shape), dtype))

        def pair(name, shape, where=ctx):
            return sb(name + "_high", shape, where, F32R), sb(name + "_low", shape, where, F32R)

        S = {n: ctx.enter_context(nc.semaphore(n)) for n in SEMS}
        arrived = [ctx.enter_context(nc.semaphore(f"arrived{i}")) for i in range(RING)]
        acc = ctx.enter_context(nc.psum_tensor("acc", [P, 4, 512], F32))
        banks = ctx.enter_context(nc.psum_tensor("banks", [P, NBANK, 512], F32))

        ring = sb("ring", [RING, CB * P])
        whi, wlo = pair("weights", [RING, CB * P])
        cst = sb("cst", [consts.shape[1]])
        col = sb("col", [N_COLS])
        rows = sb("rows", [2, 2 * D])
        srow = sb("srow", [N_SROW])
        xs = sb("xs", [2, 2, D])
        res = sb("res", [2, D])
        xT = pair("xT", [KD, T])
        stat = sb("stat", [64])
        nmx = sb("nmx", [2, 2])
        den = sb("den", [2, 2])
        coef = sb("coef", [2, 2])
        tmp = sb("tmp", [2, 2 * T])
        hT = pair("hT", [GROUP, T], in_ffn)
        hf = sb("hf", [2, T], in_ffn)
        act_buf = sb("act_buf", [2, 2 * T], in_ffn)
        gel = sb("gel", [2, T], in_ffn)
        in_ffn.close()

        def c(name, lo=0, n=None):
            off, w = const_at[name]
            return cst[:, off + lo:off + (lo + n if n else w)]

        def pcol(name, i):
            return col[:, COL_AT[name] + i:COL_AT[name] + i + 1]

        def sr(name, n, lo=0):
            return srow[:, SROW_AT[name] + lo:SROW_AT[name] + lo + n]

        ident, ones = c("ident"), c("ones")

        qkT = sb("qkT", [18, T], early)
        early.close()
        mT1 = pair("mT1", [KD, T], block_one)
        sb("pad1", [18 * T - 2 * KD * T], block_one)
        v1 = sb("v1", [2, 3 * W1], early)
        wT_sb = sb("wT_sb", [4, 384], early)
        sS1 = sb("sS1", [2, 384], early)
        prob1 = sb("prob1", [2, 384], early)
        early.close()
        oT = pair("oT", [9, T], block_one)
        sb("pad2", [2 * 3 * W1 + 8 * 384 - 18 * T], block_one)
        pT1 = sb("pT1", [2, 384], block_one)
        o1 = sb("o1", [2, 3 * W1], block_one)
        gates1 = sb("gates1", [3, 8, T], block_one)
        x_in_fm = gates1[:, 0]
        zm = res[:].rearrange("p a n -> p (a n)")[:, 0:1536].rearrange("p (a n) -> p a n", a=4)
        lg = xs[:, 0].rearrange("p a n -> p (a n)")[:, 0:1536].rearrange("p (a n) -> p a n", a=4)
        sq1 = tmp[:].rearrange("p a n -> p (a n)")[:, 0:2 * W1].rearrange("p (a n) -> p a n", a=2)
        block_one.close()
        cv = sb("cv", [12, T], early)
        zs = sb("zs", [2, 512], early)
        early.close()
        mT2 = pair("mT2", [KD, T], block_two)
        grow = sb("grow", [8, P], early)
        brep = sb("brep", [8, P], early)
        dec = sb("dec", [8, P], early)
        kv_tm = sb("kv_tm", [4, 512], early)
        early.close()
        yT = pair("yT", [8, T], block_two)
        sb("pad3", [3 * 8 * P + 4 * 512 - 16 * T], block_two)
        sS2 = sb("sS2", [2, 384], early)
        prob2 = sb("prob2", [2, 384], early)
        early.close()
        pE = pair("pE", [2, T], block_two)
        sb("pad4", [4 * 384 - 4 * T], block_two)
        pT2 = sb("pT2", [2, 384], block_two)
        sm = sb("sm", [2, 288], block_two)
        xc = sb("xc", [2, 2, T], block_two)
        rc = sb("rc", [2, 16, 2, NC], block_two)
        hh = sb("hh", [2, 2, 2 * NC], block_two)
        bdk = sb("bdk", [2, 64], block_two)
        bdv = sb("bdv", [2, T], block_two)
        gk = sb("gk", [160], block_two)
        ktail = sb("ktail", [512], block_two)
        ot0 = sb("ot0", [8, P], block_two)
        rcs = pair("rcs", [2, 16, 2 * NC], early)
        hidden_tm = sb("hidden_tm", [2, T], early)[0:2 * NC]
        early.close()
        gates2 = sb("gates2", [2, 8, T], block_two)
        block_two.close()
        ktm, vtm = kv_tm[:, 0:2], kv_tm[:, 2:4]
        csq = kv_tm[:].rearrange("p a (b n) -> p (a b) n", n=T)
        qbT = rows[:, 0, D:2 * D].rearrange("p (a n) -> p a n", a=4)
        kdup = rows[:, 1, D:2 * D].rearrange("p (a g n) -> p a g n", a=2, g=2)
        kbg = rc[:].rearrange("p a k g n -> p (a k g n)")[:, 0:512]
        p_raw = pT2[:].rearrange("p a n -> p (a n)")[:, 0:2 * T].rearrange("p (a n) -> p a n", a=2)
        cs_sb, cpT = xc[:, 0], xc[:, 1]
        og = res[:, 0, :].rearrange("p (a n) -> p a n", a=2)
        o2 = res[:, 1, :].rearrange("p (a n) -> p a n", a=2)
        lt = xs[:, 0, 0, :].rearrange("p (a n) -> p a n", a=8)
        qkd = xs[:, 0, 1, :].rearrange("p (a n) -> p a n", a=8)
        xinv, xinvT, yb = grow, dec, brep
        ot = (ot0[:], tmp[:].rearrange("p a (b n) -> p (a b) n", n=P))
        ub = ktm
        state, wT2 = vtm[:, 0, :], vtm[:, 1, :]
        ple_flat = gates2[:].rearrange("p a b t -> p (a b t)")
        attn_bufs = {0: (sS1, prob1, pT1), N_INST1: (sS2, prob2, pT2)}

        block = ctx.enter_context(nc.Block())

        def bank(name):
            return banks[:, index[name] % NBANK, :]

        def job_wait(eng, name, more=0):
            eng.wait_ge(S["job_done"], index[name] + 1 + more)

        def need(eng, sem, value):
            if not isinstance(value, int) or value > 0:
                eng.wait_ge(S[sem], value)

        def instances(base):
            made = []
            if base == 0:
                for h in range(H1):
                    made.append((0 + h // 2, 3 + h // 2, 64 * (h % 2), 64, 64 * h, SLOPES1[2 * h], 64 * h, "first"))
                for h in range(H1):
                    for m in range(2):
                        made.append((6 + h // 2, 9 + h // 2, 64 * (h % 2) + 32 * m, 32, W1 + 64 * h, SLOPES1[2 * h + 1],
                                     W1 + 64 * h, "second" if m else "first"))
            else:
                for h in range(H2):
                    for kind in range(2):
                        made.append((h // 2, (kind, h // 4), 64 * (h % 2), 64, P * kind + 64 * (h // 4), SLOPES2[h],
                                     64 * h, (h, kind)))
            return made

        inst = {0: instances(0), N_INST1: instances(N_INST1)}

        @block.sync
        def _(sp_eng):
            def load(slot, chunk):
                src = stream[chunk] if isinstance(chunk, int) else stream[bass.ds(chunk, 1)].rearrange("a p n -> (a p) n")
                sp_eng.dma_start(ring[:, slot, :], src).then_inc(arrived[slot], 16)

            for s in range(RING):
                load(s, s)
            full = N_CHUNKS // RING
            with nc.sync.Fori(1, full) as g:
                for s in range(RING):
                    sp_eng.wait_ge(S["lo_ready"], RING * g + (s - RING + 1))
                    load(s, RING * g + s)
            for ch in range(full * RING, N_CHUNKS):
                sp_eng.wait_ge(S["lo_ready"], ch - RING + 1)
                load(ch % RING, ch)
            sp_eng.wait_ge(S["final"], 2)
            for tok in range(2):
                sp_eng.dma_start(out[0, P * tok:P * tok + P, :], xs[:, 0, tok, :]).then_inc(S["out_stored"], 16)
            sp_eng.wait_ge(S["out_stored"], 32)

        @block.gpsimd
        def _(pool):
            def low(slot, value):
                pool.wait_ge(S["hi_ready"], value)
                nc.gpsimd.tensor_tensor(wlo[:, slot, :], ring[:, slot, :], whi[:, slot, :].bitcast(F32), ALU.subtract
                                        ).then_inc(S["lo_ready"], 1)

            with nc.gpsimd.Fori(0, N_CHUNKS // RING) as g:
                for s in range(RING):
                    low(s, RING * g + (s + 1))
            for ch in range(N_CHUNKS // RING * RING, N_CHUNKS):
                low(ch % RING, ch + 1)

        @block.tensor
        def _(pe):
            at = [0]
            now = [0]
            release = [False]

            def weights(n):
                b = at[0]
                at[0] += n
                if b % CB == 0:
                    ch = b // CB
                    pe.wait_ge(S["lo_ready"], ch + 1)
                    release[0] = ch > 0
                return parts(b, n)

            def parts(b, n):
                slot, pos = (b // CB) % RING, b % CB
                return whi[:, slot, pos * P:(pos + n) * P], wlo[:, slot, pos * P:(pos + n) * P]

            def mm(o, lhsT, rhs, start, stop, **kw):
                ins = nc.tensor.matmul(o, lhsT, rhs, start=start, stop=stop, **kw)
                if release[0] and not stop:
                    ins.then_inc(S["used"], 1)
                    release[0] = False
                return ins

            def mm3(o, lhsT, rhs, start, stop, **kw):
                mm(o, lhsT[0], rhs[0], start, False, **kw)
                mm(o, lhsT[0], rhs[1], False, False, **kw)
                return mm(o, lhsT[1], rhs[0], False, stop, **kw)

            def cut(both, *at_):
                return tuple(x[(slice(None),) + at_] for x in both)

            def take(name):
                assert jobs[now[0]][0] == name, (jobs[now[0]][0], name)
                j = now[0]
                now[0] += 1
                if j >= NBANK:
                    for sem, value in jobs[j - NBANK][1]:
                        pe.wait_ge(S[sem], value)
                return bank(name)

            def done(ins):
                ins.then_inc(S["job_done"], 1)

            def project_fm(name, src, half=None):
                o = take(name)
                for k in range(KD):
                    last = mm3(o[:, 0:T], weights(1), cut(src, k), k == 0, k == KD - 1)
                done(last)

            def project_tm(names, width, stored, src):
                o = [take(n) for n in names]
                for k in range(KD):
                    w = weights(stored)
                    for tok in range(2):
                        last = mm3(o[tok][:, 0:width], cut(src, k, slice(P * tok, P * tok + P)), cut(w, slice(0, width)),
                                   k == 0, k == KD - 1)
                        if k == KD - 1:
                            done(last)

            def into_acc(src, k, first, last, count=True):
                for half in range(2):
                    w = weights(4)
                    for tok in range(2):
                        ins = mm3(acc[:, 2 * tok + half, :], cut(src, k, slice(P * tok, P * tok + P)), w, first, last)
                return ins

            def turn(i):
                for g in range(4):
                    o = take(f"turn{i}.{g}")
                    for kk in range(2):
                        for tok in range(2):
                            if g == 0 and kk == 0:
                                pe.wait_ge(S["xn_ready"], 2 * i + tok + 1)
                            k = 2 * g + kk
                            last = nc.tensor.transpose(o[:, (2 * kk + tok) * P:(2 * kk + tok + 1) * P],
                                                       res[:, tok, k * P:(k + 1) * P], ident)
                    done(last)

            def ffn(n):
                b0, j0 = PART_AT[f"ffn{n}"], index[f"ffn{n}.0"]

                def gate_up(f, it=0):
                    at[0] = b0 + (0 if f == 0 else 24 * f - 8)
                    o = banks[:, (j0 + f) % NBANK, :]
                    for half in range(2):
                        for k in range(KD):
                            if half == 0 and k == 0:
                                if j0 + f < NBANK:
                                    pass
                                elif f < NBANK:
                                    for sem, value in jobs[j0 + f - NBANK][1]:
                                        pe.wait_ge(S[sem], value)
                                else:
                                    sem, value = jobs[j0 + f - NBANK][1][0]
                                    pe.wait_ge(S[sem], value + GROUP * it)
                            last = mm3(o[:, half * T:half * T + T], loop_weights(1, it), cut(xT, k), k == 0, k == KD - 1)
                    done(last)

                def loop_weights(nb, it):
                    b = at[0]
                    at[0] += nb
                    ch = b // CB
                    if b % CB == 0:
                        pe.wait_ge(S["lo_ready"], ch + 1 + ROUND * it)
                        release[0] = ch > 0
                    return parts(b, nb)

                def down(f, it=0):
                    at[0] = b0 + 24 * f + 32 if f < NF - 1 else b0 + 24 * f + 16
                    pe.wait_ge(S["hidden"], NF * n + f + 1 + GROUP * it)
                    if f == 0:
                        need(pe, "acc_read", 4 * n_acc_before)
                    for half in range(2):
                        w = loop_weights(4, it)
                        for tok in range(2):
                            first, last = isinstance(it, int) and f + GROUP * it == 0, isinstance(it, int) and f == NF - 1
                            ins = mm3(acc[:, 2 * tok + half, :], cut(hT, f % GROUP, slice(P * tok, P * tok + P)), w, first, last,
                                      skip_group_check=True)
                    if f == NF - 1:
                        ins.then_inc(S["acc_done"], 1)
                    else:
                        ins.then_inc(S["down_done"], 1)

                n_acc_before = (0, 2, 4)[n]
                gate_up(0)
                for f in range(1, 1 + GROUP):
                    gate_up(f)
                    down(f - 1)
                with nc.tensor.Fori(1, (NF - 2) // GROUP) as it:
                    for f in range(1, 1 + GROUP):
                        gate_up(f + GROUP, it - 1)
                        down(f - 1 + GROUP, it - 1)
                f = NF - 1
                gate_up(f)
                down(f - 1)
                down(f)
                now[0] = j0 + NF
                at[0] = b0 + 24 * NF

            def attention(step, base, n, kq, kk, v, src_inst):
                i = step
                _, prob, pT = attn_bufs[base]
                if i < n:
                    qi, ki, row, depth, *_ = src_inst[i]
                    o = take(f"s{base + i}")
                    q = kq(qi)[row:row + depth, :]
                    k = kk(ki)[row:row + depth, :]
                    mm(o[:, 0:P], q[:, 0:P], k[:, 0:P], True, True)
                    done(mm(o[:, P:3 * P], q[:, P:T], k[:, 0:T], True, True))
                if 1 <= i <= n:
                    j = base + i - 1
                    o = take(f"t{j}")
                    pe.wait_ge(S["probs"], 2 * (j + 1))
                    for b in range(3):
                        last = nc.tensor.transpose(o[:, b * P:(b + 1) * P], prob[:, j % 2, b * P:(b + 1) * P], ident)
                    done(last)
                if i >= 2:
                    j = base + i - 2
                    vc = src_inst[i - 2][4]
                    o = take(f"o{j}")
                    pe.wait_ge(S["pt_ready"], j + 1)
                    mm(o[:, 0:64], pT[:, j % 2, 0:P], v[:, 0, vc:vc + 64], True, True)
                    mm(o[:, 64:P], pT[:, j % 2, P:2 * P], v[:, 0, vc:vc + 64], True, False)
                    done(mm(o[:, 64:P], pT[:, j % 2, 2 * P:3 * P], v[:, 1, vc:vc + 64], False, True))

            pe.wait_ge(S["x_split"], KD)
            ffn(0)
            pe.wait_ge(S["consts_in"], 16)
            turn(0)
            pe.wait_ge(S["xT_ready"], 8)
            for t in range(18):
                project_fm(f"qk{t}", xT)
            for ch in range(3):
                project_tm([f"v{ch}.0", f"v{ch}.1"], W1, 4, xT)
            pe.wait_ge(S["qk_ready"], 18)
            pe.wait_ge(S["v_ready"], 6)
            for i in range(N_INST1 + 2):
                attention(i, 0, N_INST1, lambda t: qkT[:, t, :], lambda t: qkT[:, t, :], v1, inst[0])
                if i < 16:
                    project_fm(f"gate{i}", xT)

            def turn_o(k):
                o = take(f"oT{k}")
                for kk in range(2 if k < 4 else 1):
                    for tok in range(2):
                        f = 2 * k + kk
                        last = nc.tensor.transpose(o[:, (2 * kk + tok) * P:(2 * kk + tok + 1) * P],
                                                   o1[:, tok, f * P:(f + 1) * P], ident)
                done(last)

            for first in range(0, H1 + 4, 2):
                for i in sb_heads(first):
                    o = take(f"sbz{i}")
                    r = 64 * (i % 2)
                    q, k = qkT[r:r + 64, 12 + i // 2, :], qkT[r:r + 64, 15 + i // 2, :]
                    mm(o[:, 0:T], k[:, 0:P], q, True, True)
                    done(mm(o[:, T:T + P], k[:, P:T], q[:, P:T], True, True))
                for i in sb_gates(first, 0):
                    project_fm(f"gate{i}", xT)
                for h in sb_heads(first - 2):
                    o = take(f"sbr{h}")
                    pe.wait_ge(S["sb_softplus"], h + 1)
                    mm(o[:, 0:T], c("lower"), lg[:, h % 4, 0:T], True, False)
                    mm(o[:, P:T], ones, lg[:, h % 4, T:T + P], False, True)
                    done(mm(o[:, T:T + P], c("lower"), lg[:, h % 4, T:T + P], True, True))
                for i in sb_gates(first, 1):
                    project_fm(f"gate{i}", xT)
                for h in sb_heads(first - 4):
                    o = take(f"sbo{h}")
                    pe.wait_ge(S["sb_weight"], h + 1)
                    vc = 2 * W1 + 64 * h
                    mm(o[:, 0:64], wT_sb[:, h % 4, 0:P], v1[:, 0, vc:vc + 64], True, True)
                    mm(o[:, 64:P], wT_sb[:, h % 4, P:T], v1[:, 0, vc:vc + 64], True, False)
                    done(mm(o[:, 64:P], wT_sb[:, h % 4, T:T + P], v1[:, 1, vc:vc + 64], False, True))
            pe.wait_ge(S["o_normed"], 1)
            for k in range(5):
                if k == 3:
                    pe.wait_ge(S["sb_out"], H1)
                turn_o(k)
            pe.wait_ge(S["oT_ready"], 5)
            for n in range(8):
                o = take(f"branch{n}.a")
                for b in range(2):
                    for k in range(3):
                        last = mm3(o[:, b * T:b * T + T], weights(1), cut(oT, 3 * b + k), k == 0, k == 2)
                done(last)
                o = take(f"branch{n}.b")
                for k in range(3):
                    last = mm3(o[:, 0:T], weights(1), cut(oT, 6 + k), k == 0, k == 2)
                done(last)
            for k in range(KD):
                pe.wait_ge(S["merged"], k + 1)
                if k == 0:
                    pe.wait_ge(S["acc_read"], 4)
                last = into_acc(mT1, k, k == 0, k == KD - 1)
            last.then_inc(S["acc_done"], 1)
            turn(1)
            pe.wait_ge(S["xT_ready"], 16)
            ffn(1)
            turn(2)
            pe.wait_ge(S["xT_ready"], 24)
            for t in range(12):
                project_fm(f"conv{t}", xT)
            project_tm(["small0", "small1"], 288, 4, xT)
            project_tm(["z0", "z1"], 512, 4, xT)
            project_fm("kc", xT)
            project_fm("vc", xT)
            for t in range(4):
                project_fm(f"qb{t}", xT)
            project_fm("ks", xT)
            project_fm("kw", xT)
            for t in range(4):
                o = take(f"l2_{t}")
                pe.wait_ge(S["qkv_sq"], 2 * t + 2)
                nc.tensor.matmul(o[:, 0:T], ones, csq[:, 2 * t, :], start=True, stop=True)
                done(nc.tensor.matmul(o[:, T:2 * T], ones, csq[:, 2 * t + 1, :], start=True, stop=True))
            for kv, name in enumerate(("hk", "hv")):
                o = take(name)
                pe.wait_ge(S["kv_pos"], 2 * kv + 2)
                for k in range(16):
                    last = mm3(o[0:2 * NC, 0:T], cut(rcs, kv, k), weights(2), k == 0, k == 15)
                done(last)
            for kv, name in enumerate(("hkT", "hvT")):
                o = take(name)
                pe.wait_ge(S["cmp_hidden"], kv + 1)
                for ht in range(2):
                    last = nc.tensor.transpose(o[:, 2 * NC * ht:2 * NC * ht + 2 * NC], hidden_tm[:, kv, P * ht:P * ht + P],
                                               ident[0:2 * NC, 0:2 * NC])
                done(last)
            o = take("kc2")
            pe.wait_ge(S["cmp_turned"], 1)
            w2k = [weights(1), weights(1)]
            for ht in range(2):
                for n in range(2):
                    last = mm(o[0:64, 0:2 * NC], w2k[ht][n][:, 0:64].bitcast(F32), hh[:, 0, ht, :], (ht, n) == (0, 0),
                              (ht, n) == (1, 1))
            done(last)
            o = take("vc2")
            pe.wait_ge(S["cmp_turned"], 2)
            w2v = [weights(1), weights(1)]
            for g in range(2):
                for ht in range(2):
                    for n in range(2):
                        last = mm(o[0:NC, 64 * g:64 * g + 64], hh[:, 1, ht, NC * g:NC * g + NC],
                                  w2v[ht][n][:, 0:64].bitcast(F32), (ht, n) == (0, 0), (ht, n) == (1, 1))
            done(last)
            at[0] = PART_AT["gmix"]
            o = take("gcum")
            pe.wait_ge(S["g_ready"], 1)
            for ch in range(2):
                last = nc.tensor.matmul(o[:, HG * ch:HG * ch + HG], c("upper"), gk[:, HG * ch:HG * ch + HG], start=True, stop=True)
            done(last)
            for ch in range(2):
                o = take(f"grow{ch}")
                pe.wait_ge(S["g_rows"], 1)
                for h in range(HG):
                    last = nc.tensor.matmul(o[:, h * P:(h + 1) * P], grow[:, HG * ch + h, :], c("upper"), start=True, stop=True)
                done(last)
            for ch in range(2):
                o = take(f"brow{ch}")
                pe.wait_ge(S["g_rows"], 2)
                for h in range(HG):
                    last = nc.tensor.matmul(o[:, h * P:(h + 1) * P], brep[:, HG * ch + h, :], ident, start=True, stop=True)
                done(last)
            pe.wait_ge(S["l2_ready"], 4)
            pe.wait_ge(S["qkv_ready"], 12)
            for ch in range(2):
                t0 = P * ch
                for name, first in ((f"ktm{ch}", 4), (f"vtm{ch}", 8)):
                    o = take(name)
                    for h in range(HG):
                        last = nc.tensor.transpose(o[:, h * P:(h + 1) * P], cv[:, first + h, t0:t0 + P], ident)
                    done(last)
                for name, first in ((f"kk{ch}", 4), (f"qk2_{ch}", 0)):
                    o = take(name)
                    for h in range(HG):
                        last = nc.tensor.matmul(o[:, h * P:(h + 1) * P], cv[:, 4 + h, t0:t0 + P],
                                                cv[:, first + h, t0:t0 + P], start=True, stop=True)
                    done(last)

            def per_head(name, ch, lhsT, rhs):
                o = take(name)
                for h in range(HG):
                    last = nc.tensor.matmul(o[:, h * P:(h + 1) * P], lhsT(HG * ch + h), rhs(HG * ch + h), start=True, stop=True)
                done(last)

            for ch in range(2):
                o = take(f"x0_{ch}")
                pe.wait_ge(S["xt_ready"], ch + 1)
                for h in range(HG):
                    last = nc.tensor.transpose(o[:, h * P:(h + 1) * P], xinvT[:, HG * ch + h, :], ident)
                done(last)
            for lv in range(1, LEVELS):
                pe.wait_ge(S["ot_ready"], lv + 1)
                for ch in range(2):
                    pe.wait_ge(S["x_ready"], 2 * (lv - 1) + ch + 1)
                    per_head(f"y{lv}.{ch}", ch, lambda m: ot[lv % 2][:, m, :], lambda m: xinv[:, m, :])
                for ch in range(2):
                    pe.wait_ge(S["y_ready"], 2 * (lv - 1) + ch + 1)
                    pe.wait_ge(S["xt_ready"], 2 * (lv - 1) + ch + 1)
                    per_head(f"zt{lv}.{ch}", ch, lambda m: yb[:, m, :], lambda m: xinvT[:, m, :])
                    if lv < LEVELS - 1:
                        per_head(f"zz{lv}.{ch}", ch, lambda m: xinvT[:, m, :], lambda m: yb[:, m, :])
                for k in range(2):
                    project_fm(f"gmix{2 * (lv - 1) + k}", xT)
            pe.wait_ge(S["rhs_ready"], 4)
            pe.wait_ge(S["xt_ready"], 2 * LEVELS)
            per_head("u0", 0, lambda m: xinvT[:, m, :], lambda m: vtm[:, 0, m * P:(m + 1) * P])
            per_head("u1", 1, lambda m: xinvT[:, m, :], lambda m: vtm[:, 1, (m - HG) * P:(m - HG + 1) * P])
            per_head("wT", 1, lambda m: kbg[:, (m - HG) * P:(m - HG + 1) * P], lambda m: xinvT[:, m, :])
            pe.wait_ge(S["u_ready"], 2)
            per_head("state", 0, lambda m: ktail[:, m * P:(m + 1) * P], lambda m: ub[:, 0, m * P:(m + 1) * P])
            pe.wait_ge(S["state_ready"], 1)
            pe.wait_ge(S["wT_ready"], 1)
            per_head("ws", 0, lambda m: wT2[:, m * P:(m + 1) * P], lambda m: state[:, m * P:(m + 1) * P])
            per_head("oi0", 0, lambda m: qkd[:, m, :], lambda m: ub[:, 0, m * P:(m + 1) * P])
            pe.wait_ge(S["u_ready"], 3)
            per_head("oi1", 1, lambda m: qkd[:, m, :], lambda m: ub[:, 1, (m - HG) * P:(m - HG + 1) * P])
            per_head("ox", 0, lambda m: cv[:, m, P:T], lambda m: state[:, m * P:(m + 1) * P])
            pe.wait_ge(S["kcomp_ready"], 1)
            pe.wait_ge(S["qb_ready"], 4)
            for tok in range(2):
                o = take(f"cs{tok}")
                for pr in range(4):
                    last = nc.tensor.matmul(o[:, 64 * pr:64 * pr + 64], qbT[:, pr, P * tok:P * tok + P], bdk[:, pr // 2, :],
                                            start=True, stop=True)
                done(last)
            for tok in range(2):
                o = take(f"ct{tok}")
                pe.wait_ge(S["cmp_probs"], tok + 1)
                for g in range(2):
                    last = nc.tensor.transpose(o[:, g * P:(g + 1) * P], cs_sb[:, tok, g * P:(g + 1) * P], ident)
                done(last)
            pe.wait_ge(S["vcomp_ready"], 1)
            for tok in range(2):
                o = take(f"co{tok}")
                pe.wait_ge(S["cmp_pt"], tok + 1)
                for g in range(2):
                    last = nc.tensor.matmul(o[:, g * T:(g + 1) * T], cpT[:, tok, g * P:(g + 1) * P], bdv[:, g, :],
                                            start=True, stop=True)
                done(last)
            pe.wait_ge(S["kdup_ready"], 2)
            for i in range(N_INST2 + 2):
                attention(i, N_INST1, N_INST2, lambda t: qbT[:, t, :], lambda t: kdup[:, t[0], t[1], :], sm, inst[N_INST1])
                if i < 4:
                    project_fm(f"gmix{12 + i}", xT)
            for k in range(4):
                o = take(f"yT{k}")
                if k == 0:
                    pe.wait_ge(S["gdn_normed"], 1)
                src = og if k < 2 else o2
                if k == 2:
                    pe.wait_ge(S["attn_out"], N_INST1 + N_INST2)
                for kk in range(2):
                    for tok in range(2):
                        f = 2 * (k % 2) + kk
                        last = nc.tensor.transpose(o[:, (2 * kk + tok) * P:(2 * kk + tok + 1) * P],
                                                   src[:, tok, f * P:(f + 1) * P], ident)
                done(last)
            pe.wait_ge(S["yT_ready"], 4)
            for n in range(8):
                o = take(f"mix{n}")
                for b in range(2):
                    for k in range(4):
                        last = mm3(o[:, b * T:b * T + T], weights(1), cut(yT, 4 * b + k), k == 0, k == 3)
                done(last)
            for k in range(KD):
                pe.wait_ge(S["mixed"], k + 1)
                if k == 0:
                    pe.wait_ge(S["acc_read"], 12)
                last = into_acc(mT2, k, k == 0, k == KD - 1)
            last.then_inc(S["acc_done"], 1)
            pe.wait_ge(S["p_split"], 1)
            o = [take(f"ple{k}") for k in range(4)]
            for k in range(2):
                for half in range(2):
                    w = weights(4)
                    for tok in range(2):
                        last = mm3(o[2 * tok + half], cut(pE, k, slice(P * tok, P * tok + P)), w, k == 0, k == 1)
                        if k == 1 and (half, tok) == (1, 1):
                            last.then_inc(S["job_done"], 4)
            turn(3)
            pe.wait_ge(S["xT_ready"], 32)
            ffn(2)
            turn(4)
            pe.wait_ge(S["xT_ready"], 40)
            pe.wait_ge(S["acc_read"], 20)
            for k in range(KD):
                last = into_acc(xT, k, k == 0, k == KD - 1)
            last.then_inc(S["acc_done"], 1)
            assert now[0] == len(jobs) and at[0] == N_BLOCKS, (now, len(jobs), at, N_BLOCKS)

        @block.scalar
        def _(act):
            steps = [0]

            def link(ins):
                steps[0] += 1
                ins.then_inc(S["act_step"], 1)
                act.wait_ge(S["act_step"], steps[0])

            act.dma_start(x_in_fm, x_fm).then_inc(S["xT_in"], 16)

            def rows_in(k):
                need(act, "row_free", k - 1)
                n = len(BIG_ROWS[k]) * D
                act.dma_start(rows[:, k % 2, 0:n], big_rows[k:k + 1, 0:n].partition_broadcast(P)
                              ).then_inc(S[f"big_rows_in{k % 2}"], 16)

            fed = [0]

            def high(ch, it=0):
                act.wait_ge(arrived[ch % RING], 16 * (ch // RING + 1) + 16 * (ROUND // RING) * it)
                need(act, "used", ch - RING + 1 + ROUND * it)
                nc.scalar.copy(whi[:, ch % RING, :], ring[:, ch % RING, :]).then_inc(S["hi_ready"], 1)

            def feed(blocks, it=0):
                while fed[0] < min((blocks - 1) // CB + RING, N_CHUNKS):
                    high(fed[0], it)
                    fed[0] += 1

            def wait_job(name):
                feed(jobs[index[name]][2])
                job_wait(act, name)

            def ffn_act(n, f, it=0):
                j = index[f"ffn{n}.0"] + f
                feed(PART_AT[f"ffn{n}"] + ffn_end(f), it)
                act.wait_ge(S["job_done"], j + 1 + GROUP * it)
                if NF * n + f >= 2:
                    act.wait_ge(S["hidden"], NF * n + f - 1 + GROUP * it)
                nc.scalar.activation(act_buf[:, f % 2, 0:T], banks[:, j % NBANK, 0:T], ACT.Silu
                                     ).then_inc(S["act_done"], 1)

            def conv_col(name, i, it, per):
                o = COL_AT[name] + i
                if isinstance(it, int):
                    return col[:, o + per * GROUP * it:o + per * GROUP * it + 1]
                return col[:, bass.ds(o + per * GROUP * it, 1)]

            def geglu_act(f, it=0):
                j = index["ffn2.0"] + f
                feed(PART_AT["ffn2"] + ffn_end(f), it)
                act.wait_ge(S["job_done"], j + 1 + GROUP * it)
                act.wait_ge(S["hidden"], 2 * NF + f - 1 + GROUP * it)
                for half in range(2):
                    last = nc.scalar.activation(act_buf[:, f % 2, half * T:half * T + T], banks[:, j % NBANK, half * T:half * T + T],
                                                ACT.Identity, bias=conv_col("conv_ffn_b", half * NF + f, it, 1),
                                                scale=conv_col("conv_ffn", 3 * (half * NF + f) + 2, it, 3))
                last.then_inc(S["tap_in"], 1)
                act.wait_ge(S["taps"], f + 1 + GROUP * it)
                nc.scalar.activation(gel[:, f % 2, :], act_buf[:, f % 2, 0:T], ACT.Gelu_apprx_tanh).then_inc(S["act_done"], 1)

            def over_ffn(n, body):
                for f in range(0, 1 + GROUP):
                    body(f)
                with nc.scalar.Fori(1, (NF - 2) // GROUP) as it:
                    for f in range(1, 1 + GROUP):
                        body(f + GROUP, it - 1)
                fed[0] += ROUND * ((NF - 2) // GROUP - 2)
                body(NF - 1)
                feed(PART_AT[f"ffn{n}"] + 24 * NF)

            def warm(func):
                link(nc.scalar.activation(stat[:, 62:63], c("one"), func))

            def std(i, col_in, col_out, scale, eps):
                nc.scalar.activation(stat[:, col_out:col_out + 2], stat[:, col_in:col_in + 2], ACT.Sqrt, bias=c(eps), scale=scale
                                     ).then_inc(S["std_ready"], 1)

            def turn(i, gain=None, bias=None):
                for g in range(4):
                    wait_job(f"turn{i}.{g}")
                    for kk in range(2):
                        k = 2 * g + kk
                        src = bank(f"turn{i}.{g}")[:, kk * T:kk * T + T]
                        if gain is None:
                            ins = nc.scalar.copy(xT[0][:, k, :], src)
                        elif bias is None:
                            ins = nc.scalar.activation(xT[0][:, k, :], src, ACT.Copy, scale=pcol(gain, k))
                        else:
                            ins = nc.scalar.activation(xT[0][:, k, :], src, ACT.Identity, bias=pcol(bias, k), scale=pcol(gain, k))
                        ins.then_inc(S["xT_high"], 1)

            def attention(i, base, n):
                sS, prob, pT = attn_bufs[base]
                if i < n:
                    j = base + i
                    act.wait_ge(S["row_max"], 2 * (j + 1))
                    if j >= 2:
                        if i >= 2:
                            wait_job(f"t{j - 2}")
                        act.wait_ge(S["coef"], j - 1)
                    for t, lo, hi in ((0, 0, P), (1, P, 3 * P)):
                        nc.scalar.activation(prob[:, j % 2, lo:hi], sS[:, j % 2, lo:hi], ACT.Exp, bias=nmx[:, j % 2, t:t + 1],
                                             accum_out=den[:, j % 2, t:t + 1]).then_inc(S["probs"], 1)
                if 1 <= i <= n:
                    j = base + i - 1
                    wait_job(f"t{j}")
                    if i >= 3:
                        wait_job(f"o{j - 2}")
                    nc.scalar.copy(pT[:, j % 2, :], bank(f"t{j}")[:, 0:384]).then_inc(S["pt_ready"], 1)

            act.wait_ge(S["xT_in"], 16)
            for k in range(0, KD, 4):
                nc.scalar.copy(xT[0][:, k:k + 4, :], x_in_fm[:, k:k + 4, :]).then_inc(S["x_high"], 4)
            feed(1)

            def first_ffn(f, it=0):
                ffn_act(0, f, it)
                if f == 0:
                    act.dma_start(xs[:, 0], x_tm).then_inc(S["x_in"], 16)
                    act.dma_start(col[:], cols).then_inc(S["cols_in"], 16)
                elif f == 1:
                    act.dma_start(cst[:], consts).then_inc(S["consts_in"], 16)
                elif f == 2:
                    act.dma_start(srow[:], small_rows.partition_broadcast(P)).then_inc(S["rows_in"], 16)
                elif f == 3:
                    rows_in(0)
                elif f == 4:
                    rows_in(1)

            over_ffn(0, first_ffn)
            act.wait_ge(S["consts_in"], 16)
            act.wait_ge(S["cols_in"], 16)
            warm(ACT.Sqrt)
            act.wait_ge(S["var_ready"], 1)
            std(0, 0, 4, 1.0, "eps_ln4")
            turn(0, "ln_g0", "ln_b0")
            scale = {0: 0.125, 2: float(np.float32(32 ** -0.5)), 4: 0.125}
            for t in range(18):
                wait_job(f"qk{t}")
                ps = bank(f"qk{t}")[:, 0:T]
                nc.scalar.activation(qkT[:, t, :], ps, ACT.Copy, scale=scale.get(t // 3, 1.0)).then_inc(S["qk_ready"], 1)
            feed(PART_AT["gate"])
            act.wait_ge(S["lam_arg"], 1)
            nc.scalar.activation(stat[:, 18:20], stat[:, 16:18], ACT.Exp).then_inc(S["lam_exp"], 1)

            def gate_raw(k):
                wait_job(f"gate{k}")
                nc.scalar.activation(gates1[:, k // 8, k % 8, :], bank(f"gate{k}")[:, 0:T], ACT.Identity,
                                     bias=pcol("b_gate", k)).then_inc(S["gate_raw"], 1)

            for i in range(N_INST1 + 2):
                attention(i, 0, N_INST1)
                if i < 16:
                    gate_raw(i)
            for first in range(0, H1 + 4, 2):
                for i in sb_heads(first):
                    act.wait_ge(S["sb_neg"], i + 1)
                    nc.scalar.activation(lg[:, i % 4, :], lg[:, i % 4, :], ACT.Exp).then_inc(S["sb_exp"], 1)
                for i in sb_heads(first):
                    act.wait_ge(S["sb_exp"], i + 1)
                    nc.scalar.activation(lg[:, i % 4, :], lg[:, i % 4, :], ACT.Ln, bias=c("one")).then_inc(S["sb_log"], 1)
                for i in sb_gates(first, 0):
                    gate_raw(i)
                for h in sb_heads(first - 2):
                    act.wait_ge(S["sb_exponent"], h + 1)
                    if h >= 4:
                        wait_job(f"sbo{h - 4}")
                    nc.scalar.activation(wT_sb[:, h % 4, :], zm[:, h % 4, :], ACT.Exp).then_inc(S["sb_weight"], 1)
                for i in sb_gates(first, 1):
                    gate_raw(i)
                if first == H1 - 2:
                    act.wait_ge(S["subln_sum"], 1)
                    nc.scalar.activation(stat[:, 32:44], stat[:, 20:32], ACT.Sqrt, bias=c("eps_ln"), scale=1.0 / 64
                                         ).then_inc(S["subln_std"], 1)
            for k in range(5):
                n = 2 if k < 4 else 1
                wait_job(f"oT{k}")
                nc.scalar.copy(oT[0][:, 2 * k:2 * k + n, :].rearrange("p a t -> p (a t)"), bank(f"oT{k}")[:, 0:n * T]
                               ).then_inc(S["oT_high"], 1)
            act.wait_ge(S["gate_raw"], 24)
            g1 = gates1[:].rearrange("p a b t -> p (a b t)")
            nc.scalar.activation(g1, g1, ACT.Sigmoid).then_inc(S["gates_ready"], 1)
            feed(PART_AT["ffn1"])
            warm(ACT.Sqrt)
            act.wait_ge(S["var_ready"], 2)
            std(1, 0, 4, 1.0, "eps_ln")
            turn(1, "ln_g1", "ln_b1")
            rows_in(2)
            over_ffn(1, lambda f, it=0: ffn_act(1, f, it))
            rows_in(3)
            warm(ACT.Sqrt)
            act.wait_ge(S["var_ready"], 3)
            std(2, 0, 4, 1.0, "eps_ln4")

            def sum_squares(k, src, junk):
                for tok in range(2):
                    ins = nc.scalar.activation(junk, src(tok), ACT.Square, accum_out=stat[:, 8 + tok:9 + tok])
                    if tok == 0:
                        link(ins)
                    else:
                        ins.then_inc(S["sq_ready"], 1)
                act.wait_ge(S["sq_ready"], k)
                std(0, 8, 4, 1.0 / D, "eps_rms")

            junk2 = tmp[:].rearrange("p a b -> p (a b)")
            act.wait_ge(S["norm_sum"], 1)
            sum_squares(1, lambda tok: xs[:, 1, tok, :], junk2)
            turn(2, "mix_pre")

            def conv_silu(t):
                act.wait_ge(S["qkv_taps"], t + 1)
                nc.scalar.activation(cv[:, t, :], cv[:, t, :], ACT.Silu).then_inc(S["qkv_ready"], 1)
                if t < 8:
                    act.wait_ge(S["qkv_ready"], t + 1)
                    nc.scalar.activation(csq[:, t, :], cv[:, t, :], ACT.Square).then_inc(S["qkv_sq"], 1)

            for t in range(12):
                wait_job(f"conv{t}")
                nc.scalar.activation(cv[:, t, :], bank(f"conv{t}")[:, 0:T], ACT.Copy, scale=pcol("conv_qkv", 4 * t + 3)
                                     ).then_inc(S["qkv_tap_in"], 1)
                if t >= 1:
                    conv_silu(t - 1)
            conv_silu(11)
            for tok in range(2):
                wait_job(f"z{tok}")
                nc.scalar.activation(zs[:, tok, :], bank(f"z{tok}"), ACT.Silu).then_inc(S["z_ready"], 1)
            act.wait_ge(S["sg_arg"], 1)
            nc.scalar.activation(sm[:, :, 256:284], sm[:, :, 256:284], ACT.Exp, scale=-1.0).then_inc(S["sg_exp"], 1)
            act.wait_ge(S["dt_arg"], 1)
            link(nc.scalar.activation(gk[:, 24:32], gk[:, 24:32], ACT.Exp))
            nc.scalar.activation(gk[:, 24:32], gk[:, 24:32], ACT.Ln, bias=c("one"))
            nc.scalar.activation(gk[:, 32:36], sr("a_log", HG), ACT.Exp).then_inc(S["dt_log"], 1)
            for t in range(4):
                wait_job(f"qb{t}")
                nc.scalar.activation(qbT[:, t, :], bank(f"qb{t}")[:, 0:T], ACT.Copy, scale=0.125).then_inc(S["qb_ready"], 1)
            sq_pair = [csq[:, 2 * t:2 * t + 2, :].rearrange("p a t -> p (a t)") for t in range(4)]
            for t, pair in enumerate(sq_pair):
                wait_job(f"l2_{t}")
                nc.scalar.activation(pair, bank(f"l2_{t}"), ACT.Ln, bias=c("eps_rms")).then_inc(S["l2_log"], 1)
            for t, pair in enumerate(sq_pair):
                act.wait_ge(S["l2_log"], t + 1)
                nc.scalar.activation(pair, pair, ACT.Exp, scale=-0.5).then_inc(S["l2_scale"], 1)
            for kv, name in enumerate(("hk", "hv")):
                wait_job(name)
                nc.scalar.activation(hidden_tm[:, kv], bank(name)[0:2 * NC, 0:T], ACT.Gelu_apprx_tanh).then_inc(S["cmp_hidden"], 1)
            for kv, name in enumerate(("hkT", "hvT")):
                wait_job(name)
                nc.scalar.copy(hh[:, kv].rearrange("p a n -> p (a n)"), bank(name)[:, 0:4 * NC]).then_inc(S["cmp_turned"], 1)
            act.wait_ge(S["gcum_neg"], 1)
            nc.scalar.activation(gk[:, 64:72], gk[:, 40:48], ACT.Exp).then_inc(S["gam"], 1)
            act.wait_ge(S["tail_arg"], 1)
            nc.scalar.activation(gk[:, 72:76], gk[:, 72:76], ACT.Exp).then_inc(S["tail"], 1)
            for ch in range(2):
                act.wait_ge(S["decay_arg"], ch + 1)
                for h in range(HG):
                    m = HG * ch + h
                    nc.scalar.activation(dec[:, m, :], dec[:, m, :], ACT.Exp, bias=gk[:, 48 + m:49 + m]).then_inc(S["decay"], 1)
            for ch in range(2):
                wait_job(f"ktm{ch}")
                nc.scalar.copy(ktm[:, ch, :], bank(f"ktm{ch}")).then_inc(S["ktm_ready"], 1)
                wait_job(f"vtm{ch}")
                nc.scalar.copy(vtm[:, ch, :], bank(f"vtm{ch}")).then_inc(S["vtm_ready"], 1)

            def gmix_raw(k):
                wait_job(f"gmix{k}")
                nc.scalar.copy(gates2[:, k // 8, k % 8, :], bank(f"gmix{k}")[:, 0:T]).then_inc(S["gmix_raw"], 1)

            for lv in range(1, LEVELS):
                for ch in range(2):
                    wait_job(f"y{lv}.{ch}")
                    nc.scalar.copy(yb[:, HG * ch:HG * ch + HG, :].rearrange("p a t -> p (a t)"), bank(f"y{lv}.{ch}")
                                   ).then_inc(S["y_ready"], 1)
                for k in range(2):
                    gmix_raw(2 * (lv - 1) + k)
            for ch in range(2):
                wait_job(f"u{ch}")
                nc.scalar.copy(ub[:, ch, :], bank(f"u{ch}")).then_inc(S["u_ready"], 1)
            wait_job("wT")
            nc.scalar.copy(wT2, bank("wT")).then_inc(S["wT_ready"], 1)
            wait_job("state")
            nc.scalar.copy(state, bank("state")).then_inc(S["state_ready"], 1)
            for tok in range(2):
                act.wait_ge(S["cmp_arg"], tok + 1)
                nc.scalar.activation(cs_sb[:, tok, :], cs_sb[:, tok, :], ACT.Exp).then_inc(S["cmp_probs"], 1)
            for tok in range(2):
                wait_job(f"ct{tok}")
                nc.scalar.copy(cpT[:, tok, :], bank(f"ct{tok}")[:, 0:T]).then_inc(S["cmp_pt"], 1)
            for i in range(N_INST2 + 2):
                attention(i, N_INST1, N_INST2)
                if i < 4:
                    gmix_raw(12 + i)
            act.wait_ge(S["gdn_sum"], 1)
            nc.scalar.activation(stat[:, 32:40], stat[:, 20:28], ACT.Sqrt, bias=c("eps_rms"), scale=1.0 / P
                                 ).then_inc(S["gdn_std"], 1)
            act.wait_ge(S["gmix_raw"], 16)
            g2 = gates2[:].rearrange("p a b t -> p (a b t)")
            nc.scalar.activation(g2, g2, ACT.Sigmoid).then_inc(S["gmix_ready"], 1)
            for k in range(4):
                wait_job(f"yT{k}")
                nc.scalar.copy(yT[0][:, 2 * k:2 * k + 2, :].rearrange("p a t -> p (a t)"), bank(f"yT{k}")).then_inc(S["yT_high"], 1)
            act.dma_start(p_raw, p_fm).then_inc(S["p_in"], 16)
            act.wait_ge(S["p_in"], 16)
            nc.scalar.copy(pE[0][:], p_raw).then_inc(S["x_high"], 1)
            rows_in(4)
            feed(PART_AT["ple"])
            warm(ACT.Sqrt)
            act.wait_ge(S["acc_done"], 4)
            act.wait_ge(S["mixed"], 8)
            sum_squares(2, lambda tok: acc[:, 2 * tok:2 * tok + 2, :].rearrange("p a n -> p (a n)"), junk2)
            for k in range(4):
                wait_job(f"ple{k}")
                nc.scalar.copy(ple_flat[:, 512 * k:512 * k + 512], bank(f"ple{k}")).then_inc(S["ple_ready"], 1)
            act.wait_ge(S["norm_sum"], 2)
            sum_squares(3, lambda tok: xs[:, 0, tok, :], junk2)
            turn(3, "ffn_pre")
            rows_in(5)
            over_ffn(2, geglu_act)
            warm(ACT.Sqrt)
            act.wait_ge(S["acc_done"], 5)
            sum_squares(4, lambda tok: acc[:, 2 * tok:2 * tok + 2, :].rearrange("p a n -> p (a n)"), junk2)
            turn(4)
            feed(N_BLOCKS)
            warm(ACT.Sigmoid)
            act.wait_ge(S["acc_done"], 6)
            for tok in range(2):
                nc.scalar.activation(res[:, tok, :], acc[:, 2 * tok:2 * tok + 2, :].rearrange("p a n -> p (a n)"), ACT.Sigmoid
                                     ).then_inc(S["acc_read"], 1)
            warm(ACT.Sqrt)
            act.wait_ge(S["ple_gated"], 2)
            sum_squares(5, lambda tok: res[:, tok, :], junk2)

        @block.vector
        def _(dve):
            steps = [0]
            v = nc.vector

            def link(ins):
                steps[0] += 1
                ins.then_inc(S["dve_step"], 1)
                dve.wait_ge(S["dve_step"], steps[0])

            def mark(ins, sem, value):
                ins.then_inc(S[sem], 1)
                dve.wait_ge(S[sem], value)

            def hidden(n, f, it=0):
                j = index[f"ffn{n}.0"] + f
                dve.wait_ge(S["act_done"], NF * n + f + 1 + GROUP * it)
                if f >= GROUP:
                    dve.wait_ge(S["down_done"], (NF - 1) * n + f - GROUP + 1 + GROUP * it)
                v.tensor_tensor(hf[:, f % 2, :], act_buf[:, f % 2, 0:T], banks[:, j % NBANK, T:2 * T], ALU.mult
                                ).then_inc(S["h_made"], 1)
                split_hidden(n, f, it)

            def split_hidden(n, f, it):
                value = NF * n + f + 1 + GROUP * it
                dve.wait_ge(S["h_made"], value)
                v.tensor_copy(hT[0][:, f % GROUP, :], hf[:, f % 2, :]).then_inc(S["h_high"], 1)
                dve.wait_ge(S["h_high"], value)
                v.tensor_tensor(hT[1][:, f % GROUP, :], hf[:, f % 2, :], hT[0][:, f % GROUP, :].bitcast(F32), ALU.subtract
                                ).then_inc(S["hidden"], 1)

            def conv_col(i, it):
                o = COL_AT["conv_ffn"] + i
                if isinstance(it, int):
                    return col[:, o:o + 1]
                return col[:, bass.ds(o + 3 * GROUP * it, 1)]

            def conv_hidden(f, it=0):
                j = index["ffn2.0"] + f
                dve.wait_ge(S["tap_in"], f + 1 + GROUP * it)
                for tap in (1, 0):
                    sh = 2 - tap
                    for half in range(2):
                        buf = act_buf[:, f % 2, half * T + sh:half * T + T]
                        last = v.scalar_tensor_tensor(buf, banks[:, j % NBANK, half * T:half * T + T - sh],
                                                      conv_col(3 * (half * NF + f) + tap, it), buf, ALU.mult, ALU.add)
                    if tap == 1:
                        last.then_inc(S["dve_step"], 1)
                        dve.wait_ge(S["dve_step"], steps[0] + f + 1 + GROUP * it)
                last.then_inc(S["taps"], 1)
                dve.wait_ge(S["act_done"], 2 * NF + f + 1 + GROUP * it)
                dve.wait_ge(S["down_done"], (NF - 1) * 2 + f - GROUP + 1 + GROUP * it)
                v.tensor_tensor(hf[:, f % 2, :], gel[:, f % 2, :], act_buf[:, f % 2, T:2 * T], ALU.mult
                                ).then_inc(S["h_made"], 1)
                split_hidden(2, f, it)

            def over_ffn(body):
                for f in range(0, 1 + GROUP):
                    body(f)
                with nc.vector.Fori(1, (NF - 2) // GROUP) as it:
                    for f in range(1, 1 + GROUP):
                        body(f + GROUP, it - 1)
                body(NF - 1)

            def layer_norm(i, src, dst, factor, k, w):
                dve.wait_ge(S["acc_done"], (1, 2, 3)[i])
                for tok in range(2):
                    for half in range(2):
                        hs = slice(512 * half, 512 * half + 512)
                        mark(v.scalar_tensor_tensor(res[:, tok, hs], xs[:, src, tok, hs], factor, acc[:, 2 * tok + half, :],
                                                    ALU.mult, ALU.add), "acc_read", 4 * i + 2 * tok + half + 1)
                        link(v.bn_stats(stat[:, 44 + 6 * half:50 + 6 * half], res[:, tok, hs]))
                    link(v.bn_aggr(stat[:, 12 + 2 * tok:14 + 2 * tok], stat[:, 44:56]))
                v.tensor_copy(stat[:, 0:2], stat[:, 12:16].rearrange("p (a b) -> p a b", b=2)[:, :, 1]).then_inc(S["var_ready"], 1)
                dve.wait_ge(S["std_ready"], w)
                link(v.reciprocal(stat[:, 6:8], stat[:, 4:6]))
                for tok in range(2):
                    ins = v.tensor_scalar(res[:, tok, :], res[:, tok, :], stat[:, 12 + 2 * tok:13 + 2 * tok], stat[:, 6 + tok:7 + tok],
                                          ALU.subtract, ALU.mult)
                    if k is not None:
                        ins.then_inc(S["xn_ready"], 1)
                        dve.wait_ge(S["xn_ready"], k + tok + 1)
                    else:
                        link(ins)
                if i < 2:
                    turn(i, f"ln_g{i}", f"ln_b{i}")
                dve.wait_ge(S[f"big_rows_in{i % 2}"], 16 * (i // 2 + 1))
                for tok in range(2):
                    link(v.tensor_tensor(xs[:, dst, tok, :], res[:, tok, :], rows[:, i % 2, 0:D], ALU.mult))
                    ins = v.tensor_tensor(xs[:, dst, tok, :], xs[:, dst, tok, :], rows[:, i % 2, D:2 * D], ALU.add)
                    if tok:
                        mark(ins, "row_free", i + 1)
                    else:
                        link(ins)

            def rms_scaled(src, k, w):
                dve.wait_ge(S["std_ready"], w)
                link(v.reciprocal(stat[:, 6:8], stat[:, 4:6]))
                for tok in range(2):
                    v.tensor_scalar(res[:, tok, :], xs[:, src, tok, :], stat[:, 6 + tok:7 + tok], None, ALU.mult
                                    ).then_inc(S["xn_ready"], 1)

            def add_normed(i, src, dst, value, w, final=False):
                dve.wait_ge(S["std_ready"], w)
                link(v.reciprocal(stat[:, 6:8], stat[:, 4:6]))
                dve.wait_ge(S[f"big_rows_in{i % 2}"], 16 * (i // 2 + 1))
                for tok in range(2):
                    for half in range(2):
                        hs = slice(512 * half, 512 * half + 512)
                        ins = v.scalar_tensor_tensor(xs[:, dst, tok, hs], value(tok, half), stat[:, 6 + tok:7 + tok],
                                                     rows[:, i % 2, hs], ALU.mult, ALU.mult)
                        if final:
                            link(ins)
                        else:
                            mark(ins, "acc_read", (12, 16)[i - 3] + 2 * tok + half + 1)
                    ins = v.tensor_tensor(xs[:, dst, tok, :], xs[:, dst, tok, :], xs[:, src, tok, :], ALU.add)
                    if final:
                        ins.then_inc(S["final"], 1)
                    elif tok:
                        mark(ins, "row_free", i + 1)
                    else:
                        link(ins)

            def low(out, value, high):
                return v.tensor_tensor(out, value, high.bitcast(F32), ALU.subtract)

            def turn(i, gain=None, bias=None):
                for g in range(4):
                    dve.wait_ge(S["xT_high"], 8 * i + 2 * g + 2)
                    for kk in range(2):
                        k = 2 * g + kk
                        src = bank(f"turn{i}.{g}")[:, kk * T:kk * T + T]
                        if bias is not None:
                            value = tmp[:, k % 2, 0:T]
                            link(v.tensor_scalar(value, src, pcol(gain, k), pcol(bias, k), ALU.mult, ALU.add))
                        hi = xT[0][:, k, :]
                        if gain is None or bias is not None:
                            ins = low(xT[1][:, k, :], src if gain is None else value, hi)
                        else:
                            ins = v.scalar_tensor_tensor(xT[1][:, k, :], src, pcol(gain, k), hi.bitcast(F32), ALU.mult, ALU.subtract)
                        ins.then_inc(S["xT_ready"], 1)

            def split_merged(mT, n, value, sem):
                link(v.tensor_copy(mT[0][:, n, :], value))
                mark(low(mT[1][:, n, :], value, mT[0][:, n, :]), sem, n + 1)

            def signal(sem):
                v.tensor_copy(stat[:, 63:64], stat[:, 6:7]).then_inc(S[sem], 1)

            def attention(i, base, n):
                sS = attn_bufs[base][0]
                if i < n:
                    j = base + i
                    slope = inst[base][i][5]
                    job_wait(dve, f"s{j}")
                    if j >= 2:
                        dve.wait_ge(S["probs"], 2 * (j - 1))
                    mark(v.scalar_tensor_tensor(sS[:, j % 2, :], c("negdist"), slope, bank(f"s{j}")[:, 0:384], ALU.mult, ALU.add),
                         "biased", j + 1)
                    for t, lo, hi in ((0, 0, P), (1, P, 3 * P)):
                        v.tensor_reduce(nmx[:, j % 2, t:t + 1], sS[:, j % 2, lo:hi], AX.X, ALU.max, negate=True
                                        ).then_inc(S["row_max"], 1)
                if i >= 1 and i <= n:
                    j = base + i - 1
                    how = inst[base][i - 1][7]
                    dve.wait_ge(S["probs"], 2 * (j + 1))
                    if isinstance(how, tuple):
                        h, kind = how
                        link(v.reciprocal(coef[:, j % 2, :], den[:, j % 2, :]))
                        mark(v.tensor_tensor(coef[:, j % 2, :], coef[:, j % 2, :], sm[:, :, T + 3 * h + kind + 1], ALU.mult),
                             "coef", j + 1)
                    elif how == "second":
                        link(v.reciprocal(coef[:, j % 2, :], den[:, j % 2, :]))
                        mark(v.tensor_scalar(coef[:, j % 2, :], coef[:, j % 2, :], stat[:, 61:62], None, ALU.mult), "coef", j + 1)
                    else:
                        mark(v.reciprocal(coef[:, j % 2, :], den[:, j % 2, :]), "coef", j + 1)
                if i >= 2:
                    j = base + i - 2
                    oc, how = inst[base][i - 2][6:8]
                    dst = o1 if base == 0 else o2
                    job_wait(dve, f"o{j}")
                    for tok in range(2):
                        src = bank(f"o{j}")[:, 64 * tok:64 * tok + 64]
                        d = dst[:, tok, oc:oc + 64]
                        if how == "first":
                            last = v.tensor_scalar(d, src, coef[:, j % 2, tok:tok + 1], None, ALU.mult)
                        else:
                            last = v.scalar_tensor_tensor(d, src, coef[:, j % 2, tok:tok + 1], d, ALU.mult, ALU.add)
                    mark(last, "attn_out", j + 1)

            for k in range(KD):
                dve.wait_ge(S["x_high"], k + 1)
                low(xT[1][:, k, :], x_in_fm[:, k, :], xT[0][:, k, :]).then_inc(S["x_split"], 1)
            over_ffn(lambda f, it=0: hidden(0, f, it))
            dve.wait_ge(S["x_in"], 16)
            layer_norm(0, 0, 1, 2 * ALPHA, 0, 1)
            dve.wait_ge(S["rows_in"], 16)
            lam = sr("lambda", P)
            la = lam.rearrange("p (a b d) -> p a b d", a=2, b=2)
            link(v.tensor_tensor(tmp[:, 0, 0:64].rearrange("p (a d) -> p a d", a=2), la[:, :, 0, :], la[:, :, 1, :], ALU.mult))
            v.tensor_reduce(stat[:, 16:18], tmp[:, 0, 0:64].rearrange("p (a d) -> p a d", a=2), AX.X, ALU.add
                            ).then_inc(S["lam_arg"], 1)
            for ch in range(3):
                for tok in range(2):
                    job_wait(dve, f"v{ch}.{tok}")
                    v.tensor_copy(v1[:, tok, W1 * ch:W1 * ch + W1], bank(f"v{ch}.{tok}")[:, 0:W1]).then_inc(S["v_ready"], 1)
            dve.wait_ge(S["lam_exp"], 1)
            link(v.tensor_tensor(stat[:, 60:61], stat[:, 19:20], stat[:, 18:19], ALU.subtract))
            link(v.tensor_scalar(stat[:, 61:62], stat[:, 60:61], -(0.8 - 0.6), None, ALU.add))
            for i in range(N_INST1 + 2):
                attention(i, 0, N_INST1)

            def low_o(k):
                n = 2 if k < 4 else 1
                dve.wait_ge(S["oT_high"], k + 1)
                hi, lo = (x[:, 2 * k:2 * k + n, :].rearrange("p a t -> p (a t)") for x in oT)
                low(lo, bank(f"oT{k}")[:, 0:n * T], hi).then_inc(S["oT_ready"], 1)

            for first in range(0, H1 + 4, 2):
                for i in sb_heads(first):
                    job_wait(dve, f"sbz{i}")
                    if i >= 4:
                        dve.wait_ge(S["sb_weight"], i - 3)
                    link(v.tensor_tensor(zm[:, i % 4, :], bank(f"sbz{i}")[:, 0:384], c("sbmask"), ALU.add))
                    mark(v.scalar_tensor_tensor(lg[:, i % 4, :], zm[:, i % 4, :], -1.0, zm[:, i % 4, :], ALU.mult, ALU.min),
                         "sb_neg", i + 1)
                for h in sb_heads(first - 2):
                    job_wait(dve, f"sbr{h}")
                    mark(v.tensor_tensor(zm[:, h % 4, :], zm[:, h % 4, :], bank(f"sbr{h}")[:, 0:384], ALU.subtract),
                         "sb_exponent", h + 1)
                for h in sb_heads(first):
                    dve.wait_ge(S["sb_log"], h + 1)
                    mark(v.scalar_tensor_tensor(lg[:, h % 4, :], zm[:, h % 4, :], 0.0, lg[:, h % 4, :], ALU.max, ALU.add),
                         "sb_softplus", h + 1)
                if first == 2:
                    od = o1[:, :, W1:2 * W1]
                    odh = od.rearrange("p a (h d) -> p a h d", d=64)
                    link(v.tensor_tensor(sq1, od, od, ALU.mult))
                    v.tensor_reduce(stat[:, 20:32], sq1.rearrange("p a (h d) -> p (a h) d", d=64), AX.X, ALU.add
                                    ).then_inc(S["subln_sum"], 1)
                if first == H1:
                    dve.wait_ge(S["subln_std"], 1)
                    link(v.reciprocal(stat[:, 44:56], stat[:, 32:44]))
                    link(v.tensor_scalar(stat[:, 44:56], stat[:, 44:56], 1.0 - (0.8 - 0.6), None, ALU.mult))
                    for tok in range(2):
                        link(v.tensor_tensor(odh[:, tok], odh[:, tok],
                                             stat[:, 44 + H1 * tok:44 + H1 * tok + H1].unsqueeze(2).broadcast_to([P, H1, 64]), ALU.mult))
                        ins = v.tensor_tensor(odh[:, tok], odh[:, tok], sr("subln", 64).unsqueeze(1).broadcast_to([P, H1, 64]), ALU.mult)
                    ins.then_inc(S["o_normed"], 1)
                for h in sb_heads(first - 4):
                    job_wait(dve, f"sbo{h}")
                    oc = 2 * W1 + 64 * h
                    v.tensor_copy(o1[:, :, oc:oc + 64], bank(f"sbo{h}")[:, 0:P].rearrange("p (a d) -> p a d", a=2)
                                  ).then_inc(S["sb_out"], 1)
            for k in range(5):
                low_o(k)
            dve.wait_ge(S["gates_ready"], 1)
            for n in range(8):
                job_wait(dve, f"branch{n}.a")
                mark(v.tensor_tensor(tmp[:, 0, :].rearrange("p (a t) -> p a t", a=2), gates1[:, 0:2, n, :],
                                     bank(f"branch{n}.a").rearrange("p (a t) -> p a t", a=2), ALU.mult), "branch_a", n + 1)
                job_wait(dve, f"branch{n}.b")
                mark(v.tensor_tensor(tmp[:, 1, 0:T], gates1[:, 2, n, :], bank(f"branch{n}.b")[:, 0:T], ALU.mult), "branch_b", n + 1)
                link(v.tensor_tensor(tmp[:, 0, 0:T], tmp[:, 0, 0:T], tmp[:, 0, T:2 * T], ALU.add))
                link(v.tensor_tensor(tmp[:, 0, 0:T], tmp[:, 0, 0:T], tmp[:, 1, 0:T], ALU.add))
                split_merged(mT1, n, tmp[:, 0, 0:T], "merged")
            layer_norm(1, 1, 0, ALPHA, 2, 2)
            over_ffn(lambda f, it=0: hidden(1, f, it))
            layer_norm(2, 0, 1, 2 * ALPHA, None, 3)
            signal("norm_sum")
            rms_scaled(1, 4, 4)
            turn(2, "mix_pre")

            for t in range(12):
                dve.wait_ge(S["qkv_tap_in"], t + 1)
                for tap in (2, 1, 0):
                    sh = 3 - tap
                    ins = v.scalar_tensor_tensor(cv[:, t, sh:T], bank(f"conv{t}")[:, 0:T - sh], pcol("conv_qkv", 4 * t + tap),
                                                 cv[:, t, sh:T], ALU.mult, ALU.add)
                    if tap:
                        link(ins)
                    else:
                        ins.then_inc(S["qkv_taps"], 1)
            for tok in range(2):
                job_wait(dve, f"small{tok}")
                mark(v.tensor_copy(sm[:, tok, :], bank(f"small{tok}")[:, 0:288]), "small_ready", tok + 1)
            signal("sg_arg")
            a8 = gk[:, 16:24]
            link(v.tensor_tensor(a8.rearrange("p (a h) -> p a h", a=2), sm[:, :, 284:288],
                                 sr("dt_bias", HG).unsqueeze(1).broadcast_to([P, 2, HG]), ALU.add))
            v.scalar_tensor_tensor(gk[:, 24:32], a8, -1.0, a8, ALU.mult, ALU.min).then_inc(S["dt_arg"], 1)
            dve.wait_ge(S["sg_exp"], 1)
            link(v.tensor_scalar(sm[:, :, 256:284], sm[:, :, 256:284], 1.0, None, ALU.add))
            mark(v.reciprocal(sm[:, :, 256:284], sm[:, :, 256:284]), "sg_ready", 1)
            dve.wait_ge(S["dt_log"], 1)
            link(v.scalar_tensor_tensor(gk[:, 24:32], a8, 0.0, gk[:, 24:32], ALU.max, ALU.add))
            g8 = gk[:, 0:8]
            mark(v.scalar_tensor_tensor(g8.rearrange("p (a h) -> p a h", a=2), gk[:, 24:32].rearrange("p (a h) -> p a h", a=2), -1.0,
                                        gk[:, 32:36].unsqueeze(1).broadcast_to([P, 2, HG]), ALU.mult, ALU.mult), "g_ready", 1)
            mark(v.tensor_copy(grow[:], g8.unsqueeze(2).broadcast_to([P, 8, P])), "g_rows", 1)
            b8 = gk[:, 8:16]
            link(v.tensor_copy(b8.rearrange("p (a h) -> p a h", a=2), sm[:, :, 280:284]))
            mark(v.tensor_copy(brep[:], b8.unsqueeze(2).broadcast_to([P, 8, P])), "g_rows", 2)
            for kv, name in enumerate(("kc", "vc")):
                job_wait(dve, name)
                ps = bank(name)
                for g in range(2):
                    for l in range(2):
                        last = v.tensor_copy(xc[64 * l:64 * l + 64, kv, g, 0:T - l], ps[64 * g:64 * g + 64, l:T])
                mark(last, f"{name}_shifted", 1)
                x16 = xc[:, kv, :, 0:240].rearrange("p g (n k l) -> p g n k l", k=8, l=2)[:, :, :, :, 0]
                y16 = xc[:, kv, :, 16:256].rearrange("p g (n k l) -> p g n k l", k=8, l=2)[:, :, :, :, 0]
                pos = COL_AT["pos_k" if kv == 0 else "pos_v"]
                for g in range(2):
                    for half, src in ((0, x16), (1, y16)):
                        last = v.tensor_tensor(rc[:, kv, 8 * half:8 * half + 8, g, :], src[:, g].rearrange("p n k -> p k n"),
                                               col[:, pos + 8 * half:pos + 8 * half + 8].unsqueeze(2).broadcast_to([P, 8, NC]), ALU.add)
                link(last)
                both = rc[:, kv].rearrange("p k g n -> p (k g n)")
                hi, lo = (x[:, kv].rearrange("p k n -> p (k n)") for x in rcs)
                mark(v.tensor_copy(hi, both), "kv_pos", 2 * kv + 1)
                mark(low(lo, both, hi), "kv_pos", 2 * kv + 2)
            for kind, name in enumerate(("ks", "kw")):
                job_wait(dve, name)
                ps = bank(name)
                for g in range(2):
                    for half in range(2):
                        last = v.tensor_copy(kdup[64 * half:64 * half + 64, kind, g, :], ps[64 * g:64 * g + 64, 0:T])
                last.then_inc(S["kdup_ready"], 1)
            for t in range(4):
                dve.wait_ge(S["l2_scale"], t + 1)
                dve.wait_ge(S["qkv_ready"], 2 * t + 2)
                two = cv[:, 2 * t:2 * t + 2, :].rearrange("p a t -> p (a t)")
                v.scalar_tensor_tensor(two, two, float(np.float32(P ** -0.5)) if t < 2 else 1.0,
                                       csq[:, 2 * t:2 * t + 2, :].rearrange("p a t -> p (a t)"), ALU.mult, ALU.mult
                                       ).then_inc(S["l2_ready"], 1)
            v.memset(bdk[:], 0.0).then_inc(S["zeroed"], 1)
            v.memset(bdv[:], 0.0).then_inc(S["zeroed"], 1)
            dve.wait_ge(S["zeroed"], 2)
            job_wait(dve, "kc2")
            for g in range(2):
                for half in range(2):
                    last = v.tensor_copy(bdk[64 * half:64 * half + 64, g, 32 * half:32 * half + NC],
                                         bank("kc2")[0:64, NC * g:NC * g + NC])
            last.then_inc(S["kcomp_ready"], 1)
            job_wait(dve, "vc2")
            for g in range(2):
                for h in range(4):
                    last = v.tensor_copy(bdv[32 * h:32 * h + NC, g, 64 * h:64 * h + 64], bank("vc2")[0:NC, 64 * g:64 * g + 64])
            last.then_inc(S["vcomp_ready"], 1)
            job_wait(dve, "gcum")
            mark(v.tensor_copy(gk[:, 40:48], bank("gcum")[:, 0:8]), "gcum_ready", 1)
            mark(v.tensor_scalar(gk[:, 48:56], gk[:, 40:48], -1.0, None, ALU.mult), "gcum_neg", 1)
            job_wait(dve, "grow0")
            v.tensor_tensor(gk[:, 72:76], bank("grow0").rearrange("p (h t) -> p h t", h=HG)[:, :, P - 1], gk[:, 40:44], ALU.subtract
                            ).then_inc(S["tail_arg"], 1)
            for ch in range(2):
                job_wait(dve, f"grow{ch}")
                v.tensor_tensor(dec[:, HG * ch:HG * ch + HG, :], bank(f"grow{ch}").rearrange("p (h t) -> p h t", h=HG),
                                c("decmask").unsqueeze(1).broadcast_to([P, HG, P]), ALU.add).then_inc(S["decay_arg"], 1)
            for ch in range(2):
                job_wait(dve, f"brow{ch}")
                v.tensor_copy(brep[:, HG * ch:HG * ch + HG, :].rearrange("p h t -> p (h t)"), bank(f"brow{ch}")
                              ).then_inc(S["beta_row"], 1)
            for ch in range(2):
                hs = slice(HG * ch, HG * ch + HG)
                job_wait(dve, f"kk{ch}")
                dve.wait_ge(S["decay"], HG * (ch + 1))
                dve.wait_ge(S["beta_row"], ch + 1)
                mark(v.tensor_tensor(lt[:, hs, :], bank(f"kk{ch}").rearrange("p (h t) -> p h t", h=HG), dec[:, hs, :], ALU.mult),
                     "kk_ready", ch + 1)
                mark(v.tensor_tensor(lt[:, hs, :], lt[:, hs, :], brep[:, hs, :], ALU.mult), "lt_ready", ch + 1)
                job_wait(dve, f"qk2_{ch}")
                v.tensor_tensor(qkd[:, hs, :], bank(f"qk2_{ch}").rearrange("p (h t) -> p h t", h=HG), dec[:, hs, :], ALU.mult
                                ).then_inc(S["qkd_ready"], 1)
            def level(lv):
                if lv >= 3:
                    job_wait(dve, f"y{lv - 2}.1")
                mark(v.tensor_tensor(ot[lv % 2], lt, c(f"level{lv}").unsqueeze(1).broadcast_to([P, 8, P]), ALU.mult),
                     "ot_ready", lv + 1)

            level(0)
            level(1)
            for ch in range(2):
                hs = slice(HG * ch, HG * ch + HG)
                mark(v.tensor_tensor(xinvT[:, hs, :], ident.unsqueeze(1).broadcast_to([P, HG, P]), ot[0][:, hs, :], ALU.subtract),
                     "xt_ready", ch + 1)
            for ch in range(2):
                job_wait(dve, f"x0_{ch}")
                v.tensor_copy(xinv[:, HG * ch:HG * ch + HG, :].rearrange("p h t -> p (h t)"), bank(f"x0_{ch}")
                              ).then_inc(S["x_ready"], 1)
            def heads(buf):
                return buf.rearrange("p (h t) -> p h t", h=HG)

            def wide(lo):
                return gk[:, lo:lo + HG].unsqueeze(2).broadcast_to([P, HG, P])

            dve.wait_ge(S["vtm_ready"], 2)
            dve.wait_ge(S["gam"], 1)
            dve.wait_ge(S["tail"], 1)
            link(v.tensor_tensor(gk[:, 80:84], gk[:, 12:16], gk[:, 68:72], ALU.mult))
            v.tensor_tensor(heads(vtm[:, 0, :]), heads(vtm[:, 0, :]), wide(8), ALU.mult).then_inc(S["rhs_ready"], 1)
            v.tensor_tensor(heads(vtm[:, 1, :]), heads(vtm[:, 1, :]), wide(12), ALU.mult).then_inc(S["rhs_ready"], 1)
            v.tensor_tensor(heads(kbg[:]), heads(ktm[:, 1, :]), wide(80), ALU.mult).then_inc(S["rhs_ready"], 1)
            v.tensor_tensor(heads(ktail[:]), heads(ktm[:, 0, :]), wide(72), ALU.mult).then_inc(S["rhs_ready"], 1)
            for lv in range(1, LEVELS):
                if lv + 1 < LEVELS:
                    level(lv + 1)
                for ch in range(2):
                    hs = slice(HG * ch, HG * ch + HG)
                    job_wait(dve, f"zz{lv}.{ch}" if lv < LEVELS - 1 else f"zt{lv}.{ch}")
                    flat = xinvT[:, hs, :].rearrange("p h t -> p (h t)")
                    v.tensor_tensor(flat, flat, bank(f"zt{lv}.{ch}"), ALU.subtract).then_inc(S["xt_ready"], 1)
                    if lv < LEVELS - 1:
                        flat = xinv[:, hs, :].rearrange("p h t -> p (h t)")
                        v.tensor_tensor(flat, flat, bank(f"zz{lv}.{ch}"), ALU.subtract).then_inc(S["x_ready"], 1)
            job_wait(dve, "ws")
            v.tensor_tensor(ub[:, 1, :], ub[:, 1, :], bank("ws"), ALU.subtract).then_inc(S["u_ready"], 1)
            job_wait(dve, "oi0")
            v.tensor_copy(og[:, 0, :], bank("oi0")).then_inc(S["gdn_out"], 1)
            job_wait(dve, "ox")
            mark(v.tensor_tensor(heads(og[:, 1, :]), heads(bank("ox")), wide(68), ALU.mult), "gdn_out", 2)
            job_wait(dve, "oi1")
            mark(v.tensor_tensor(og[:, 1, :], og[:, 1, :], bank("oi1"), ALU.add), "gdn_out", 3)
            ccol = gk[:, 96:160]
            for tok in range(2):
                job_wait(dve, f"cs{tok}")
                s3 = cs_sb[:, tok, :].rearrange("p (h n) -> p h n", h=H2)
                mark(v.tensor_tensor(cs_sb[:, tok, :], bank(f"cs{tok}")[:, 0:T], c(f"cmp{tok}"), ALU.add), "cmp_biased", tok + 1)
                mx = ccol[:, 24 * tok:24 * tok + 8]
                link(v.tensor_reduce(mx, s3, AX.X, ALU.max))
                v.tensor_tensor(s3, s3, mx.unsqueeze(2).broadcast_to([P, H2, 32]), ALU.subtract).then_inc(S["cmp_arg"], 1)
            for tok in range(2):
                s3 = cs_sb[:, tok, :].rearrange("p (h n) -> p h n", h=H2)
                sums, cc = ccol[:, 24 * tok + 8:24 * tok + 16], ccol[:, 24 * tok + 16:24 * tok + 24]
                dve.wait_ge(S["cmp_probs"], tok + 1)
                link(v.tensor_reduce(sums, s3, AX.X, ALU.add))
                link(v.reciprocal(cc, sums))
                link(v.tensor_tensor(cc, cc, sm[:, tok, T:T + 24].rearrange("p (h b) -> p h b", b=3)[:, :, 0], ALU.mult))
                if tok == 0:
                    link(v.tensor_scalar(cc, cc, c("rowvalid"), None, ALU.mult))
            for tok in range(2):
                job_wait(dve, f"co{tok}")
                cc = ccol[:, 24 * tok + 16:24 * tok + 24]
                mark(v.tensor_tensor(o2[:, tok, :].rearrange("p (h d) -> p h d", h=H2), bank(f"co{tok}").rearrange("p (h d) -> p h d", h=H2),
                                     cc.unsqueeze(2).broadcast_to([P, H2, 64]), ALU.mult), "cmp_out", tok + 1)
            ogf = res[:, 0, :]
            og8 = ogf.rearrange("p (m d) -> p m d", d=P)
            ybf = yb[:].rearrange("p h t -> p (h t)")
            link(v.tensor_tensor(ybf, ogf, ogf, ALU.mult))
            v.tensor_reduce(stat[:, 20:28], yb[:], AX.X, ALU.add).then_inc(S["gdn_sum"], 1)
            for i in range(N_INST2 + 2):
                attention(i, N_INST1, N_INST2)
            dve.wait_ge(S["gdn_std"], 1)
            dve.wait_ge(S["z_ready"], 2)
            link(v.reciprocal(stat[:, 44:52], stat[:, 32:40]))
            link(v.tensor_tensor(og8, og8, stat[:, 44:52].unsqueeze(2).broadcast_to([P, 8, P]), ALU.mult))
            link(v.tensor_tensor(og8, og8, sr("gdn_norm", P).unsqueeze(1).broadcast_to([P, 8, P]), ALU.mult))
            v.tensor_tensor(ogf, ogf, zs[:].rearrange("p a n -> p (a n)"), ALU.mult).then_inc(S["gdn_normed"], 1)
            for k in range(4):
                dve.wait_ge(S["yT_high"], k + 1)
                hi, lo = (x[:, 2 * k:2 * k + 2, :].rearrange("p a t -> p (a t)") for x in yT)
                low(lo, bank(f"yT{k}"), hi).then_inc(S["yT_ready"], 1)
            dve.wait_ge(S["x_high"], KD + 1)
            low(pE[1][:], p_raw, pE[0][:]).then_inc(S["p_split"], 1)
            dve.wait_ge(S["gmix_ready"], 1)
            for n in range(8):
                job_wait(dve, f"mix{n}")
                mark(v.tensor_tensor(tmp[:, n % 2, :].rearrange("p (a t) -> p a t", a=2), gates2[:, :, n, :],
                                     bank(f"mix{n}").rearrange("p (a t) -> p a t", a=2), ALU.mult), "mix_gated", n + 1)
                link(v.tensor_tensor(tmp[:, n % 2, 0:T], tmp[:, n % 2, 0:T], tmp[:, n % 2, T:2 * T], ALU.add))
                split_merged(mT2, n, tmp[:, n % 2, 0:T], "mixed")
            add_normed(3, 1, 0, lambda tok, half: acc[:, 2 * tok + half, :], 5)
            signal("norm_sum")
            rms_scaled(0, 6, 6)
            turn(3, "ffn_pre")
            over_ffn(conv_hidden)
            steps[0] += NF
            dve.wait_ge(S["acc_done"], 5)
            add_normed(4, 0, 1, lambda tok, half: acc[:, 2 * tok + half, :], 7)
            for tok in range(2):
                v.tensor_copy(res[:, tok, :], xs[:, 1, tok, :]).then_inc(S["xn_ready"], 1)
            turn(4)
            dve.wait_ge(S["ple_ready"], 4)
            for tok in range(2):
                dve.wait_ge(S["acc_read"], 20 + tok + 1)
                v.tensor_tensor(res[:, tok, :], res[:, tok, :], ple_flat[:, D * tok:D * tok + D], ALU.mult).then_inc(S["ple_gated"], 1)
            dve.wait_ge(S["ple_gated"], 2)
            add_normed(5, 1, 0, lambda tok, half: res[:, tok, 512 * half:512 * half + 512], 8, final=True)


def fm_blocks(w):
    k, n = w.shape
    return w.reshape(k // P, P, n // P, P).transpose(2, 0, 1, 3).reshape(-1, P, P)


def tm_blocks(w):
    k, n = w.shape
    return w.reshape(k // P, P, n // P, P).transpose(0, 2, 1, 3).reshape(-1, P, P)


def ffn_blocks(gate, up, down):
    g, u, d = (a.reshape(NF, 8, P, P) for a in (fm_blocks(gate), fm_blocks(up), tm_blocks(down)))
    parts = [g[0], u[0]]
    for f in range(1, NF):
        parts += [g[f], u[f], d[f - 1]]
    return parts + [d[NF - 1]]


def padded(w, n):
    out = np.zeros((w.shape[0], n), w.dtype)
    out[:, :w.shape[1]] = w
    return out


def pack_stream(a):
    w_in, w2 = a["w_in"][0], a["w_in_2"][0]
    parts = ffn_blocks(a["ffn_w_gate"][0, 0], a["ffn_w_up"][0, 0], a["ffn_w_down"][0, 0])
    q = W1
    for m in range(3):
        parts += [fm_blocks(w_in[:, 3 * q * m:3 * q * m + q]), fm_blocks(w_in[:, 3 * q * m + q:3 * q * m + 2 * q])]
    vcat = np.concatenate([w_in[:, 3 * q * m + 2 * q:3 * q * m + 3 * q] for m in range(3)], 1)
    parts += [tm_blocks(padded(vcat[:, q * m:q * m + q], 512)) for m in range(3)]
    parts.append(fm_blocks(w_in[:, 9 * q:]))
    br = [fm_blocks(a[n][0]).reshape(8, 3, P, P) for n in ("w_br_moba", "w_br_diff", "w_br_sb")]
    parts.append(np.stack(br, 1).reshape(-1, P, P))
    parts.append(tm_blocks(a["w_out"][0]))
    parts += ffn_blocks(a["ffn_w_gate"][0, 1], a["ffn_w_up"][0, 1], a["ffn_w_down"][0, 1])
    at = {}
    off = 0
    for name, n in (("qkv", 1536), ("z", 512), ("b", 4), ("a", 4), ("q", 512), ("kc", 128), ("vc", 128), ("ks", 128),
                    ("vs", 128), ("kw", 128), ("vw", 128), ("gn", 24), ("gm", 2048)):
        at[name] = w2[:, off:off + n]
        off += n
    parts.append(fm_blocks(at["qkv"]))
    small = np.concatenate([at["vs"], at["vw"], at["gn"], at["b"], at["a"]], 1)
    parts.append(tm_blocks(padded(small, 512)))
    parts.append(tm_blocks(at["z"]))
    parts += [fm_blocks(at[n]) for n in ("kc", "vc", "q", "ks", "kw")]
    parts += [tm_blocks(a["cmp_w1_k_2"][0]), tm_blocks(a["cmp_w1_v_2"][0])]
    parts += [fm_blocks(padded(a["cmp_w2_k_2"][0], P)), fm_blocks(padded(a["cmp_w2_v_2"][0], P)), np.zeros((4, P, P), np.float32)]
    parts.append(fm_blocks(at["gm"]))
    ab = [fm_blocks(a[n][0]).reshape(8, 4, P, P) for n in ("w_a2d_2", "w_b2d_2")]
    parts.append(np.stack(ab, 1).reshape(-1, P, P))
    parts.append(tm_blocks(a["w_o_2"][0]))
    parts.append(tm_blocks(a["w_ple_2"][0]))
    up = a["w_up_2"][0]
    parts += ffn_blocks(up[:, :FF], up[:, FF:], a["w_down_2"][0])
    parts.append(tm_blocks(a["w_ple_gate_2"][0]))
    blocks = np.concatenate(parts, 0)
    assert blocks.shape[0] == N_BLOCKS, (blocks.shape, N_BLOCKS)
    if N_CHUNKS * CB > N_BLOCKS:
        blocks = np.concatenate([blocks, np.zeros((N_CHUNKS * CB - N_BLOCKS, P, P), blocks.dtype)], 0)
    return np.ascontiguousarray(blocks.reshape(N_CHUNKS, CB, P, P).transpose(0, 2, 1, 3).reshape(N_CHUNKS, P, CB * P))


def as_cols(vec):
    return vec.reshape(-1, P).T


def kernel(**inputs):
    import concourse.bacc as bacc
    from concourse.bass_utils import run_bass_kernel_spmd

    a = {k: np.asarray(v) for k, v in inputs.items()}
    const, const_at = constants()
    lg_, lb_ = a["ln_g"][0], a["ln_b"][0]

    def pos_cols(pos):
        return pos.reshape(16, 2 * 64).T

    cols = np.concatenate([
        as_cols(lg_[0]), as_cols(lb_[0]), as_cols(lg_[1]), as_cols(lb_[1]), as_cols(a["norm_mix_pre_2"][0]),
        as_cols(a["norm_ffn_pre_2"][0]), as_cols(a["b_gate"][0].reshape(-1)),
        a["conv_qkv_2"][0].reshape(4, 12, P).transpose(2, 1, 0).reshape(P, -1),
        a["conv_ffn_2"][0].reshape(3, 2 * NF, P).transpose(2, 1, 0).reshape(P, -1),
        as_cols(a["conv_ffn_b_2"][0]), pos_cols(a["cmp_pos_k_2"][0]), pos_cols(a["cmp_pos_v_2"][0])], 1)
    big = np.zeros((len(BIG_ROWS), 2 * D), np.float32)
    named = {f"ln_g{i}": lg_[i] for i in range(3)} | {f"ln_b{i}": lb_[i] for i in range(3)} | {
        "mix_post": a["norm_mix_post_2"][0], "ffn_post": a["norm_ffn_post_2"][0], "ple_post": a["norm_ple_post_2"][0]}
    for i, names in enumerate(BIG_ROWS):
        for j, n in enumerate(names):
            big[i, D * j:D * j + D] = named[n]
    small = np.concatenate([a["gdn_norm_2"][0], a["diff_subln_g"][0], a["diff_lambda"][0].reshape(-1), a["a_log_2"][0],
                            a["dt_bias_2"][0]])[None, :]
    x = a["x"][0]
    arrays = {
        "x_tm": x.reshape(2, P, D).transpose(1, 0, 2), "x_fm": x.T.reshape(KD, P, T).transpose(1, 0, 2),
        "p_fm": a["p_2"][0, 0].T.reshape(2, P, T).transpose(1, 0, 2), "stream": pack_stream(a), "consts": const,
        "cols": cols, "big_rows": big, "small_rows": small,
    }
    arrays = {k: np.ascontiguousarray(v) for k, v in arrays.items()}
    nc = bacc.Bacc("TRN2", target_bir_lowering=False, num_devices=1)
    args = [nc.dram_tensor(f"in_{k}", v.shape, mybir.dt.from_np(v.dtype), kind="ExternalInput").ap() for k, v in arrays.items()]
    out = nc.dram_tensor("out_0", (1, T, D), F32, kind="ExternalOutput").ap()
    build(nc, *args, out, const_at)
    r = run_bass_kernel_spmd(nc, [{f"in_{k}": v for k, v in arrays.items()}], core_ids=[0])
    return r.results[0]["out_0"]
```
